# Optimizing a Trainium2 kernel written in Bass

```python
import jax, jax.numpy as jnp
from jax import lax
import numpy as np
import math

D_MODEL = 1024
BATCH = 1
SEQ = 256
DEPTH = 2

RET_HEADS = 4
RET_DK = 128
RET_DV = 128
FOX_HEADS = 8
FOX_DH = 64
D_FF = 2816
CHUNK = 128
Q_BLOCK = 128
ROPE_BASE = 10000.0
EPS = 1e-6

RET_QK = RET_HEADS * RET_DK
RET_V = RET_HEADS * RET_DV
FOX_W = FOX_HEADS * FOX_DH
IN_SPLITS = (RET_QK, RET_QK, RET_V, RET_V, FOX_W, FOX_W, FOX_W, FOX_HEADS, D_MODEL, D_MODEL)
IN_COLS = sum(IN_SPLITS)


def rmsnorm(x, g):
    xf = x.astype(jnp.float32)
    y = xf * lax.rsqrt(jnp.mean(xf * xf, axis=-1, keepdims=True) + EPS)
    return (y * g.astype(jnp.float32)).astype(x.dtype)

def swiglu(h, w_in, w_out):
    gu = h @ w_in
    a, b = gu[..., :D_FF], gu[..., D_FF:]
    return (jax.nn.silu(a) * b) @ w_out

def split_cols(p):
    outs = []
    off = 0
    for w in IN_SPLITS:
        outs.append(p[..., off:off + w])
        off += w
    return outs

def to_heads(t, n_heads):
    b, s, _ = t.shape
    return t.reshape(b, s, n_heads, -1).transpose(0, 2, 1, 3)

def from_heads(t):
    b, h, s, d = t.shape
    return t.transpose(0, 2, 1, 3).reshape(b, s, h * d)

def rope(t):
    s, d = t.shape[2], t.shape[3]
    inv = jnp.power(ROPE_BASE, -jnp.arange(0, d, 2, dtype=jnp.float32) / d)
    ang = jnp.arange(s, dtype=jnp.float32)[:, None] * inv[None, :]
    cos, sin = jnp.cos(ang), jnp.sin(ang)
    tf = t.astype(jnp.float32)
    t1, t2 = tf[..., : d // 2], tf[..., d // 2:]
    return jnp.concatenate([t1 * cos - t2 * sin, t1 * sin + t2 * cos], axis=-1).astype(t.dtype)

def retention_chunkwise(q, k, v):
    in_dtype = v.dtype
    q = q.astype(jnp.float32)
    k = k.astype(jnp.float32) * (q.shape[-1] ** -0.5)
    v = v.astype(jnp.float32)
    b, h, s, dk = q.shape
    dv = v.shape[-1]
    n = s // CHUNK
    log_gamma = jnp.log1p(-jnp.exp2(-5.0 - jnp.arange(h, dtype=jnp.float32)))
    idx = jnp.arange(CHUNK, dtype=jnp.float32)
    diff = idx[:, None] - idx[None, :]
    decay_intra = jnp.where(diff >= 0, jnp.exp(log_gamma[:, None, None] * jnp.maximum(diff, 0.0)), 0.0)
    xi = jnp.exp(log_gamma[:, None] * (idx + 1.0))
    zeta = jnp.exp(log_gamma[:, None] * (CHUNK - 1.0 - idx))
    gamma_c = jnp.exp(log_gamma * CHUNK)

    qc = q.reshape(b, h, n, CHUNK, dk)
    kc = k.reshape(b, h, n, CHUNK, dk)
    vc = v.reshape(b, h, n, CHUNK, dv)

    scores = jnp.einsum('bhncd,bhnsd->bhncs', qc, kc) * decay_intra[None, :, None]
    inner = jnp.einsum('bhncs,bhnse->bhnce', scores, vc)

    kv = jnp.einsum('bhncd,bhnce->bhnde', kc * zeta[None, :, None, :, None], vc)

    def step(state, kv_n):
        return gamma_c[None, :, None, None] * state + kv_n, state

    _, state_prev = lax.scan(step, jnp.zeros((b, h, dk, dv), jnp.float32), jnp.moveaxis(kv, 2, 0))
    state_prev = jnp.moveaxis(state_prev, 0, 2)
    cross = jnp.einsum('bhncd,bhnde->bhnce', qc * xi[None, :, None, :, None], state_prev)
    return (inner + cross).reshape(b, h, s, dv).astype(in_dtype)

def forgetting_attention(q, k, v, log_f):
    b, h, s, d = q.shape
    c = jnp.cumsum(log_f, axis=-1)
    kpos = jnp.arange(s)
    scale = d ** -0.5
    n_blocks = s // Q_BLOCK

    def block(i):
        start = i * Q_BLOCK
        qb = lax.dynamic_slice_in_dim(q, start, Q_BLOCK, axis=2)
        cb = lax.dynamic_slice_in_dim(c, start, Q_BLOCK, axis=2)
        qpos = start + jnp.arange(Q_BLOCK)
        logits = jnp.einsum('bhqd,bhkd->bhqk', qb, k).astype(jnp.float32) * scale
        logits = logits + (cb[..., :, None] - c[..., None, :])
        logits = jnp.where(kpos[None, :] <= qpos[:, None], logits, -1e30)
        p = jax.nn.softmax(logits, axis=-1)
        return jnp.einsum('bhqk,bhkd->bhqd', p.astype(v.dtype), v)

    out = lax.map(block, jnp.arange(n_blocks))
    return jnp.moveaxis(out, 0, 2).reshape(b, h, s, d)

def mixing_sublayer(h, w_in, b_forget, ret_norm, w_o_ret, w_o_fox, w_out):
    proj = h @ w_in
    rq, rk, rv, rg, fq, fk, fv, ff, gate_r, gate_f = split_cols(proj)

    ret = retention_chunkwise(rope(to_heads(rq, RET_HEADS)), rope(to_heads(rk, RET_HEADS)), to_heads(rv, RET_HEADS))
    retf = ret.astype(jnp.float32)
    retf = retf * lax.rsqrt(jnp.mean(retf * retf, axis=-1, keepdims=True) + EPS)
    ret = from_heads(retf.astype(h.dtype)) * ret_norm
    y_ret = (jax.nn.silu(rg) * ret) @ w_o_ret

    log_f = jax.nn.log_sigmoid((ff + b_forget).astype(jnp.float32))
    fox = forgetting_attention(to_heads(fq, FOX_HEADS), to_heads(fk, FOX_HEADS), to_heads(fv, FOX_HEADS),
                               log_f.transpose(0, 2, 1))
    y_fox = from_heads(fox) @ w_o_fox

    merged = jax.nn.sigmoid(gate_r) * y_ret + jax.nn.sigmoid(gate_f) * y_fox
    return merged @ w_out

def first_inputs(seed: int = 0) -> dict:
    key = jax.random.key(seed)
    ks = jax.random.split(key, 16)
    f32 = jnp.float32

    def nrm(k, shape, fan_in):
        return jax.random.normal(k, shape, f32) * (fan_in ** -0.5)

    def gain(k, shape):
        return 1.0 + 0.02 * jax.random.normal(k, shape, f32)

    return {
        "x": jax.random.normal(ks[0], (BATCH, SEQ, D_MODEL), f32),
        "norm_ffn1": gain(ks[1], (DEPTH, D_MODEL)),
        "w_ffn1_in": nrm(ks[2], (DEPTH, D_MODEL, 2 * D_FF), D_MODEL),
        "w_ffn1_out": nrm(ks[3], (DEPTH, D_FF, D_MODEL), D_FF),
        "norm_mix": gain(ks[4], (DEPTH, D_MODEL)),
        "w_in": nrm(ks[5], (DEPTH, D_MODEL, IN_COLS), D_MODEL),
        "b_forget": jax.random.uniform(ks[6], (DEPTH, FOX_HEADS), f32, minval=1.0, maxval=4.0),
        "ret_norm": gain(ks[7], (DEPTH, RET_V)),
        "w_o_ret": nrm(ks[8], (DEPTH, RET_V, D_MODEL), RET_V),
        "w_o_fox": nrm(ks[9], (DEPTH, FOX_W, D_MODEL), FOX_W),
        "w_out": nrm(ks[10], (DEPTH, D_MODEL, D_MODEL), D_MODEL),
        "norm_ffn2": gain(ks[11], (DEPTH, D_MODEL)),
        "w_ffn2_in": nrm(ks[12], (DEPTH, D_MODEL, 2 * D_FF), D_MODEL),
        "w_ffn2_out": nrm(ks[13], (DEPTH, D_FF, D_MODEL), D_FF),
        "norm_final": gain(ks[14], (D_MODEL,)),
    }

def first_block(x, norm_ffn1, w_ffn1_in, w_ffn1_out, norm_mix, w_in, b_forget, ret_norm,
              w_o_ret, w_o_fox, w_out, norm_ffn2, w_ffn2_in, w_ffn2_out, norm_final):
    for l in range(DEPTH):
        x = x + 0.5 * swiglu(rmsnorm(x, norm_ffn1[l]), w_ffn1_in[l], w_ffn1_out[l])
        h = rmsnorm(x, norm_mix[l])
        x = x + mixing_sublayer(h, w_in[l], b_forget[l], ret_norm[l], w_o_ret[l], w_o_fox[l], w_out[l])
        x = x + 0.5 * swiglu(rmsnorm(x, norm_ffn2[l]), w_ffn2_in[l], w_ffn2_out[l])
    return rmsnorm(x, norm_final)


GRID_W = 64
CTX_LEN = 256
HEAD_DIM = 64
A_Q_HEADS = 16
A_KV_HEADS = 4
A_GROUP = A_Q_HEADS // A_KV_HEADS
WINDOW = 128
BLOCK = 128
B_HEADS = D_MODEL // (2 * HEAD_DIM)
N_EXPERTS = 16
N_GROUPS = 4
GROUP_SIZE = N_EXPERTS // N_GROUPS
TOP_K = 2
GROUP_SCORE_K = 2
D_EXPERT = D_MODEL // 2
ROPE_THETA = 10000.0
N_A_LAYERS = (DEPTH + 1) // 2
N_B_LAYERS = DEPTH // 2
DEEPNORM_ALPHA = (2 * DEPTH) ** 0.25
DEEPNORM_BETA = (8 * DEPTH) ** -0.25
LN_EPS = 1e-6
SUBLN_EPS = 1e-5
NEG_INF = -1e30
ATTN_SCALE = HEAD_DIM ** -0.5


F32 = jnp.float32

def layer_norm(x, g, b):
    xf = x.astype(F32)
    mu = xf.mean(-1, keepdims=True)
    var = jnp.square(xf - mu).mean(-1, keepdims=True)
    return ((xf - mu) * lax.rsqrt(var + LN_EPS) * g.astype(F32) + b.astype(F32)).astype(x.dtype)

def rms_norm(x, g):
    xf = x.astype(F32)
    return (xf * lax.rsqrt(jnp.square(xf).mean(-1, keepdims=True) + SUBLN_EPS) * g.astype(F32)).astype(x.dtype)

def axial_rope_tables(n_tokens):
    n_rows = n_tokens // GRID_W
    rows = jnp.broadcast_to(jnp.arange(n_rows)[:, None], (n_rows, GRID_W)).reshape(-1)
    cols = jnp.broadcast_to(jnp.arange(GRID_W)[None, :], (n_rows, GRID_W)).reshape(-1)
    quarter = HEAD_DIM // 4
    inv_freq = ROPE_THETA ** (-jnp.arange(quarter, dtype=F32) / quarter)
    ang_r = rows.astype(F32)[:, None] * inv_freq
    ang_c = cols.astype(F32)[:, None] * inv_freq
    return (jnp.cos(ang_r), jnp.sin(ang_r), jnp.cos(ang_c), jnp.sin(ang_c))

def _rotate(x, cos, sin):
    x1, x2 = jnp.split(x, 2, axis=-1)
    return jnp.concatenate([x1 * cos - x2 * sin, x2 * cos + x1 * sin], axis=-1)

def apply_axial_rope(x, tables):
    cos_r, sin_r, cos_c, sin_c = tables
    shape = (x.shape[1],) + (1,) * (x.ndim - 3) + (cos_r.shape[-1],)
    xr, xc = jnp.split(x.astype(F32), 2, axis=-1)
    out = jnp.concatenate([_rotate(xr, cos_r.reshape(shape), sin_r.reshape(shape)),
                           _rotate(xc, cos_c.reshape(shape), sin_c.reshape(shape))], axis=-1)
    return out.astype(x.dtype)

def sink_attend(q, parts, sink):
    scores = []
    for k, v, mask in parts:
        s = jnp.einsum('bqhgd,bkhd->bhgqk', q, k).astype(F32) * ATTN_SCALE
        if mask is not None:
            s = jnp.where(mask, s, NEG_INF)
        scores.append(s)
    snk = sink.astype(F32)[None, :, :, None, None]
    m = snk
    for s in scores:
        m = jnp.maximum(m, s.max(-1, keepdims=True))
    probs = [jnp.exp(s - m) for s in scores]
    denom = jnp.exp(snk - m)
    for p in probs:
        denom = denom + p.sum(-1, keepdims=True)
    out = None
    for p, (k, v, mask) in zip(probs, parts):
        o = jnp.einsum('bhgqk,bkhd->bqhgd', (p / denom).astype(v.dtype), v)
        out = o if out is None else out + o
    return out

def window_attention_latent(q, k, v, kc, vc, sink):
    S = q.shape[1]
    nb = S // BLOCK
    span = BLOCK + 2 * WINDOW
    kp = jnp.pad(k, ((0, 0), (WINDOW, WINDOW), (0, 0), (0, 0)))
    vp = jnp.pad(v, ((0, 0), (WINDOW, WINDOW), (0, 0), (0, 0)))
    r = jnp.arange(span)
    qi = jnp.arange(BLOCK)
    band = jnp.abs((r - WINDOW)[None, :] - qi[:, None]) <= WINDOW

    def block(n):
        start = n * BLOCK
        qb = lax.dynamic_slice_in_dim(q, start, BLOCK, axis=1)
        kb = lax.dynamic_slice_in_dim(kp, start, span, axis=1)
        vb = lax.dynamic_slice_in_dim(vp, start, span, axis=1)
        key_pos = start - WINDOW + r
        mask = band & ((key_pos >= 0) & (key_pos < S))[None, :]
        return sink_attend(qb, [(kb, vb, mask), (kc, vc, None)], sink)

    out = lax.map(block, jnp.arange(nb))
    return jnp.moveaxis(out, 0, 1).reshape(q.shape)

def window_gqa_mixer(hl, hc, w_qkv, w_o, sink, tables, with_ctx_out):
    B, S, _ = hl.shape
    C = hc.shape[1]
    q_dim = A_Q_HEADS * HEAD_DIM
    kv_dim = A_KV_HEADS * HEAD_DIM
    ql, kl, vl = jnp.split(hl @ w_qkv, [q_dim, q_dim + kv_dim], axis=-1)
    ql = apply_axial_rope(ql.reshape(B, S, A_KV_HEADS, A_GROUP, HEAD_DIM), tables)
    kl = apply_axial_rope(kl.reshape(B, S, A_KV_HEADS, HEAD_DIM), tables)
    vl = vl.reshape(B, S, A_KV_HEADS, HEAD_DIM)
    kc, vc = jnp.split(hc @ w_qkv[:, q_dim:], 2, axis=-1)
    kc = kc.reshape(B, C, A_KV_HEADS, HEAD_DIM)
    vc = vc.reshape(B, C, A_KV_HEADS, HEAD_DIM)
    sink_hg = sink.reshape(A_KV_HEADS, A_GROUP)
    out_l = window_attention_latent(ql, kl, vl, kc, vc, sink_hg).reshape(B, S, q_dim) @ w_o
    if not with_ctx_out:
        return out_l, None
    qc = (hc @ w_qkv[:, :q_dim]).reshape(B, C, A_KV_HEADS, A_GROUP, HEAD_DIM)
    out_c = sink_attend(qc, [(kc, vc, None)], sink_hg).reshape(B, C, q_dim) @ w_o
    return out_l, out_c

def diff_attend(q, k, v, lam):
    s = jnp.einsum('bqhmd,bkhmd->bhmqk', q, k).astype(F32) * ATTN_SCALE
    p = jax.nn.softmax(s, axis=-1)
    a = p[:, :, 0] - lam * p[:, :, 1]
    return jnp.einsum('bhqk,bkhe->bqhe', a.astype(v.dtype), v)

def diff_mixer(hl, hc, w_qkv, w_o, lam_params, subln_g, lam_init, tables, with_ctx_out):
    B, S, _ = hl.shape
    C = hc.shape[1]
    dq = B_HEADS * 2 * HEAD_DIM
    ql, kl, vl = jnp.split(hl @ w_qkv, [dq, 2 * dq], axis=-1)
    ql = apply_axial_rope(ql.reshape(B, S, B_HEADS, 2, HEAD_DIM), tables)
    kl = apply_axial_rope(kl.reshape(B, S, B_HEADS, 2, HEAD_DIM), tables)
    vl = vl.reshape(B, S, B_HEADS, 2 * HEAD_DIM)
    kc, vc = jnp.split(hc @ w_qkv[:, dq:], 2, axis=-1)
    kc = kc.reshape(B, C, B_HEADS, 2, HEAD_DIM)
    vc = vc.reshape(B, C, B_HEADS, 2 * HEAD_DIM)
    lp = lam_params.astype(F32)
    lam = jnp.exp(jnp.sum(lp[0] * lp[1])) - jnp.exp(jnp.sum(lp[2] * lp[3])) + lam_init
    k_all = jnp.concatenate([kl, kc], axis=1)
    v_all = jnp.concatenate([vl, vc], axis=1)

    def block(n):
        qb = lax.dynamic_slice_in_dim(ql, n * BLOCK, BLOCK, axis=1)
        return diff_attend(qb, k_all, v_all, lam)

    out_l = jnp.moveaxis(lax.map(block, jnp.arange(S // BLOCK)), 0, 1).reshape(B, S, B_HEADS, 2 * HEAD_DIM)

    def finish(o):
        n = o.shape[1]
        return (rms_norm(o, subln_g) * (1.0 - lam_init)).reshape(B, n, dq) @ w_o

    if not with_ctx_out:
        return finish(out_l), None
    qc = (hc @ w_qkv[:, :dq]).reshape(B, C, B_HEADS, 2, HEAD_DIM)
    out_c = diff_attend(qc, kc, vc, lam)
    return finish(out_l), finish(out_c)

def moe_ffn(h, w_router, router_bias, w_gate, w_up, w_down):
    N = h.shape[0]
    s = jax.nn.sigmoid(h.astype(F32) @ w_router.astype(F32))
    biased = s + router_bias.astype(F32)
    bg = biased.reshape(N, N_GROUPS, GROUP_SIZE)
    gscore = lax.top_k(bg, GROUP_SCORE_K)[0].sum(-1)
    gsel = jnp.argmax(gscore, axis=-1)
    in_group = jnp.take_along_axis(bg, gsel[:, None, None], axis=1)[:, 0]
    _, loc = lax.top_k(in_group, TOP_K)
    eid = gsel[:, None] * GROUP_SIZE + loc
    s_sel = jnp.take_along_axis(s, eid, axis=-1)
    w = s_sel / s_sel.sum(-1, keepdims=True)
    gates = (jax.nn.one_hot(eid, N_EXPERTS, dtype=F32) * w[..., None]).sum(1)
    out = jnp.zeros_like(h)
    for e in range(N_EXPERTS):
        y = (jax.nn.silu(h @ w_gate[e]) * (h @ w_up[e])) @ w_down[e]
        out = out + gates[:, e:e + 1].astype(h.dtype) * y
    return out

def second_inputs(seed: int = 0) -> dict:
    key = jax.random.key(seed)
    ks = jax.random.split(key, 22)

    def nrm(k, shape, scale):
        return jax.random.normal(k, shape, F32) * scale

    D = D_MODEL
    qa = A_Q_HEADS * HEAD_DIM
    kva = A_KV_HEADS * HEAD_DIM
    dq = B_HEADS * 2 * HEAD_DIM
    return {
        "x": nrm(ks[0], (BATCH, SEQ, D), 1.0),
        "c": nrm(ks[1], (BATCH, D), 1.0),
        "ctx": nrm(ks[2], (BATCH, CTX_LEN, D), 1.0),
        "c_ctx": nrm(ks[3], (D,), 1.0),
        "w_ada": nrm(ks[4], (DEPTH, D, 6 * D), 0.5 * D ** -0.5),
        "b_ada": nrm(ks[5], (DEPTH, 6 * D), 0.02),
        "wqkv_a": nrm(ks[6], (N_A_LAYERS, D, qa + 2 * kva), D ** -0.5),
        "wo_a": nrm(ks[7], (N_A_LAYERS, qa, D), qa ** -0.5 * DEEPNORM_BETA),
        "sink_a": nrm(ks[8], (N_A_LAYERS, A_Q_HEADS), 0.5),
        "wqkv_b": nrm(ks[9], (N_B_LAYERS, D, 3 * dq), D ** -0.5),
        "wo_b": nrm(ks[10], (N_B_LAYERS, dq, D), dq ** -0.5 * DEEPNORM_BETA),
        "lambda_b": nrm(ks[11], (N_B_LAYERS, 4, HEAD_DIM), 0.1),
        "subln_b": 1.0 + nrm(ks[12], (N_B_LAYERS, 2 * HEAD_DIM), 0.02),
        "ln_attn_g": 1.0 + nrm(ks[13], (DEPTH, D), 0.02),
        "ln_attn_b": nrm(ks[14], (DEPTH, D), 0.02),
        "ln_ffn_g": 1.0 + nrm(ks[15], (DEPTH, D), 0.02),
        "ln_ffn_b": nrm(ks[16], (DEPTH, D), 0.02),
        "w_router": nrm(ks[17], (D, N_EXPERTS), D ** -0.5),
        "router_bias": nrm(ks[18], (N_EXPERTS,), 0.01),
        "w_gate": nrm(ks[19], (DEPTH, N_EXPERTS, D, D_EXPERT), D ** -0.5),
        "w_up": nrm(ks[20], (DEPTH, N_EXPERTS, D, D_EXPERT), D ** -0.5),
        "w_down": nrm(ks[21], (DEPTH, N_EXPERTS, D_EXPERT, D), D_EXPERT ** -0.5 * DEEPNORM_BETA),
    }

def second_block(x, c, ctx, c_ctx, w_ada, b_ada, wqkv_a, wo_a, sink_a, wqkv_b, wo_b, lambda_b, subln_b,
              ln_attn_g, ln_attn_b, ln_ffn_g, ln_ffn_b, w_router, router_bias, w_gate, w_up, w_down):
    B, S, D = x.shape
    C = ctx.shape[1]
    tables = axial_rope_tables(S)
    xl, xc = x, ctx
    silu_c = jax.nn.silu(c)
    silu_cc = jax.nn.silu(c_ctx)
    for i in range(DEPTH):
        last = i == DEPTH - 1
        mod_l = (silu_c @ w_ada[i] + b_ada[i])[:, None, :]
        mod_c = silu_cc @ w_ada[i] + b_ada[i]
        sh1_l, sc1_l, g1_l, sh2_l, sc2_l, g2_l = jnp.split(mod_l, 6, axis=-1)
        sh1_c, sc1_c, g1_c, sh2_c, sc2_c, g2_c = jnp.split(mod_c, 6, axis=-1)

        hl = xl * (1.0 + sc1_l) + sh1_l
        hc = xc * (1.0 + sc1_c) + sh1_c
        j = i // 2
        if i % 2 == 0:
            al, ac = window_gqa_mixer(hl, hc, wqkv_a[j], wo_a[j], sink_a[j], tables, not last)
        else:
            lam_init = 0.8 - 0.6 * math.exp(-0.3 * i)
            al, ac = diff_mixer(hl, hc, wqkv_b[j], wo_b[j], lambda_b[j], subln_b[j], lam_init, tables, not last)
        xl = layer_norm(DEEPNORM_ALPHA * xl + g1_l * al, ln_attn_g[i], ln_attn_b[i])

        hl2 = (xl * (1.0 + sc2_l) + sh2_l).reshape(B * S, D)
        if last:
            yl = moe_ffn(hl2, w_router, router_bias, w_gate[i], w_up[i], w_down[i]).reshape(B, S, D)
        else:
            xc = layer_norm(DEEPNORM_ALPHA * xc + g1_c * ac, ln_attn_g[i], ln_attn_b[i])
            hc2 = (xc * (1.0 + sc2_c) + sh2_c).reshape(B * C, D)
            y = moe_ffn(jnp.concatenate([hl2, hc2], axis=0), w_router, router_bias, w_gate[i], w_up[i], w_down[i])
            yl = y[:B * S].reshape(B, S, D)
            yc = y[B * S:].reshape(B, C, D)
            xc = layer_norm(DEEPNORM_ALPHA * xc + g2_c * yc, ln_ffn_g[i], ln_ffn_b[i])
        xl = layer_norm(DEEPNORM_ALPHA * xl + g2_l * yl, ln_ffn_g[i], ln_ffn_b[i])
    return xl


def setup_inputs(seed=0):
    out = dict(first_inputs(seed))
    for name, value in second_inputs(seed + 1).items():
        if name != "x":
            out[name + "_2"] = value
    return out


def reference(
    x, norm_ffn1, w_ffn1_in, w_ffn1_out, norm_mix, w_in, b_forget, ret_norm, w_o_ret, w_o_fox,
    w_out, norm_ffn2, w_ffn2_in, w_ffn2_out, norm_final, c_2, ctx_2, c_ctx_2, w_ada_2, b_ada_2,
    wqkv_a_2, wo_a_2, sink_a_2, wqkv_b_2, wo_b_2, lambda_b_2, subln_b_2, ln_attn_g_2,
    ln_attn_b_2, ln_ffn_g_2, ln_ffn_b_2, w_router_2, router_bias_2, w_gate_2, w_up_2, w_down_2,
):
    x = first_block(
        x, norm_ffn1, w_ffn1_in, w_ffn1_out, norm_mix, w_in, b_forget, ret_norm, w_o_ret,
        w_o_fox, w_out, norm_ffn2, w_ffn2_in, w_ffn2_out, norm_final,
    )
    return second_block(
        x, c_2, ctx_2, c_ctx_2, w_ada_2, b_ada_2, wqkv_a_2, wo_a_2, sink_a_2, wqkv_b_2, wo_b_2,
        lambda_b_2, subln_b_2, ln_attn_g_2, ln_attn_b_2, ln_ffn_g_2, ln_ffn_b_2, w_router_2,
        router_bias_2, w_gate_2, w_up_2, w_down_2,
    )


_drawn_inputs = setup_inputs


def setup_inputs(seed=0):
    import zlib

    import numpy as np

    out = dict(_drawn_inputs(seed))
    spreads = {}
    factors = {'norm_ffn1': 3.225,
     'ret_norm': 16.758,
     'norm_ffn2': 3.668,
     'b_ada_2': 3.131,
     'sink_a_2': 56.348,
     'lambda_b_2': 6.026,
     'subln_b_2': 124.097,
     'b_forget': 3.361,
     'norm_final': 3.169}
    for name, (base, spread) in spreads.items():
        noise = np.random.default_rng([zlib.crc32(name.encode()), seed]).standard_normal(out[name].shape)
        drawn = base * np.exp(spread * noise) if base else spread * noise
        out[name] = __import__('jax').numpy.asarray(drawn.astype(out[name].dtype))
    for name, factor in factors.items():
        out[name] = (out[name] * factor).astype(out[name].dtype)
    return out
```

```python
from contextlib import ExitStack

import numpy as np

import concourse.bass as bass
from concourse import mybir

P = 128
D = 1024
FF = 2816
NE = 16
DE = 512
ALU = mybir.AluOpType
ACT = mybir.ActivationFunctionType
F32 = mybir.dt.float32
F32R = mybir.dt.float32r
U32 = mybir.dt.uint32
AX = mybir.AxisListType.X
EPS = 1e-6
ALPHA = 4.0 ** 0.25
LAM_INIT = 0.8 - 0.6 * float(np.exp(-0.3))
BIG = 16384.0

CONSTS = [("ident", 128), ("negtri", 128), ("negones", 128), ("cmask", 128), ("wmask", 128),
          ("cos1", 128), ("sin1", 128), ("cos2", 128), ("sin2", 128), ("iota", 128), ("tid", 4), ("lt4", 16),
          ("eoff", 16), ("bl", 128), ("bc", 128), ("half", 1)]


def constants():
    i = np.arange(P, dtype=np.float64)
    t = {}
    t["ident"] = np.eye(P)
    t["negtri"] = -(i[:, None] <= i[None, :]).astype(np.float64)
    t["negones"] = -np.ones((P, P))
    t["cmask"] = np.where(i[None, :] > i[:, None], -1e30, 0.0)
    t["wmask"] = np.where(i[None, :] < i[:, None], -1e30, 0.0)
    dec = np.zeros((P, 4, 2, P))
    for h in range(4):
        lg = np.log1p(-np.exp2(-5.0 - h))
        d = i[None, :] - i[:, None]
        dec[:, h, 0] = np.where(d >= 0, np.exp(lg * np.maximum(d, 0)), 0.0) * 128 ** -0.5
        dec[:, h, 1] = np.exp(lg * (128 + d)) * 128 ** -0.5
    tok = (np.arange(2)[None, :] * P + i[:, None]).astype(np.float32)
    inv = np.power(np.float32(10000.0), -np.arange(0, 128, 2, dtype=np.float32) / np.float32(128))
    ang = (tok[:, :, None] * inv).astype(np.float32).astype(np.float64)
    t["cos1"] = np.cos(ang).reshape(P, 128)
    t["sin1"] = np.sin(ang).reshape(P, 128)
    inv2 = np.power(np.float32(10000.0), -np.arange(16, dtype=np.float32) / np.float32(16))
    ar = ((tok // 64)[:, :, None] * inv2).astype(np.float32).astype(np.float64)
    ac = ((tok % 64)[:, :, None] * inv2).astype(np.float32).astype(np.float64)
    t["cos2"] = np.concatenate([np.cos(ar), np.cos(ar), np.cos(ac), np.cos(ac)], -1).reshape(P, 128)
    t["sin2"] = np.concatenate([-np.sin(ar), np.sin(ar), -np.sin(ac), np.sin(ac)], -1).reshape(P, 128)
    t["iota"] = np.broadcast_to(i[None, :], (P, P))
    t["tid"] = np.arange(4)[None, :] * P + i[:, None]
    t["lt4"] = np.broadcast_to((np.arange(4)[None, :] < np.arange(4)[:, None]).reshape(1, 16), (P, 16))
    t["eoff"] = np.broadcast_to(np.arange(16)[None, :] * P - 1.0, (P, 16))
    t["bl"] = np.where(np.isin(np.arange(P), (0, 1, 4))[:, None], 1.0, 0.0) * np.ones((P, P))
    t["bc"] = np.where(np.isin(np.arange(P), (2, 3, 4))[:, None], 1.0, 0.0) * np.ones((P, P))
    t["half"] = np.full((P, 1), -0.5)
    return (np.concatenate([np.asarray(t[n], np.float32).reshape(P, w) for n, w in CONSTS], 1),
            dec.reshape(P, 1024).astype(np.float32))


class Queue:

    def __init__(self, sem):
        self.sem, self.n, self.ops, self.met = sem, 0, [], {}
        self.dmas, self.open, self.soft = {}, [], set()

    def wait(self, *tickets):
        for t in tickets:
            if t is None:
                continue
            if isinstance(t, list):
                self.wait(*t)
                continue
            s, v = t
            if self.met.get(id(s), 0) < v:
                self.met[id(s)] = v
                self.ops.append(lambda e, s=s, v=v: e.wait_ge(s, v))

    def quiet(self, fn, *tickets):
        self.wait(*tickets)
        self.ops.append(fn)

    def __call__(self, fn, *tickets):
        self.wait(*tickets)
        self.n += 1
        self.ops.append(lambda e: fn(e).then_inc(self.sem, 1))
        return (self.sem, self.n)

    def activation(self, o, i, func, bias=0.0, scale=1.0, accum_out=None, after=()):
        return self(lambda e: e.activation(o, i, func, bias=bias, scale=scale, accum_out=accum_out), *after)

    def tensor_tensor(self, o, a, b, op, after=()):
        return self(lambda e: e.tensor_tensor(o, a, b, op), *after)

    def tensor_scalar(self, o, a, s1, s2, op0, op1=ALU.bypass, after=()):
        return self(lambda e: e.tensor_scalar(o, a, s1, s2, op0, op1), *after)

    def scalar_tensor_tensor(self, o, a, s, b, op0, op1, after=()):
        return self(lambda e: e.scalar_tensor_tensor(o, a, s, b, op0, op1), *after)

    def tensor_copy(self, o, i, after=()):
        return self(lambda e: e.tensor_copy(o, i), *after)

    def reciprocal(self, o, i, after=()):
        return self(lambda e: e.reciprocal(o, i), *after)

    def reduce_max(self, o, i, ax, negate=False, after=()):
        return self(lambda e: e.reduce_max(o, i, ax, negate=negate), *after)

    def reduce_sum(self, o, i, ax, after=()):
        return self(lambda e: e.reduce_sum(o, i, ax), *after)

    def bn_stats(self, o, i, after=()):
        return self(lambda e: e.bn_stats(o, i), *after)

    def bn_aggr(self, o, i, after=()):
        return self(lambda e: e.bn_aggr(o, i), *after)

    def memset(self, o, value, after=()):
        return self(lambda e: e.memset(o, value), *after)

    def gather_rows(self, o, table, index, sem, count, after=()):
        self.quiet(lambda e: e.indirect_dma_start(
            out=o, out_offset=None, in_=table,
            in_offset=bass.IndirectOffsetOnAxis(ap=index, axis=0)).then_inc(sem, 16), *after)
        self.soft.add(sem)
        self.dmas[sem] = 16 * count
        return (sem, 16 * count)

    def dma(self, out, in_, sem, count, *tickets):
        self.wait(*tickets)
        self.ops.append(lambda e: e.dma_start(out, in_).then_inc(sem, 16))
        self.dmas[sem] = 16 * count
        return (sem, 16 * count)

    def gather_either(self, o, table, short, count, limit, index, sem, times):
        def run(e):
            value = e.value_load(count, min_val=0, max_val=512)
            with e.If(value > limit):
                e.indirect_dma_start(out=o, out_offset=None, in_=table,
                                     in_offset=bass.IndirectOffsetOnAxis(ap=index, axis=0)).then_inc(sem, 16)
            with e.Else():
                e.indirect_dma_start(out=o, out_offset=None, in_=short,
                                     in_offset=bass.IndirectOffsetOnAxis(ap=index, axis=0)).then_inc(sem, 16)

        self.quiet(run)
        self.dmas[sem] = 16 * times
        self.soft.add(sem)
        return (sem, 16 * times)

    def begin(self):
        self.open.append((self.ops, dict(self.met), self.n, dict(self.dmas)))
        self.ops = []

    def end(self, count, limit):
        body, n1, dmas1 = self.ops, self.n, dict(self.dmas)
        self.ops, self.met, n0, dmas0 = self.open.pop()
        owed = [(self.sem, n0, n1 - n0)] if n1 > n0 else []
        owed += [(s, dmas0.get(s, 0), v - dmas0.get(s, 0)) for s, v in dmas1.items() if v > dmas0.get(s, 0)]

        def run(e):
            value = e.value_load(count, min_val=0, max_val=512)
            with e.If(value > limit):
                for op in body:
                    op(e)
            with e.Else():
                for s, v0, _ in owed:
                    if v0:
                        e.wait_ge(s, v0)
                for s, _, d in owed:
                    if s in self.soft:
                        e.inc_swdge_sem([s], [d], mode="add")
                    else:
                        e.sem_inc(s, d)

        self.ops.append(run)

    def play(self, e):
        for op in self.ops:
            op(e)


NRAW = 3
NSPLIT = 3
AHEAD = NSPLIT - 1


def build(nc, A, out, consts, decay, plan):
    with ExitStack() as ctx:
        def sb(name, shape, dt=F32):
            return ctx.enter_context(nc.sbuf_tensor(name, shape, dt))

        def sem(name):
            return ctx.enter_context(nc.semaphore(name))

        RAW = sb("RAW", [P, NRAW, 2048])
        HI = sb("HI", [P, NSPLIT, 2048], F32R)
        LO = sb("LO", [P, NSPLIT, 2048], F32R)
        FR = sb("FR", [P, 8192], F32R)
        CS = sb("CS", [P, 8, P], F32R)
        XL = sb("XL", [P, 2, D])
        XC = sb("XC", [P, 2, D])
        HB = sb("HB", [P, 2, D])
        GB = sb("GB", [P, 2, D])
        SC = sb("SC", [P, 13700])
        CN = sb("CN", [P, sum(w for _, w in CONSTS)])
        SM = sb("SM", [P, 1300])
        CNT = sb("CNT", [P, 17], U32)
        IDX = sb("IDX", [P, 72], U32)
        PS = [ctx.enter_context(nc.psum_tensor(f"PS{i}", [P, 512], F32)) for i in range(8)]
        HD = nc.dram_tensor("HD", [512, D], F32, kind="Internal").ap()
        YD = nc.dram_tensor("YD", [NE * 512, D], F32, kind="Internal").ap()

        pe, act, dve, pool, sp = (Queue(sem(n)) for n in ("s_pe", "s_act", "s_dve", "s_pool", "s_sp"))
        s_raw = [sem(f"s_raw{i}") for i in range(NRAW)]
        s_hd, s_yd, s_xg, s_yg = ([sem(f"{n}{i}") for i in range(2)] for n in ("s_hd", "s_yd", "s_xg", "s_yg"))
        s_gain = [sem(f"s_gain{i}") for i in range(2)]
        s_const, s_ctx, s_r, s_fill, s_out = (sem(n) for n in (
            "s_const", "s_ctx", "s_r", "s_fill", "s_out"))

        C, at = {}, 0
        for n, w in CONSTS:
            C[n] = CN[:, at:at + w]
            at += w
        ident = C["ident"]

        bank_free = [None] * 8
        buf_free = {}

        class Banks:
            def __init__(self, ids):
                self.ids, self.i = ids, 0

            def take(self):
                b = self.ids[self.i % len(self.ids)]
                self.i += 1
                return b

        def mm(o, l, r, start, stop, tr=False, skip=False):
            return lambda e: e.matmul(o, l, r, start=start, stop=stop, is_transpose=True) if tr else \
                e.matmul(o, l, r, start=start, stop=stop)

        def pe_group(items, *tickets):
            pe.wait(*tickets)
            for it in items[:-1]:
                pe.quiet(it)
            return pe(items[-1])

        n_const = [0]

        def const_load(q, o, i):
            n_const[0] += 1
            q.dma(o, i, s_const, n_const[0])

        class Small:
            def __init__(self):
                self.at = 0

            def __call__(self, n):
                self.at += n
                assert self.at <= 1300, self.at
                return SM[:, self.at - n:self.at]

        small = Small()
        const_load(act, CN[:, :], consts)
        const_load(act, XL[:, :, :], A["x"][0].rearrange("(t p) d -> p t d", p=P))
        XCF = XC[:, :, :].rearrange("p t d -> p (t d)")
        dec = XCF[:, 0:1024].rearrange("p (h b c) -> p h b c", h=4, b=2)
        const_load(act, XCF[:, 0:1024], decay)
        rnorm = [XCF[:, 1024 + 512 * i:1536 + 512 * i] for i in range(2)]
        bfor = [small(8) for _ in range(2)]
        for l in range(2):
            const_load(act, rnorm[l], A["ret_norm"][l:l + 1, :].partition_broadcast(P).rearrange("p a n -> p (a n)"))
            const_load(act, bfor[l], A["b_forget"][l:l + 1, :].partition_broadcast(P).rearrange("p a n -> p (a n)"))
        sink = small(16)
        const_load(act, sink, A["sink_a_2"][0:1, :].partition_broadcast(P).rearrange("p a n -> p (a n)"))
        subln = small(128)
        const_load(act, subln, A["subln_b_2"][0:1, :].partition_broadcast(P).rearrange("p a n -> p (a n)"))
        rbias = small(16)
        const_load(act, rbias, A["router_bias_2"].rearrange("(a n) -> a n", a=1).partition_broadcast(P)
                   .rearrange("p a n -> p (a n)"))
        lamb = small(256)
        const_load(act, lamb, A["lambda_b_2"][0].rearrange("a n -> (a n)").rearrange("(a n) -> a n", a=1)
                   .partition_broadcast(P).rearrange("p a n -> p (a n)"))
        crow = small(128)
        const_load(act, crow[0:8, :], A["c_2"][0].rearrange("(k p) -> k p", p=P))
        const_load(act, crow[8:16, :], A["c_ctx_2"].rearrange("(k p) -> k p", p=P))
        stat = small(512)
        loaded = (s_const, 16 * n_const[0])
        for q in (pe, act, dve, pool):
            q.wait(loaded)

        class Weights:
            def __init__(self):
                self.log, self.n, self.split, self.tick, self.part = [], 0, 0, {}, 0

            def fetch(self, n):
                at_, nk, ncol, _ = plan[n]
                r, s, w = n % NRAW, n % NSPLIT, nk * ncol
                raw = RAW[:, r, 0:w].rearrange("p (k c) -> p k c", k=nk)
                got = sp.dma(raw, chunk_ap(*at_), s_raw[r], n // NRAW + 1, self.lo.get(n - NRAW))
                free = self.tick.get(n - NSPLIT)
                hi = act.activation(HI[:, s, 0:w], RAW[:, r, 0:w], ACT.Copy, after=[got, free])
                self.lo[n] = dve.tensor_tensor(LO[:, s, 0:w], RAW[:, r, 0:w], HI[:, s, 0:w].bitcast(F32),
                    ALU.subtract, after=[hi, free])

            lo = {}

            def next(self, ap, nk, ncol):
                n = self.n
                self.n += 1
                self.log.append((ap, nk, ncol, self.part))
                assert plan is None or plan[n] == self.log[n]
                if plan is not None:
                    while self.split <= min(n + AHEAD, len(plan) - 1) and plan[self.split][3] == self.part:
                        self.fetch(self.split)
                        self.split += 1
                s, w = n % NSPLIT, nk * ncol
                v = [X[:, s, 0:w].rearrange("p (k c) -> p k c", k=nk) for X in (HI, LO)]
                return v[0], v[1], self.lo.get(n), n

            def done(self, n, ticket):
                self.tick[n] = ticket

        W = Weights()
        W.lo = {}
        engines = (sp, pool, act, dve, pe)

        def begin():
            W.part += 1
            for q in engines:
                q.begin()

        def end(count, limit):
            W.part += 1
            for q in engines:
                q.end(count, limit)

        def rows(w, k0, nk, c0, ncol):
            return (w, k0, nk, c0, ncol)

        def chunk_ap(w, k0, nk, c0, ncol):
            a = A[w[0]]
            for i in w[1:]:
                a = a[i]
            return a[k0 * P:(k0 + nk) * P, c0:c0 + ncol].rearrange("(k p) c -> p k c", p=P)

        def gemm(w, k0, nk, c0, ncol, xh, xl, tiles, banks, first, last, *tickets):
            hi, lo, ready, n = W.next(rows(w, k0, nk, c0, ncol), nk, ncol)
            pe.wait(ready, *tickets)
            done = []
            for i, t in enumerate(tiles):
                b = banks[i]
                if first:
                    pe.wait(bank_free[b])
                o = PS[b][:, 0:ncol]
                items = []
                for k in range(nk):
                    l, ll = xh[:, k, t * P:(t + 1) * P], xl[:, k, t * P:(t + 1) * P]
                    items += [mm(o, l, hi[:, k, :], first and k == 0, False), mm(o, l, lo[:, k, :], False, False),
                              mm(o, ll, hi[:, k, :], False, last and k == nk - 1)]
                done.append(pe_group(items))
            W.done(n, done[-1])
            return done

        def proj(w, c0, ncol, xh, xl, tiles, banks, *tickets):
            if ncol > 256:
                gemm(w, 0, 4, c0, ncol, xh[:, 0:4, :], xl[:, 0:4, :], tiles, banks, True, False, *tickets)
                return gemm(w, 4, 4, c0, ncol, xh[:, 4:8, :], xl[:, 4:8, :], tiles, banks, False, True)
            return gemm(w, 0, 8, c0, ncol, xh, xl, tiles, banks, True, True, *tickets)

        def to_T(src, nk, hi, lo, rot, ready, free=None):
            last = None
            for g in range(0, nk, 4):
                m = min(4, nk - g)
                b = rot.take()
                t = pe_group([mm(PS[b][:, k * P:(k + 1) * P], src[:, (g + k) * P:(g + k + 1) * P], ident, True, True,
                                 tr=True) for k in range(m)], ready, bank_free[b])
                v = PS[b][:, 0:m * P].rearrange("p (k c) -> p k c", k=m)
                a = act.activation(hi[:, g:g + m, :], v, ACT.Copy, after=[t, free])
                last = dve.tensor_tensor(lo[:, g:g + m, :], v, hi[:, g:g + m, :].bitcast(F32), ALU.subtract,
                    after=[a, free])
                bank_free[b] = last
            return last

        def to_T32(srcs, dst, rot, ready, free=None, eng=None):
            m = len(srcs)
            b = rot.take()
            t = pe_group([mm(PS[b][:, k * P:(k + 1) * P], s, ident, True, True, tr=True)
                          for k, s in enumerate(srcs)], ready, bank_free[b])
            v = PS[b][:, 0:m * P].rearrange("p (k c) -> p k c", k=m)
            if eng is dve:
                bank_free[b] = dve.tensor_copy(dst, v, after=[t, free])
            else:
                bank_free[b] = act.activation(dst, v, ACT.Copy, after=[t, free])
            return bank_free[b]

        n_gain = [0]
        gain_use = [None, None]

        def load_gain(row):
            i = n_gain[0] % 2
            n_gain[0] += 1
            t = sp.dma(GB[:, i, :], row.partition_broadcast(P).rearrange("p a n -> p (a n)"), s_gain[i],
                       (n_gain[0] + 1) // 2, gain_use[i])
            return GB[:, i, :], t, i

        def rstd_of(ss, n, eps, scale, ready):
            v = dve.tensor_scalar(ss, ss, scale, eps, ALU.mult, ALU.add, after=[ready])
            return pool.tensor_tensor(ss, ss, C["half"].to_broadcast([P, n]), ALU.pow, after=[v])

        def rms(src, dst, gain, col, ready, free=None):
            g, garr, slot = gain
            ss = stat[:, col:col + 1]
            a = act.activation(dst, src, ACT.Square, accum_out=ss, after=[ready, free])
            r = rstd_of(ss, 1, EPS, 1.0 / D, a)
            return dve.scalar_tensor_tensor(dst, src, ss, g, ALU.mult, ALU.mult, after=[r, garr])

        XTh = FR[:, 0:2048].rearrange("p (k t) -> p k t", k=8)
        XTl = FR[:, 2048:4096].rearrange("p (k t) -> p k t", k=8)

        h_free = [None, None]
        x_ready = [None, None]
        xt_free = [None]

        def norm_T(gain, rot):
            done = []
            for t in range(2):
                r = rms(XL[:, t, :], HB[:, t, :], gain, t, x_ready[t], h_free[t])
                d = to_T(HB[:, t, :], 8, XTh[:, :, t * P:(t + 1) * P], XTl[:, :, t * P:(t + 1) * P], rot, r, xt_free[0])
                h_free[t] = d
                gain_use[gain[2]] = r
                done.append(d)
            return done

        def swiglu_unit(xh, xl, tiles, rot, wa, wb, wo, blocks, sbuf, gbuf, gts, flush, ready):
            pend = None
            T = len(tiles)
            for j, blk in enumerate(list(blocks) + [None]):
                if pend is not None:
                    pj, pc, gr = pend
                    nk = pc // P
                    gh, gl = gts[pj % 2]
                    tl = []
                    for i in range(T):
                        d = to_T(gbuf[pj % 2][:, i, 0:pc], nk, gh[:, 0:nk, i * P:(i + 1) * P],
                                 gl[:, 0:nk, i * P:(i + 1) * P], rot, gr[i], buf_free.get(("gt", pj % 2)))
                        tl.append(d)
                    buf_free[("g", pj % 2)] = tl[-1]
                if blk is not None:
                    c0, ncol = blk
                    ba = [rot.take() for _ in range(T)]
                    ra = proj(wa[0], wa[1] + c0, ncol, xh, xl, tiles, ba, ready)
                    bb = [rot.take() for _ in range(T)]
                    sr = []
                    for i in range(T):
                        sr.append(act.activation(sbuf[j % 2][:, i, 0:ncol], PS[ba[i]][:, 0:ncol], ACT.Silu,
                            after=[ra[i], buf_free.get(("s", j % 2))]))
                        bank_free[ba[i]] = sr[i]
                    rb = proj(wb[0], wb[1] + c0, ncol, xh, xl, tiles, bb)
                    gr = []
                    for i in range(T):
                        gr.append(dve.tensor_tensor(gbuf[j % 2][:, i, 0:ncol], sbuf[j % 2][:, i, 0:ncol],
                            PS[bb[i]][:, 0:ncol], ALU.mult, after=[rb[i], sr[i], buf_free.get(("g", j % 2))]))
                        bank_free[bb[i]] = gr[i]
                    buf_free[("s", j % 2)] = gr[-1]
                if pend is not None:
                    buf_free[("gt", pj % 2)] = flush(pj, pc, gts[pj % 2], tl)
                pend = (j, ncol, gr) if blk is not None else None

        SC0 = [0]

        def sc(n):
            SC0[0] += n
            assert SC0[0] <= 13700, SC0[0]
            return SC[:, SC0[0] - n:SC0[0]]

        ffn_gt = [(FR[:, 4096 + 2048 * i:4096 + 2048 * i + 1024].rearrange("p (k t) -> p k t", k=4),
                   FR[:, 4096 + 2048 * i + 1024:4096 + 2048 * i + 2048].rearrange("p (k t) -> p k t", k=4))
                  for i in range(2)]

        def ffn(l, w_in, w_out, gain):
            rot = Banks([0, 1, 2, 3])
            SC0[0] = 0
            sbuf = [sc(1024).rearrange("p (t c) -> p t c", t=2) for _ in range(2)]
            gbuf = [sc(1024).rearrange("p (t c) -> p t c", t=2) for _ in range(2)]
            ready = norm_T(gain, rot)
            blocks = [(512 * j, 512) for j in range(5)] + [(2560, 256)]
            fin = []

            def flush(j, pc, gt, tl):
                gh, gl = gt
                c0 = 512 * j
                last = j == 5
                d = None
                for k in range(0, pc // P, 2):
                    hi, lo, rdy, n = W.next(rows(w_out, c0 // P + k, 2, 0, D), 2, D)
                    pe.wait(rdy, tl)
                    for t in range(2):
                        for h in range(2):
                            o = PS[4 + 2 * t + h][:, :]
                            st = j == 0 and k == 0
                            if st:
                                pe.wait(bank_free[4 + 2 * t + h])
                            items = []
                            for kk in range(2):
                                a, b = gh[:, k + kk, t * P:(t + 1) * P], gl[:, k + kk, t * P:(t + 1) * P]
                                hh, ll = hi[:, kk, 512 * h:512 * h + 512], lo[:, kk, 512 * h:512 * h + 512]
                                fl = last and k == pc // P - 2 and kk == 1
                                items += [mm(o, a, hh, st and kk == 0, False), mm(o, a, ll, False, False),
                                          mm(o, b, hh, False, fl)]
                            d = pe_group(items)
                            if last and k == pc // P - 2:
                                fin.append(d)
                    W.done(n, d)
                return d

            swiglu_unit(XTh, XTl, [0, 1], rot, (w_in, 0), (w_in, FF), None, blocks, sbuf, gbuf, ffn_gt, flush, ready)
            for t in range(2):
                for h in range(2):
                    b = 4 + 2 * t + h
                    xs = XL[:, t, 512 * h:512 * h + 512]
                    x_ready[t] = bank_free[b] = dve.scalar_tensor_tensor(xs, PS[b][:, :], 0.5, xs, ALU.mult, ALU.add,
                        after=[fin[2 * t + h]])
            xt_free[0] = fin[-1]

        OFF = {"rq": 0, "rk": 512, "rv": 1024, "rg": 1536, "fq": 2048, "fk": 2560, "fv": 3072, "ff": 3584,
               "gr": 3592, "gf": 4616}

        def sigmoid_from(psrc, dst, ready, free=None):
            a = act.activation(dst, psrc, ACT.Exp, scale=-1.0, after=[ready, free])
            b = dve.tensor_scalar(dst, dst, 1.0, None, ALU.add, after=[a])
            return dve.reciprocal(dst, dst, after=[b]), a

        def attend(units, rot, pbuf, ptbuf):
            n = len(units)
            st = [None] * n
            for i in range(n + 2):
                if i < n:
                    u = units[i]
                    w = u["w"]
                    pb = pbuf[i % len(pbuf)]
                    es = []
                    for m, qk in enumerate(u["qk"]):
                        b = rot.take()
                        pe.wait(bank_free[b])
                        s = pe_group(qk(PS[b]), u["ready"])
                        nm = stat[:, u["col"] + 4 * m:u["col"] + 4 * m + 1]
                        ss = stat[:, u["col"] + 4 * m + 1:u["col"] + 4 * m + 2]
                        x = dve.reduce_max(nm, PS[b][:, 0:w], AX, negate=True, after=[s])
                        if "negsink" in u:
                            x = dve.tensor_tensor(nm, nm, u["negsink"], ALU.min, after=[x])
                        pm = pb[:, 512 * m:512 * m + w]
                        y = act.activation(pm, PS[b][:, 0:w], ACT.Exp, bias=nm, accum_out=ss,
                            after=[x, buf_free.get(("p", i % len(pbuf)))])
                        bank_free[b] = y
                        if "negsink" in u:
                            q = stat[:, u["col"] + 4 * m + 2:u["col"] + 4 * m + 3]
                            z = act.activation(q, nm, ACT.Exp, bias=u["sink"], after=[x])
                            y = dve.tensor_tensor(ss, ss, q, ALU.add, after=[z, y])
                        r = u["rinv"][m]
                        y = dve.reciprocal(r, ss, after=[y])
                        es.append(y)
                    wt = u["weigh"](pb, es) if "weigh" in u else es[-1]
                    st[i] = [wt, pb, None]
                if 0 <= i - 1 < n:
                    u = units[i - 1]
                    k = u["w"] // P
                    wt, pb, _ = st[i - 1]
                    pt = ptbuf[(i - 1) % len(ptbuf)]
                    st[i - 1][2] = to_T32([pb[:, P * j:P * j + P] for j in range(k)],
                                          pt[:, 0:k * P].rearrange("p (k c) -> p k c", k=k), rot, wt,
                                          buf_free.get(("pt", (i - 1) % len(ptbuf))), dve if i % 2 else act)
                    buf_free[("p", (i - 1) % len(pbuf))] = st[i - 1][2]
                if 0 <= i - 2 < n:
                    u = units[i - 2]
                    k = u["w"] // P
                    pt = ptbuf[(i - 2) % len(ptbuf)]
                    if "out_free" in u:
                        pe.wait(u["out_free"]())
                    d = pe_group([mm(u["out"], pt[:, P * j:P * j + P], u["v"][j], j == 0, j == k - 1)
                                  for j in range(k)], st[i - 2][2])
                    buf_free[("pt", (i - 2) % len(ptbuf))] = d
                    if "then" in u:
                        u["then"](d)

        def split_heads(t, n):
            return t.rearrange("p (h d) -> p h d", h=n)

        def mixer(l, gain):
            w = ("w_in", l)
            rot = Banks([0, 1, 2, 3, 4, 5])
            ready = norm_T(gain, rot)
            SC0[0] = 0
            qT, kT, v, rg, fqT, fkT, fv = (sc(1024) for _ in range(7))
            tok = [sc(512) for _ in range(2)]
            tA, tB = sc(512), sc(512)
            pbuf = [sc(512) for _ in range(3)]
            ptbuf = [sc(256) for _ in range(2)]
            lfB = sc(2048).rearrange("p (t h c) -> p t h c", t=2, h=8)
            lf = sc(64)
            v3 = lambda a, t: a[:, 512 * t:512 * t + 512]
            tok_free = [None, None]
            fin = {}
            for name, dst in (("rq", qT), ("rk", kT)):
                bb = [rot.take(), rot.take()]
                r = proj(w, OFF[name], 512, XTh, XTl, [0, 1], bb, ready)
                for t in range(2):
                    cos = C["cos1"][:, 64 * t:64 * t + 64]
                    sin = C["sin1"][:, 64 * t:64 * t + 64]
                    src = PS[bb[t]][:, :].rearrange("p (h a d) -> p h a d", h=4, a=2)
                    a4 = tA.rearrange("p (h a d) -> p h a d", h=4, a=2)
                    b4 = tB.rearrange("p (h a d) -> p h a d", h=4, a=2)
                    o4 = tok[t].rearrange("p (h a d) -> p h a d", h=4, a=2)
                    fr = buf_free.get("rope")
                    x1 = dve.tensor_tensor(a4, src, cos.unsqueeze(1).unsqueeze(1).to_broadcast([P, 4, 2, 64]),
                        ALU.mult, after=[r[t], fr])
                    x2 = dve.tensor_tensor(b4[:, :, 0, :], src[:, :, 1, :], sin.unsqueeze(1).to_broadcast([P, 4, 64]),
                        ALU.mult, after=[fr])
                    x3 = dve.tensor_tensor(b4[:, :, 1, :], src[:, :, 0, :], sin.unsqueeze(1).to_broadcast([P, 4, 64]),
                        ALU.mult)
                    bank_free[bb[t]] = x3
                    pool.tensor_tensor(o4[:, :, 0, :], a4[:, :, 0, :], b4[:, :, 0, :], ALU.subtract,
                        after=[x3, tok_free[t]])
                    y = pool.tensor_tensor(o4[:, :, 1, :], a4[:, :, 1, :], b4[:, :, 1, :], ALU.add)
                    buf_free["rope"] = y
                    fin[name, t] = to_T32([tok[t][:, P * h:P * h + P] for h in range(4)],
                                          dst.rearrange("p (h c) -> p h c", h=4)[:, :, t * P:t * P + P], rot, y,
                                          eng=act)
                    tok_free[t] = fin[name, t]
            for name, dst in (("rv", v), ("fv", fv)):
                bb = [rot.take(), rot.take()]
                r = proj(w, OFF[name], 512, XTh, XTl, [0, 1], bb)
                for t in range(2):
                    fin[name, t] = bank_free[bb[t]] = act.activation(v3(dst, t), PS[bb[t]][:, :], ACT.Copy,
                        after=[r[t]])
            bb = [rot.take(), rot.take()]
            r = proj(w, OFF["rg"], 512, XTh, XTl, [0, 1], bb)
            for t in range(2):
                s, _ = sigmoid_from(PS[bb[t]][:, :], v3(rg, t), r[t])
                fin["rg", t] = bank_free[bb[t]] = dve.tensor_tensor(v3(rg, t), v3(rg, t), PS[bb[t]][:, :], ALU.mult,
                    after=[s])
            for name, dst, sca in (("fq", fqT, 0.125), ("fk", fkT, 1.0)):
                bb = [rot.take(), rot.take()]
                r = proj(w, OFF[name], 512, XTh, XTl, [0, 1], bb)
                for t in range(2):
                    y = bank_free[bb[t]] = act.activation(tok[t], PS[bb[t]][:, :], ACT.Copy, scale=sca,
                        after=[r[t], tok_free[t]])
                    fin[name, t] = to_T32([tok[t][:, P * h:P * h + P] for h in range(4)],
                                          dst.rearrange("p (h c) -> p h c", h=4)[:, :, t * P:t * P + P], rot, y,
                                          eng=act)
                    tok_free[t] = fin[name, t]
            bb = [rot.take(), rot.take()]
            r = proj(w, OFF["ff"], 8, XTh, XTl, [0, 1], bb)
            for t in range(2):
                z, e1, e2 = lf[:, 24 * t:24 * t + 8], lf[:, 24 * t + 8:24 * t + 16], lf[:, 24 * t + 16:24 * t + 24]
                x = bank_free[bb[t]] = dve.tensor_tensor(z, PS[bb[t]][:, 0:8], bfor[l], ALU.add, after=[r[t]])
                x1 = dve.tensor_scalar(e1, z, -1.0, None, ALU.mult, after=[x])
                x1 = dve.tensor_tensor(e1, e1, z, ALU.min, after=[x1])
                x2 = act.activation(e1, e1, ACT.Exp, after=[x1])
                x2 = dve.tensor_scalar(e1, e1, 1.0, None, ALU.add, after=[x2])
                x2 = act.activation(e2, e1, ACT.Ln, after=[x2])
                x3 = dve.tensor_scalar(z, z, 0.0, None, ALU.min, after=[x1])
                x3 = dve.tensor_tensor(z, z, e2, ALU.subtract, after=[x3, x2])
                fin["lf", t] = dve.tensor_copy(lfB[:, t, :, :], z.unsqueeze(2).to_broadcast([P, 8, P]), after=[x3])
            prev = None
            rr = [fin["rq", 0], fin["rq", 1], fin["rk", 0], fin["rk", 1], fin["rv", 0], fin["rv", 1]]
            rdone = []
            for h in range(5):
                if h < 4:
                    b = rot.take()
                    q, k = qT[:, 256 * h:256 * h + 256], kT[:, 256 * h:256 * h + 256]
                    s = pe_group([mm(PS[b][:, 0:256], k[:, 0:P], q, True, True),
                                  mm(PS[b][:, 256:384], k[:, P:256], q[:, P:256], True, True)], rr, bank_free[b])
                    pb = pbuf[h % 3]
                    x = dve.tensor_tensor(pb[:, 0:256], PS[b][:, 0:256],
                        dec[:, h, :, :].rearrange("p b c -> p (b c)"), ALU.mult,
                        after=[s, buf_free.get(("p", h % 3))])
                    x = bank_free[b] = dve.tensor_tensor(pb[:, 256:384], PS[b][:, 256:384], dec[:, h, 0, :], ALU.mult,
                        after=[s])
                if prev is not None:
                    ph, ppb, px = prev
                    vv = [v3(v, t)[:, P * ph:P * ph + P] for t in range(2)]
                    if ph == 0:
                        pe.wait(bank_free[6], bank_free[7])
                    d = pe_group([mm(PS[6][:, P * ph:P * ph + P], ppb[:, 0:P], vv[0], True, True),
                                  mm(PS[7][:, P * ph:P * ph + P], ppb[:, P:256], vv[0], True, False),
                                  mm(PS[7][:, P * ph:P * ph + P], ppb[:, 256:384], vv[1], False, True)], px)
                    buf_free[("p", ph % 3)] = d
                prev = (h, pb, x) if h < 4 else None
            RTh, RTl = (FR[:, 4096 + 1024 * i:5120 + 1024 * i].rearrange("p (k t) -> p k t", k=4) for i in range(2))
            FTh, FTl = (FR[:, 6144 + 1024 * i:7168 + 1024 * i].rearrange("p (k t) -> p k t", k=4) for i in range(2))
            rT = []
            for t in range(2):
                ra, rb = tA, tB
                ss = stat[:, 16 + 4 * t:20 + 4 * t]
                y = bank_free[6 + t] = act.activation(tok[t], PS[6 + t][:, :], ACT.Copy, after=[d, tok_free[t]])
                y1 = dve.tensor_tensor(tA, tok[t], tok[t], ALU.mult, after=[y, buf_free.get("rope")])
                y2 = dve.reduce_sum(ss, split_heads(tA, 4), AX, after=[y1])
                y3 = rstd_of(ss, 4, EPS, 1.0 / 128, y2)
                y4 = dve.tensor_tensor(split_heads(tok[t], 4), split_heads(tok[t], 4),
                    ss.unsqueeze(2).to_broadcast([P, 4, P]), ALU.mult, after=[y3])
                y5 = pool.tensor_tensor(v3(rg, t), v3(rg, t), rnorm[l], ALU.mult, after=[fin["rg", t]])
                y6 = dve.tensor_tensor(tok[t], tok[t], v3(rg, t), ALU.mult, after=[y4, y5])
                rT.append(to_T(tok[t], 4, RTh[:, :, t * P:t * P + P], RTl[:, :, t * P:t * P + P], rot, y6, xt_free[0]))
                tok_free[t] = rT[-1]
            units = []
            fr = [fin[n, t] for n in ("fq", "fk", "fv", "lf") for t in range(2)]
            rinv = stat[:, 32:48].rearrange("p (t h) -> p t h", t=2)
            for h in range(8):
                o = 64 * (h % 2)
                q = fqT[o:o + 64, 256 * (h // 2):256 * (h // 2) + 256]
                k = fkT[o:o + 64, 256 * (h // 2):256 * (h // 2) + 256]
                for t in range(2):
                    def qk(B, h=h, t=t, q=q, k=k):
                        if t == 0:
                            return [mm(B[:, 0:P], q[:, 0:P], k[:, 0:P], True, False),
                                    mm(B[:, 0:P], lfB[:, 0, h, :], C["negtri"], False, False),
                                    mm(B[:, 0:P], ident, C["cmask"], False, True)]
                        return [mm(B[:, 0:256], q[:, P:256], k, True, False),
                                mm(B[:, 0:P], lfB[:, 0, h, :], C["negtri"], False, False),
                                mm(B[:, P:256], lfB[:, 0, h, :], C["negones"], False, False),
                                mm(B[:, P:256], lfB[:, 1, h, :], C["negtri"], False, False),
                                mm(B[:, P:256], ident, C["cmask"], False, True)]
                    u = {"w": 128 * (t + 1), "qk": [qk], "ready": fr, "col": 64 + 8 * (2 * h + t),
                         "rinv": [rinv[:, t, h:h + 1]], "out": PS[6 + t][:, 64 * h:64 * h + 64],
                         "v": [v3(fv, s)[:, 64 * h:64 * h + 64] for s in range(2)]}
                    if h == 0:
                        u["out_free"] = lambda t=t: bank_free[6 + t]
                    if h == 7:
                        u["then"] = lambda d, t=t: fin.__setitem__(("fo", t), d)
                    units.append(u)
            attend(units, rot, pbuf, ptbuf)
            fT = []
            for t in range(2):
                y = bank_free[6 + t] = dve.tensor_tensor(split_heads(tok[t], 8), split_heads(PS[6 + t][:, :], 8),
                    rinv[:, t, :].unsqueeze(2).to_broadcast([P, 8, 64]), ALU.mult, after=[fin["fo", t], tok_free[t]])
                fT.append(to_T(tok[t], 4, FTh[:, :, t * P:t * P + P], FTl[:, :, t * P:t * P + P], rot, y, xt_free[0]))
                tok_free[t] = fT[-1]
            mg_ready = {}
            for h in range(2):
                for wo, go, xh, xl_, rd in ((("w_o_ret", l), "gr", RTh, RTl, rT), (("w_o_fox", l), "gf", FTh, FTl, fT)):
                    bb = [rot.take(), rot.take()]
                    r = proj(w, OFF[go] + 512 * h, 512, XTh, XTl, [0, 1], bb)
                    sg = []
                    for t in range(2):
                        dst = (tA, tB)[t]
                        s, a = sigmoid_from(PS[bb[t]][:, :], dst, r[t], buf_free.get(("sg", t)))
                        bank_free[bb[t]] = a
                        sg.append(s)
                    yb = [rot.take(), rot.take()]
                    r = gemm(wo, 0, 4, 512 * h, 512, xh, xl_, [0, 1], yb, True, True, rd)
                    for t in range(2):
                        dst = (tA, tB)[t]
                        m = HB[:, t, 512 * h:512 * h + 512]
                        if go == "gr":
                            y = dve.tensor_tensor(m, dst, PS[yb[t]][:, :], ALU.mult, after=[r[t], sg[t], h_free[t]])
                            bank_free[yb[t]] = y
                            buf_free["sg", t] = y
                        else:
                            y = dve.tensor_tensor(dst, dst, PS[yb[t]][:, :], ALU.mult, after=[r[t], sg[t]])
                            bank_free[yb[t]] = y
                            y = dve.tensor_tensor(m, m, dst, ALU.add, after=[y, mg_ready[t, h]])
                            buf_free["sg", t] = y
                        mg_ready[t, h] = y
            xt_done = r[-1]
            mT = []
            for t in range(2):
                mT.append(to_T(HB[:, t, :], 8, XTh[:, :, t * P:t * P + P], XTl[:, :, t * P:t * P + P], rot,
                               [mg_ready[t, 0], mg_ready[t, 1]], xt_done))
                h_free[t] = mT[-1]
            for h in range(2):
                bb = [rot.take(), rot.take()]
                r = proj(("w_out", l), 512 * h, 512, XTh, XTl, [0, 1], bb, mT)
                for t in range(2):
                    xs = XL[:, t, 512 * h:512 * h + 512]
                    x_ready[t] = bank_free[bb[t]] = dve.tensor_tensor(xs, PS[bb[t]][:, :], xs, ALU.add, after=[r[t]])
            xt_free[0] = r[-1]
            buf_free["rope"] = None

        g_next = load_gain(A["norm_ffn1"][0:1, :])
        for l in range(2):
            g, g_next = g_next, load_gain(A["norm_mix"][l:l + 1, :])
            ffn(l, ("w_ffn1_in", l), ("w_ffn1_out", l), g)
            g, g_next = g_next, load_gain(A["norm_ffn2"][l:l + 1, :])
            mixer(l, g)
            g, g_next = g_next, load_gain(A["norm_ffn1"][1:2, :] if l == 0 else
                                          A["norm_final"].rearrange("(a n) -> a n", a=1))
            ffn(l, ("w_ffn2_in", l), ("w_ffn2_out", l), g)
        for t in range(2):
            x_ready[t] = rms(XL[:, t, :], HB[:, t, :], g_next, t, x_ready[t], h_free[t])
            gain_use[g_next[2]] = x_ready[t]
            x_ready[t] = act.activation(XL[:, t, :], HB[:, t, :], ACT.Copy, after=[x_ready[t]])
            h_free[t] = x_ready[t]

        SC0[0] = 0
        cs_z = dve.memset(CS[:, :, :].bitcast(F32), 0.0)
        ccol, csig = small(16), small(16)
        x = pe_group([mm(PS[0][:, 0:16], crow[0:16, :], ident[0:16, 0:16], True, True, tr=True)], bank_free[0])
        y = act.activation(ccol, PS[0][:, 0:16], ACT.Copy, after=[x])
        s, a = sigmoid_from(PS[0][:, 0:16], csig, x)
        bank_free[0] = [y, a]
        y = dve.tensor_tensor(ccol, ccol, csig, ALU.mult, after=[y, s])
        cv = ccol.rearrange("p (v k) -> p k v", v=2)
        cs4 = CS[:, :, 0:4].rearrange("p k (v a) -> p k v a", a=2)
        y = act.activation(cs4[:, :, :, 0], cv, ACT.Copy, after=[y, cs_z])
        cs_ready = dve.tensor_tensor(cs4[:, :, :, 1], cv, cs4[:, :, :, 0].bitcast(F32), ALU.subtract, after=[y])
        lt, l2 = small(128), small(2)
        y = dve.tensor_tensor(lt.rearrange("p (a n) -> p a n", a=2),
            lamb.rearrange("p (a b n) -> p a b n", a=2, b=2)[:, :, 0, :],
            lamb.rearrange("p (a b n) -> p a b n", a=2, b=2)[:, :, 1, :], ALU.mult)
        y = dve.reduce_sum(l2, lt.rearrange("p (a n) -> p a n", a=2), AX, after=[y])
        y = act.activation(l2, l2, ACT.Exp, after=[y])
        neglam = small(1)
        y = dve.tensor_tensor(neglam, l2[:, 1:2], l2[:, 0:1], ALU.subtract, after=[y])
        lam_ready = dve.tensor_scalar(neglam, neglam, -LAM_INIT, None, ALU.add, after=[y])
        negsink = small(16)
        sink_ready = dve.tensor_scalar(negsink, sink, -1.0, None, ALU.mult)
        subs_ready = dve.tensor_scalar(subln, subln, 1.0 - LAM_INIT, None, ALU.mult)

        n_r = [0]
        r_free = [None]
        RR = SC[0:5, 10628:13700]
        r_ready = [None]

        def ada(l, sec, rot):
            n_r[0] += 1
            bias = sp.dma(RR[4:5, :], A["b_ada_2"][l:l + 1, 3072 * sec:3072 * sec + 3072], s_r, n_r[0], r_free[0])
            y = None
            for c in range(6):
                b = rot.take()
                for hk in range(2):
                    hi, lo, rdy, n = W.next(rows(("w_ada_2", l), 4 * hk, 4, 3072 * sec + 512 * c, 512), 4, 512)
                    pe.wait(rdy, cs_ready)
                    if hk == 0:
                        pe.wait(bank_free[b])
                    items = []
                    for k in range(4):
                        cs = CS[:, 4 * hk + k, :]
                        items += [mm(PS[b][:, :], cs, hi[:, k, :], hk == 0 and k == 0, False),
                                  mm(PS[b][:, :], cs, lo[:, k, :], False, hk == 1 and k == 3)]
                    d = pe_group(items)
                    W.done(n, d)
                y = bank_free[b] = act.activation(RR[0:4, 512 * c:512 * c + 512], PS[b][0:4, :], ACT.Copy,
                    after=[d, r_free[0]])
            r_ready[0] = [y, bias]

        def spread(which, col, rot):
            b = rot.take()
            m = C["bl" if which == 0 else "bc"][0:5, :]
            t = pe_group([mm(PS[b][:, :], m, RR[:, col:col + 512], True, True)], r_ready[0], bank_free[b])
            r_free[0] = t
            return b, t

        def modulate(x, which, tiles, dsts, rot, ready, free):
            done = [None] * len(tiles)
            for h in range(2):
                bs, ts = spread(which, 1024 + 512 * h, rot)
                bh, th = spread(which, 512 * h, rot)
                for i, t in enumerate(tiles):
                    o = dsts[i][:, 512 * h:512 * h + 512]
                    xs = x[:, t, 512 * h:512 * h + 512]
                    y = dve.scalar_tensor_tensor(o, PS[bs][:, :], 1.0, xs, ALU.add, ALU.mult,
                        after=[ts, ready[i], free[i]])
                    bank_free[bs] = y
                    y = bank_free[bh] = dve.tensor_tensor(o, o, PS[bh][:, :], ALU.add, after=[y, th])
                    done[i] = y
            return done

        def layer_norm(x, gt, bt, col, ready):
            bn, mv = stat[:, col:col + 12], stat[:, col + 12:col + 14]
            y = None
            for h in range(2):
                y = dve.bn_stats(bn[:, 6 * h:6 * h + 6], x[:, 512 * h:512 * h + 512], after=[ready])
            y = dve.bn_aggr(mv, bn, after=[y])
            y = rstd_of(mv[:, 1:2], 1, EPS, 1.0, y)
            y = dve.tensor_scalar(x, x, mv[:, 0:1], mv[:, 1:2], ALU.subtract, ALU.mult, after=[y])
            y = dve.tensor_tensor(x, x, gt[0], ALU.mult, after=[y, gt[1]])
            y = dve.tensor_tensor(x, x, bt[0], ALU.add, after=[y, bt[1]])
            gain_use[gt[2]] = gain_use[bt[2]] = y
            return y

        ctx_in = sp.dma(XC[:, :, :], A["ctx_2"][0].rearrange("(t p) d -> p t d", p=P), s_ctx, 1, x_ready)
        c_ready = [ctx_in, ctx_in]

        def residual(x, t, u, gate, col, gt, bt, ready):
            y = dve.tensor_tensor(u, u, gate, ALU.mult, after=[ready])
            y = dve.scalar_tensor_tensor(x[:, t, :], x[:, t, :], ALPHA, u, ALU.mult, ALU.add, after=[y])
            h = y
            return layer_norm(x[:, t, :], gt, bt, col, y), h

        def gate_tile(which, dst, rot, free=None):
            y = None
            for h in range(2):
                b, t = spread(which, 2048 + 512 * h, rot)
                y = bank_free[b] = act.activation(dst[:, 512 * h:512 * h + 512], PS[b][:, :], ACT.Copy,
                    after=[t, free])
            return y

        X4h = FR[:, 0:4096].rearrange("p (k t) -> p k t", k=8)
        X4l = FR[:, 4096:8192].rearrange("p (k t) -> p k t", k=8)

        def hidden_T(nctx, rot, to_dram=None):
            done = []
            for which in range(2 if nctx else 1):
                x = XC if which else XL
                rd = c_ready if which else x_ready
                hs = modulate(x, which, [0, 1], [HB[:, 0, :], HB[:, 1, :]], rot, rd, h_free)
                for t in range(2):
                    g = 2 * which + t
                    fr = []
                    if to_dram is not None:
                        fr = [to_dram(g, HB[:, t, :], hs[t])]
                    d = to_T(HB[:, t, :], 8, X4h[:, :, g * P:g * P + P], X4l[:, :, g * P:g * P + P], rot, hs[t],
                             xt_free[0])
                    done.append(d)
                    h_free[t] = [d] + fr
            return done

        def rope2(src, dst, t, nh, ready, tmp, free, pairs=False):
            cos, sin = C["cos2"][:, 64 * t:64 * t + 64], C["sin2"][:, 64 * t:64 * t + 64]
            a, bq = tmp[0][:, 0:64 * nh], tmp[1][:, 0:64 * nh]
            v5 = lambda z: z.rearrange("p (h b a d) -> p h b a d", h=nh, b=2, a=2)
            s4 = sin.rearrange("p (b a d) -> p b a d", b=2, a=2)
            fr = buf_free.get("rope")
            x = dve.tensor_tensor(split_heads(a, nh), split_heads(src, nh),
                cos.unsqueeze(1).to_broadcast([P, nh, 64]), ALU.mult, after=[ready, fr])
            for half in range(2):
                x = dve.tensor_tensor(v5(bq)[:, :, :, half, :], v5(src)[:, :, :, 1 - half, :],
                    s4[:, :, half, :].unsqueeze(1).to_broadcast([P, nh, 2, 16]), ALU.mult, after=[fr])
            if pairs:
                dst, a, bq = paired(dst), a.rearrange("p (v g d) -> p v g d", v=2, g=4), \
                    bq.rearrange("p (v g d) -> p v g d", v=2, g=4)
            y = pool.tensor_tensor(dst, a, bq, ALU.add, after=[x, free])
            buf_free["rope"] = y
            return y, x

        def paired(dst):
            return dst.rearrange("p (g v d) -> p v g d", g=4, v=2)

        def attn_a(rot):
            SC0[0] = 0
            qT, kT, v = sc(4096), sc(1024), sc(1024)
            tok = [sc(512) for _ in range(2)]
            pbuf = [sc(512) for _ in range(3)]
            ptbuf = [sc(512) for _ in range(2)]
            tmp = pbuf[0:2]
            assert SC0[0] <= 10628
            w = ("wqkv_a_2", 0)
            ready = hidden_T(True, rot)
            q4 = qT.rearrange("p (n t) -> p n t", n=8)
            k4 = kT.rearrange("p (n t) -> p n t", n=2)
            fin = []
            tf = [None, None]
            ti = 0
            for blk in (2, 0, 1):
                bb = [rot.take() for _ in range(4)]
                r = proj(w, 512 * blk, 512, X4h, X4l, [0, 1, 2, 3], bb, ready)
                for t in range(4):
                    src = PS[bb[t]][:, :]
                    dst = tok[ti % 2]
                    if blk == 2:
                        if t < 2:
                            y, x = rope2(src[:, 0:256], dst[:, 0:256], t, 4, r[t], tmp, tf[ti % 2])
                        else:
                            y = x = act.activation(dst[:, 0:256], src[:, 0:256], ACT.Copy, after=[r[t], tf[ti % 2]])
                        z = act.activation(v[:, 256 * t:256 * t + 256], src[:, 256:512], ACT.Copy, after=[r[t], x])
                        bank_free[bb[t]] = [x, z]
                        fin.append(z)
                        tf[ti % 2] = to_T32([dst[:, P * n:P * n + P] for n in range(2)],
                                            k4[:, :, t * P:t * P + P], rot2, y, eng=act)
                    else:
                        if t < 2:
                            y, x = rope2(src, dst, t, 8, r[t], tmp, tf[ti % 2], pairs=True)
                        else:
                            y = x = act.activation(paired(dst), src.rearrange("p (v g d) -> p v g d", v=2, g=4),
                                ACT.Copy, after=[r[t], tf[ti % 2]])
                        bank_free[bb[t]] = x
                        tf[ti % 2] = to_T32([dst[:, P * g:P * g + P] for g in range(4)],
                                            q4[:, 4 * blk:4 * blk + 4, t * P:t * P + P], rot2, y, eng=act)
                    fin.append(tf[ti % 2])
                    ti += 1
            xt_free[0] = r[-1]
            rinv = stat[:, 448:464]
            oT = []
            buf_free["p", 0] = buf_free["p", 1] = buf_free["rope"]
            rot3 = Banks([0, 1, 2, 3, 4, 5])
            qs = dve.tensor_scalar(qT, qT, 0.125, None, ALU.mult, after=[fin])
            for t in range(4):
                units = []
                hold = {}
                for h in range(16):
                    kv, g = h // 4, h % 4
                    o = 64 * (kv % 2)
                    q = q4[o:o + 64, 4 * (kv // 2) + g, t * P:t * P + P]
                    k = k4[o:o + 64, kv // 2, :]
                    if t < 2:
                        def qk(B, q=q, k=k, t=t):
                            m = (B[:, P:256], C["cmask"]) if t == 0 else (B[:, 0:P], C["wmask"])
                            return [mm(B[:, 0:512], q, k, True, False), mm(m[0], ident, m[1], False, True)]
                        vt = [0, 1, 2, 3]
                    else:
                        def qk(B, q=q, k=k):
                            return [mm(B[:, 0:256], q, k[:, 256:512], True, True)]
                        vt = [2, 3]
                    u = {"w": P * len(vt), "qk": [qk], "ready": [qs] + fin, "col": 64 + 8 * (h % 16),
                         "rinv": [rinv[:, h:h + 1]], "negsink": negsink[:, h:h + 1], "sink": sink[:, h:h + 1],
                         "out": PS[6 + h // 8][:, 64 * (h % 8):64 * (h % 8) + 64],
                         "v": [v[:, 256 * s + 64 * kv:256 * s + 64 * kv + 64] for s in vt]}
                    if h % 8 == 0:
                        u["out_free"] = lambda h=h: bank_free[6 + h // 8]
                    if h == 15:
                        u["then"] = lambda d: hold.__setitem__("d", d)
                    units.append(u)
                act.wait(sink_ready)
                attend(units, rot3, pbuf, ptbuf)
                hb = HB[:, t % 2, :]
                y = None
                for hh in range(2):
                    y = bank_free[6 + hh] = dve.tensor_tensor(split_heads(hb[:, 512 * hh:512 * hh + 512], 8),
                        split_heads(PS[6 + hh][:, :], 8),
                        rinv[:, 8 * hh:8 * hh + 8].unsqueeze(2).to_broadcast([P, 8, 64]), ALU.mult,
                        after=[hold["d"], h_free[t % 2]])
                d = to_T(hb, 8, X4h[:, :, t * P:t * P + P], X4l[:, :, t * P:t * P + P], rot3, y, xt_free[0])
                h_free[t % 2] = d
                oT.append(d)
            return oT

        def attn_b(rot):
            SC0[0] = 0
            qT, kT, v = sc(2048), sc(4096), None
            tok = [sc(512) for _ in range(2)]
            pbuf = [sc(1024) for _ in range(2)]
            ptbuf = [sc(512) for _ in range(2)]
            tmp = [pbuf[0][:, 0:512], pbuf[1][:, 0:512]]
            assert SC0[0] <= 10628
            w = ("wqkv_b_2", 0)
            ready = hidden_T(True, rot)
            q4 = qT.rearrange("p (n t) -> p n t", n=8)
            k4 = kT.rearrange("p (n t) -> p n t", n=8)
            vt = [XC[:, 0, :], XC[:, 1, :], VX[:, 0:1024], VX[:, 1024:2048]]
            fin, tf, ti = [], [None, None], 0
            ctx_dead = ready
            for blk in range(6):
                tiles = [0, 1] if blk < 2 else [0, 1, 2, 3]
                bb = [rot.take() for _ in tiles]
                r = proj(w, 512 * blk, 512, X4h, X4l, tiles, bb, ready)
                for t in tiles:
                    src, dst = PS[bb[t]][:, :], tok[ti % 2]
                    if blk >= 4:
                        z = bank_free[bb[t]] = act.activation(vt[t][:, 512 * (blk - 4):512 * (blk - 4) + 512], src,
                            ACT.Copy, after=[r[t], ctx_dead])
                        fin.append(z)
                        continue
                    if t < 2:
                        y, x = rope2(src, dst, t, 8, r[t], tmp, tf[ti % 2])
                    else:
                        y = x = act.activation(dst, src, ACT.Copy, after=[r[t], tf[ti % 2]])
                    bank_free[bb[t]] = x
                    dd = (q4 if blk < 2 else k4)[:, 4 * (blk % 2):4 * (blk % 2) + 4, t * P:t * P + P]
                    tf[ti % 2] = to_T32([dst[:, P * n:P * n + P] for n in range(4)], dd, rot2, y, eng=act)
                    fin.append(tf[ti % 2])
                    ti += 1
            xt_free[0] = r[-1]
            buf_free["p", 0] = buf_free["p", 1] = buf_free["rope"]
            rot3 = Banks([0, 1, 2, 3, 4, 5])
            qs = dve.tensor_scalar(qT, qT, 0.125, None, ALU.mult, after=[fin])
            rinv = stat[:, 448:480]
            oT = []
            for t in range(2):
                units, hold = [], {}
                for h in range(8):
                    qks = []
                    for m in range(2):
                        qks.append(lambda B, h=h, m=m, t=t: [mm(
                            B[:, 0:512], q4[64 * m:64 * m + 64, h, t * P:t * P + P], k4[64 * m:64 * m + 64, h, :],
                            True, True)])
                    r0, r1 = rinv[:, 2 * h:2 * h + 1], rinv[:, 2 * h + 1:2 * h + 2]

                    def weigh(pb, es, r0=r0, r1=r1):
                        y = dve.tensor_tensor(r1, r1, neglam, ALU.mult, after=[es, lam_ready])
                        y = dve.tensor_scalar(pb[:, 512:1024], pb[:, 512:1024], r1, None, ALU.mult, after=[y])
                        return dve.scalar_tensor_tensor(pb[:, 0:512], pb[:, 0:512], r0, pb[:, 512:1024], ALU.mult,
                            ALU.add, after=[y])
                    u = {"w": 512, "qk": qks, "ready": [qs] + fin, "col": 64 + 8 * h, "rinv": [r0, r1],
                         "weigh": weigh, "out": PS[6 + h // 4][:, P * (h % 4):P * (h % 4) + P],
                         "v": [vt[s][:, P * h:P * h + P] for s in range(4)]}
                    if h % 4 == 0:
                        u["out_free"] = lambda h=h: bank_free[6 + h // 4]
                    if h == 7:
                        u["then"] = lambda d: hold.__setitem__("d", d)
                    units.append(u)
                attend(units, rot3, pbuf, ptbuf)
                hb = HB[:, t, :]
                ss = stat[:, 480 + 8 * t:488 + 8 * t]
                for hh in range(2):
                    y = bank_free[6 + hh] = act.activation(hb[:, 512 * hh:512 * hh + 512], PS[6 + hh][:, :], ACT.Copy,
                        after=[hold["d"], h_free[t]])
                    sq = pbuf[0][:, 512 * hh:512 * hh + 512]
                    y = dve.tensor_tensor(sq, hb[:, 512 * hh:512 * hh + 512], hb[:, 512 * hh:512 * hh + 512],
                        ALU.mult, after=[y, buf_free["p", 0]])
                    y = dve.reduce_sum(ss[:, 4 * hh:4 * hh + 4], split_heads(sq, 4), AX, after=[y])
                buf_free["p", 0] = y
                y = rstd_of(ss, 8, 1e-5, 1.0 / 128, y)
                y = dve.tensor_tensor(split_heads(hb, 8), split_heads(hb, 8), ss.unsqueeze(2).to_broadcast([P, 8, P]),
                    ALU.mult, after=[y])
                y = dve.tensor_tensor(split_heads(hb, 8), split_heads(hb, 8),
                    subln.unsqueeze(1).to_broadcast([P, 8, P]), ALU.mult, after=[y, subs_ready])
                d = to_T(hb, 8, X4h[:, :, t * P:t * P + P], X4l[:, :, t * P:t * P + P], rot3, y, xt_free[0])
                h_free[t] = d
                oT.append(d)
            return oT

        VX = SC[:, 10240:12288]

        def attn_out(l, wo, tiles, oT, rot):
            gl = load_gain(A["ln_attn_g_2"][l:l + 1, :])
            bl = load_gain(A["ln_attn_b_2"][l:l + 1, :])
            SC0[0] = 0
            gates = [sc(1024), sc(1024)]
            u = [sc(1024) for _ in range(4)]
            gr = [gate_tile(w, gates[w], rot, oT) for w in range(2 if len(tiles) > 2 else 1)]
            ur = {}
            for h in range(2):
                bb = [rot.take() for _ in tiles]
                r = proj(wo, 512 * h, 512, X4h, X4l, tiles, bb, oT)
                for i, t in enumerate(tiles):
                    us = u[t][:, 512 * h:512 * h + 512]
                    ur[t, h] = bank_free[bb[i]] = act.activation(us, PS[bb[i]][:, :], ACT.Copy, after=[r[i], oT])
            xt_free[0] = r[-1]
            for t in tiles:
                x, rd = (XL, x_ready) if t < 2 else (XC, c_ready)
                y, _ = residual(x, t % 2, u[t], gates[t // 2], 16 * t, gl, bl,
                                [ur[t, 0], ur[t, 1], gr[t // 2], rd[t % 2]])
                rd[t % 2] = y

        n_fill = [0]
        n_hd, n_yd, n_xg, n_yg = [0, 0], [0, 0], [0, 0], [0, 0]

        def both(sems, counts):
            return [(sems[i], 16 * counts[i]) for i in range(2) if counts[i]]

        hd_free = [None]
        yd_free = [None]

        def top(b, n, ranks, tmp, lim, ready):
            big = tmp[0].rearrange("p (g i j) -> p g i j", i=4, j=4)[:, 0:n, :, :]
            eq = tmp[1].rearrange("p (g i j) -> p g i j", i=4, j=4)[:, 0:n, :, :]
            bj = b.unsqueeze(2).to_broadcast([P, n, 4, 4])
            bi = b.unsqueeze(3).to_broadcast([P, n, 4, 4])
            lt = C["lt4"].rearrange("p (i j) -> p i j", i=4).unsqueeze(1).to_broadcast([P, n, 4, 4])
            x = dve.tensor_tensor(big, bj, bi, ALU.is_gt, after=[ready])
            y = dve.tensor_tensor(eq, bj, bi, ALU.is_equal, after=[ready])
            y = dve.tensor_tensor(eq, eq, lt, ALU.mult, after=[y])
            y = dve.tensor_tensor(big, big, eq, ALU.add, after=[x, y])
            y = dve.reduce_sum(ranks, big, AX, after=[y])
            return dve.tensor_scalar(ranks, ranks, lim, None, ALU.is_lt, after=[y])

        def moe(l, NT):
            gl = load_gain(A["ln_ffn_g_2"][l:l + 1, :])
            bl = load_gain(A["ln_ffn_b_2"][l:l + 1, :])
            rot = Banks(list(range(8)))
            rows_out = []

            def to_dram(g, h, rd):
                n_hd[g % 2] += 1
                return sp.dma(HD[g * P:g * P + P, :], h, s_hd[g % 2], n_hd[g % 2], rd, hd_free[0])

            ready = hidden_T(NT == 4, rot, to_dram)
            hd_ready = both(s_hd, n_hd)
            SC0[0] = 0
            N16 = NT * 16
            z = [sc(64)[:, 0:N16] for _ in range(10)]
            tmp = [sc(256), sc(256)]
            gs, gsel, s2 = sc(16)[:, 0:NT * 4], sc(16)[:, 0:NT * 4], sc(64)
            xg = [sc(1024) for _ in range(2)]
            ysb = [sc(1024) for _ in range(2)]
            sbuf = [sc(512) for _ in range(2)]
            gbuf = [sc(512) for _ in range(2)]
            pe_b = [sc(128) for _ in range(4)]
            assert SC0[0] <= 10628, SC0[0]
            b = rot.take()
            hi, lo, rdy, n = W.next(rows(("w_router_2",), 0, 8, 0, 16), 8, 16)
            pe.wait(rdy, ready, bank_free[b])
            for t in range(NT):
                o = PS[b][:, 16 * t:16 * t + 16]
                it = []
                for k in range(8):
                    h, ll = X4h[:, k, t * P:t * P + P], X4l[:, k, t * P:t * P + P]
                    it += [mm(o, h, hi[:, k, :], k == 0, False), mm(o, h, lo[:, k, :], False, False),
                           mm(o, ll, hi[:, k, :], False, k == 7)]
                d = pe_group(it)
            W.done(n, d)
            xt_free[0] = d
            s, bb, ing, sel, wgt, posm, slot, t0, t1, t2 = z
            y, a = sigmoid_from(PS[b][:, 0:N16], s, d)
            bank_free[b] = a
            v3 = lambda q: q.rearrange("p (t e) -> p t e", t=NT)
            g4 = lambda q: q.rearrange("p (g j) -> p g j", j=4)
            y = dve.tensor_tensor(v3(bb), v3(s), rbias.unsqueeze(1).to_broadcast([P, NT, 16]), ALU.add, after=[y])
            y = top(g4(bb), NT * 4, g4(ing), tmp, 1.5, y)
            y = dve.tensor_tensor(t0, bb, ing, ALU.mult, after=[y])
            y = dve.reduce_sum(gs, g4(t0), AX, after=[y])
            y = top(g4(gs), NT, g4(gsel), tmp, 0.5, y)
            y = dve.tensor_tensor(g4(sel), g4(ing), gsel.unsqueeze(2).to_broadcast([P, NT * 4, 4]), ALU.mult,
                after=[y])
            sel_r = y
            y = dve.tensor_tensor(t0, s, sel, ALU.mult, after=[y])
            den, sl0, sl1, w0, w1 = (s2[:, 4 * i:4 * i + NT] for i in range(5))
            y = dve.reduce_sum(den, v3(t0), AX, after=[y])
            y = dve.reciprocal(den, den, after=[y])
            wr = dve.tensor_tensor(v3(wgt), v3(t0), den.unsqueeze(2).to_broadcast([P, NT, 16]), ALU.mult, after=[y])
            b = rot.take()
            pe.wait(bank_free[b], sel_r)
            for t in range(NT):
                d = pe_group([mm(PS[b][:, 16 * t:16 * t + 16], C["negtri" if u == t else "negones"],
                                 v3(sel)[:, u, :], u == 0, u == t) for u in range(t + 1)])
            d = pe_group([mm(PS[b][:, 64:80], C["negones"], v3(sel)[:, u, :], u == 0, u == NT - 1) for u in range(NT)])
            cf = s2[:, 32:49]
            y = dve.tensor_scalar(cf[:, 0:16], PS[b][:, 64:80], -1.0, None, ALU.mult, after=[d])
            y = dve.reduce_max(cf[:, 16:17], cf[:, 0:16], AX, after=[y])
            cnt_r = dve.tensor_copy(CNT[:, :], cf, after=[y])
            y = dve.tensor_scalar(posm, sel, -4096.0, 4095.0, ALU.mult, ALU.add, after=[sel_r])
            pos_r = dve.tensor_tensor(posm, posm, PS[b][:, 0:N16], ALU.subtract, after=[y, d])
            y = dve.tensor_tensor(v3(slot), C["eoff"].unsqueeze(1).to_broadcast([P, NT, 16]),
                v3(PS[b][:, 0:N16]), ALU.subtract, after=[d])
            for j in range(1, NT):
                y1 = dve.tensor_scalar(t0, PS[b][:, 0:N16], -(P * j + 1.0), float(NE * P - P), ALU.is_le, ALU.mult,
                                       after=[y, wr])
                y = dve.tensor_tensor(slot, slot, t0, ALU.add, after=[y1])
            bank_free[b] = y
            y1 = dve.tensor_tensor(t1, slot, sel, ALU.mult, after=[y])
            y1 = dve.reduce_max(sl1, v3(t1), AX, after=[y1])
            y2 = dve.tensor_scalar(t2, slot, -1.0, BIG, ALU.mult, ALU.add, after=[y])
            y2 = dve.tensor_tensor(t2, t2, sel, ALU.mult, after=[y2])
            y2 = dve.reduce_max(sl0, v3(t2), AX, after=[y2])
            y2 = dve.tensor_scalar(sl0, sl0, -1.0, BIG, ALU.mult, ALU.add, after=[y2])
            for sl, ww, yy, tt in ((sl0, w0, y2, t1), (sl1, w1, y1, t2)):
                y = dve.tensor_tensor(v3(tt), v3(slot), sl.unsqueeze(2).to_broadcast( [P, NT, 16]), ALU.is_equal,
                    after=[yy, y1, y2])
                y = dve.tensor_tensor(tt, tt, wgt, ALU.mult, after=[y, wr])
                w_r = dve.reduce_sum(ww, v3(tt), AX, after=[y])
            sidx = IDX[:, 64:64 + 2 * NT].rearrange("p (k t) -> p k t", k=2)
            dve.tensor_copy(sidx[:, 0, :], sl0, after=[y2])
            sidx_r = dve.tensor_copy(sidx[:, 1, :], sl1, after=[y1])

            def indices(e_list, j, icol, rdy):
                b = rot.take()
                pe.wait(bank_free[b])
                d = None
                for i, e_ in enumerate(e_list):
                    for t in range(NT):
                        q = (i * NT + t) % 4
                        col = posm[:, 16 * t + e_:16 * t + e_ + 1]
                        y = dve.tensor_scalar(pe_b[q], C["iota"], float(P * j), col, ALU.add, ALU.is_equal,
                            after=[rdy, buf_free.get(("pe", q))])
                        d = buf_free["pe", q] = pe_group([mm(PS[b][:, 2 * i:2 * i + 1], pe_b[q],
                                                             C["tid"][:, t:t + 1], t == 0, t == NT - 1)], y)
                m = len(e_list)
                r = bank_free[b] = dve.tensor_copy(IDX[:, icol:icol + m],
                    PS[b][:, 0:2 * m].rearrange("p (m a) -> p m a", a=2)[:, :, 0],
                    after=[d, buf_free.get(("idx", icol))])
                return r

            xts = [(FR[:, 2048 * i:2048 * i + 1024].rearrange("p (k t) -> p k t", k=8),
                    FR[:, 2048 * i + 1024:2048 * i + 2048].rearrange("p (k t) -> p k t", k=8)) for i in range(2)]
            gts = [(FR[:, 4096 + 1024 * i:4096 + 1024 * i + 512].rearrange("p (k t) -> p k t", k=4),
                    FR[:, 4608 + 1024 * i:4608 + 1024 * i + 512].rearrange("p (k t) -> p k t", k=4)) for i in range(2)]
            buf_free["xt", 0] = buf_free["xt", 1] = buf_free["gt", 0] = buf_free["gt", 1] = d

            def gather(i, icol, rdy):
                n_xg[i % 2] += 1
                return pool.gather_rows(xg[i % 2], HD[:, :], IDX[:, icol:icol + 1], s_xg[i % 2], n_xg[i % 2],
                                        after=[rdy, hd_ready, buf_free.get(("xg", i % 2))])

            xt_r, g_t = {}, {}

            def fetch(i, e_, j, rdy):
                g_t[i] = gather(i, 16 * j + e_, rdy)

            def prep(i):
                xh, xl_ = xts[i % 2]
                xt_r[i] = to_T(xg[i % 2], 8, xh, xl_, rot, g_t[i], buf_free["xt", i % 2])
                buf_free["xg", i % 2] = xt_r[i]

            def up(i, e_):
                xh, xl_ = xts[i % 2]
                ba, bb_ = rot.take(), rot.take()
                ra = proj(("w_gate_2", l, e_), 0, DE, xh, xl_, [0], [ba], xt_r[i])
                sr = bank_free[ba] = act.activation(sbuf[i % 2], PS[ba][:, :], ACT.Silu,
                                                    after=[ra, buf_free.get(("s", i % 2))])
                rb = proj(("w_up_2", l, e_), 0, DE, xh, xl_, [0], [bb_])
                buf_free["xt", i % 2] = rb[0]
                gr = bank_free[bb_] = dve.tensor_tensor(gbuf[i % 2], sbuf[i % 2], PS[bb_][:, :], ALU.mult,
                                                        after=[rb, sr, buf_free.get(("g", i % 2))])
                buf_free["s", i % 2] = gr
                return gr

            def turn(i, gr):
                gh, gw = gts[i % 2]
                buf_free["g", i % 2] = to_T(gbuf[i % 2], 4, gh, gw, rot, gr, buf_free["gt", i % 2])
                return buf_free["g", i % 2]

            def down(i, e_, j, tl, fill=None):
                gh, gw = gts[i % 2]
                for h in range(2):
                    by = rot.take()
                    r = gemm(("w_down_2", l, e_), 0, 4, 512 * h, 512, gh, gw, [0], [by], True, True, tl)
                    y = bank_free[by] = act.activation(ysb[i % 2][:, 512 * h:512 * h + 512], PS[by][:, :], ACT.Copy,
                                                       after=[r, buf_free.get(("y", i % 2))])
                buf_free["gt", i % 2] = r[0]
                n_yd[i % 2] += 1
                base = (j * NE + e_) * P
                buf_free["y", i % 2] = sp.dma(YD[base:base + P, :], ysb[i % 2], s_yd[i % 2], n_yd[i % 2], y, yd_free[0],
                                             fill)

            rdy = indices(list(range(NE)), 0, 0, pos_r)
            fetch(0, 0, 0, rdy)
            prep(0)
            gr = [None] * NE
            for i in range(NE + 1):
                if i + 1 < NE:
                    fetch(i + 1, i + 1, 0, rdy)
                if i:
                    tl = turn(i - 1, gr[i - 1])
                if i < NE:
                    gr[i] = up(i, i)
                if i + 1 < NE:
                    prep(i + 1)
                if i:
                    down(i - 1, i - 1, 0, tl)
            for q in engines:
                q.wait(cnt_r)
            i = NE
            for j in range(1, NT):
                begin()
                n_fill[0] += 1
                fill = sp.dma(YD[j * NE * P:(j + 1) * NE * P, :].rearrange("(n p) d -> p n d", p=P),
                              XL[:, 0, :].unsqueeze(1).to_broadcast([P, NE, D]), s_fill, n_fill[0], x_ready[0], yd_free[0])
                rdy = indices(list(range(NE)), j, 16 * j, pos_r)
                for e_ in range(NE):
                    begin()
                    fetch(i, e_, j, rdy)
                    prep(i)
                    down(i, e_, j, turn(i, up(i, e_)), fill)
                    end(CNT[0:1, e_:e_ + 1], P * j)
                    i += 1
                end(CNT[0:1, 16:17], P * j)
            r = [(pe.sem, pe.n)]
            xt_free[0] = buf_free["gt", 0] = buf_free["gt", 1] = r[0]
            hd_free[0] = both(s_xg, n_xg)
            yd_all = both(s_yd, n_yd) + [(s_fill, 16 * n_fill[0])]
            gates = [HB[:, 0, :], HB[:, 1, :]]
            gr = [gate_tile(w, gates[w], rot, h_free[w]) for w in range(2 if NT == 4 else 1)]
            ya = [(xg[0], xg[1]), (ysb[0], ysb[1])]
            yfree = [[buf_free["xg", 0], buf_free["xg", 1]], [yd_all]]
            for t in range(NT):
                pr = ya[t % 2]
                for k in range(2):
                    n_yg[t % 2] += 1
                    pool.wait(yd_all, sidx_r, yfree[t % 2])
                    got = pool.gather_either(pr[k], YD[0:NT * NE * P, :], YD[0:NE * P, :], CNT[0:1, 16:17], P,
                                             sidx[:, k, t:t + 1], s_yg[t % 2], n_yg[t % 2])
                y = dve.tensor_scalar(pr[0], pr[0], w0[:, t:t + 1], None, ALU.mult, after=[got, w_r])
                y = dve.scalar_tensor_tensor(pr[0], pr[1], w1[:, t:t + 1], pr[0], ALU.mult, ALU.add, after=[y])
                x, rd = (XL, x_ready) if t < 2 else (XC, c_ready)
                y, fr = residual(x, t % 2, pr[0], gates[t // 2], 16 * t, gl, bl, [y, gr[t // 2], rd[t % 2]])
                rd[t % 2] = y
                yfree[t % 2] = [fr]
                h_free[t // 2] = [fr, h_free[t // 2]] if False else [fr]
            yd_free[0] = both(s_yg, n_yg)

        r4 = Banks([0, 1, 2, 3, 4, 5])
        rot2 = Banks([4, 5, 6, 7])
        for l in range(2):
            rotp = Banks([0, 1, 2, 3])
            ada(l, 0, rotp)
            oT = (attn_a if l == 0 else attn_b)(rotp)
            attn_out(l, ("wo_a_2" if l == 0 else "wo_b_2", 0), [0, 1, 2, 3] if l == 0 else [0, 1], oT,
                     Banks(list(range(8))))
            ada(l, 1, Banks(list(range(8))))
            moe(l, 4 if l == 0 else 2)
        fin = sp.dma(out[0].rearrange("(t p) d -> p t d", p=P), XL[:, :, :], s_out, 1, x_ready[0], x_ready[1])
        sp.wait(fin, both(s_hd, n_hd), both(s_yd, n_yd))

        if plan is None:
            return W.log
        assert len(plan) == W.n and W.split == W.n
        block = ctx.enter_context(nc.Block())

        @block.sync
        def _(e):
            sp.play(e)

        @block.gpsimd
        def _(e):
            pool.play(e)

        @block.scalar
        def _(e):
            act.play(e)

        @block.vector
        def _(e):
            dve.play(e)

        @block.tensor
        def _(e):
            pe.play(e)


_INS = ["x", "norm_ffn1", "w_ffn1_in", "w_ffn1_out", "norm_mix", "w_in", "b_forget", "ret_norm", "w_o_ret", "w_o_fox",
        "w_out", "norm_ffn2", "w_ffn2_in", "w_ffn2_out", "norm_final", "c_2", "ctx_2", "c_ctx_2", "w_ada_2", "b_ada_2",
        "wqkv_a_2", "wo_a_2", "sink_a_2", "wqkv_b_2", "wo_b_2", "lambda_b_2", "subln_b_2", "ln_attn_g_2",
        "ln_attn_b_2", "ln_ffn_g_2", "ln_ffn_b_2", "w_router_2", "router_bias_2", "w_gate_2", "w_up_2", "w_down_2"]


def kernel(**inputs):
    import concourse.bacc as _bacc
    from concourse.bass_utils import run_bass_kernel_spmd as _run

    arrays = {f"in_{n}": np.ascontiguousarray(inputs[n]) for n in _INS}
    arrays["consts"], arrays["decay"] = constants()

    def program(plan):
        nc = _bacc.Bacc("TRN2", target_bir_lowering=False, num_devices=1)
        ap = {n: nc.dram_tensor(n, a.shape, mybir.dt.from_np(a.dtype), kind="ExternalInput").ap()
              for n, a in arrays.items()}
        out = nc.dram_tensor("out_0", (1, 256, D), F32, kind="ExternalOutput").ap()
        return nc, build(nc, {n: ap[f"in_{n}"] for n in _INS}, out, ap["consts"], ap["decay"], plan)

    _, plan = program(None)
    nc, _ = program(plan)
    r = _run(nc, [arrays], core_ids=[0])
    return r.results[0]["out_0"]
```

```python
from contextlib import ExitStack

import numpy as np

import concourse.bass as bass
from concourse import mybir

P = 128
D = 1024
FF = 2816
NE = 16
DE = 512
ALU = mybir.AluOpType
ACT = mybir.ActivationFunctionType
F32 = mybir.dt.float32
F32R = mybir.dt.float32r
U32 = mybir.dt.uint32
AX = mybir.AxisListType.X
EPS = 1e-6
ALPHA = 4.0 ** 0.25
LAM_INIT = 0.8 - 0.6 * float(np.exp(-0.3))
BIG = 16384.0

CONSTS = [("ident", 128), ("negtri", 128), ("negones", 128), ("cmask", 128), ("wmask", 128),
          ("cos1", 128), ("sin1", 128), ("cos2", 128), ("sin2", 128), ("iota", 128), ("tid", 4), ("lt4", 16),
          ("eoff", 16), ("bl", 128), ("bc", 128), ("half", 1)]


def constants():
    i = np.arange(P, dtype=np.float64)
    t = {}
    t["ident"] = np.eye(P)
    t["negtri"] = -(i[:, None] <= i[None, :]).astype(np.float64)
    t["negones"] = -np.ones((P, P))
    t["cmask"] = np.where(i[None, :] > i[:, None], -1e30, 0.0)
    t["wmask"] = np.where(i[None, :] < i[:, None], -1e30, 0.0)
    dec = np.zeros((P, 4, 2, P))
    for h in range(4):
        lg = np.log1p(-np.exp2(-5.0 - h))
        d = i[None, :] - i[:, None]
        dec[:, h, 0] = np.where(d >= 0, np.exp(lg * np.maximum(d, 0)), 0.0) * 128 ** -0.5
        dec[:, h, 1] = np.exp(lg * (128 + d)) * 128 ** -0.5
    tok = (np.arange(2)[None, :] * P + i[:, None]).astype(np.float32)
    inv = np.power(np.float32(10000.0), -np.arange(0, 128, 2, dtype=np.float32) / np.float32(128))
    ang = (tok[:, :, None] * inv).astype(np.float32).astype(np.float64)
    t["cos1"] = np.cos(ang).reshape(P, 128)
    t["sin1"] = np.sin(ang).reshape(P, 128)
    inv2 = np.power(np.float32(10000.0), -np.arange(16, dtype=np.float32) / np.float32(16))
    ar = ((tok // 64)[:, :, None] * inv2).astype(np.float32).astype(np.float64)
    ac = ((tok % 64)[:, :, None] * inv2).astype(np.float32).astype(np.float64)
    t["cos2"] = np.concatenate([np.cos(ar), np.cos(ar), np.cos(ac), np.cos(ac)], -1).reshape(P, 128)
    t["sin2"] = np.concatenate([-np.sin(ar), np.sin(ar), -np.sin(ac), np.sin(ac)], -1).reshape(P, 128)
    t["iota"] = np.broadcast_to(i[None, :], (P, P))
    t["tid"] = np.arange(4)[None, :] * P + i[:, None]
    t["lt4"] = np.broadcast_to((np.arange(4)[None, :] < np.arange(4)[:, None]).reshape(1, 16), (P, 16))
    t["eoff"] = np.broadcast_to(np.arange(16)[None, :] * P - 1.0, (P, 16))
    t["bl"] = np.where(np.isin(np.arange(P), (0, 1, 4))[:, None], 1.0, 0.0) * np.ones((P, P))
    t["bc"] = np.where(np.isin(np.arange(P), (2, 3, 4))[:, None], 1.0, 0.0) * np.ones((P, P))
    t["half"] = np.full((P, 1), -0.5)
    return (np.concatenate([np.asarray(t[n], np.float32).reshape(P, w) for n, w in CONSTS], 1),
            dec.reshape(P, 1024).astype(np.float32))


class Queue:

    def __init__(self, sem):
        self.sem, self.n, self.ops, self.met = sem, 0, [], {}
        self.dmas, self.open, self.soft = {}, [], set()

    def wait(self, *tickets):
        for t in tickets:
            if t is None:
                continue
            if isinstance(t, list):
                self.wait(*t)
                continue
            s, v = t
            if self.met.get(id(s), 0) < v:
                self.met[id(s)] = v
                self.ops.append(lambda e, s=s, v=v: e.wait_ge(s, v))

    def quiet(self, fn, *tickets):
        self.wait(*tickets)
        self.ops.append(fn)

    def __call__(self, fn, *tickets):
        self.wait(*tickets)
        self.n += 1
        self.ops.append(lambda e: fn(e).then_inc(self.sem, 1))
        return (self.sem, self.n)

    def activation(self, o, i, func, bias=0.0, scale=1.0, accum_out=None, after=()):
        return self(lambda e: e.activation(o, i, func, bias=bias, scale=scale, accum_out=accum_out), *after)

    def tensor_tensor(self, o, a, b, op, after=()):
        return self(lambda e: e.tensor_tensor(o, a, b, op), *after)

    def tensor_scalar(self, o, a, s1, s2, op0, op1=ALU.bypass, after=()):
        return self(lambda e: e.tensor_scalar(o, a, s1, s2, op0, op1), *after)

    def scalar_tensor_tensor(self, o, a, s, b, op0, op1, after=()):
        return self(lambda e: e.scalar_tensor_tensor(o, a, s, b, op0, op1), *after)

    def tensor_copy(self, o, i, after=()):
        return self(lambda e: e.tensor_copy(o, i), *after)

    def reciprocal(self, o, i, after=()):
        return self(lambda e: e.reciprocal(o, i), *after)

    def reduce_max(self, o, i, ax, negate=False, after=()):
        return self(lambda e: e.reduce_max(o, i, ax, negate=negate), *after)

    def reduce_sum(self, o, i, ax, after=()):
        return self(lambda e: e.reduce_sum(o, i, ax), *after)

    def bn_stats(self, o, i, after=()):
        return self(lambda e: e.bn_stats(o, i), *after)

    def bn_aggr(self, o, i, after=()):
        return self(lambda e: e.bn_aggr(o, i), *after)

    def memset(self, o, value, after=()):
        return self(lambda e: e.memset(o, value), *after)

    def gather_rows(self, o, table, index, sem, count, after=()):
        self.quiet(lambda e: e.indirect_dma_start(
            out=o, out_offset=None, in_=table,
            in_offset=bass.IndirectOffsetOnAxis(ap=index, axis=0)).then_inc(sem, 16), *after)
        self.soft.add(sem)
        self.dmas[sem] = 16 * count
        return (sem, 16 * count)

    def dma(self, out, in_, sem, count, *tickets):
        self.wait(*tickets)
        self.ops.append(lambda e: e.dma_start(out, in_).then_inc(sem, 16))
        self.dmas[sem] = 16 * count
        return (sem, 16 * count)

    def begin(self):
        self.open.append((self.ops, dict(self.met), self.n, dict(self.dmas)))
        self.ops = []

    def end(self, count, limit):
        body, n1, dmas1 = self.ops, self.n, dict(self.dmas)
        self.ops, self.met, n0, dmas0 = self.open.pop()
        owed = [(self.sem, n0, n1 - n0)] if n1 > n0 else []
        owed += [(s, dmas0.get(s, 0), v - dmas0.get(s, 0)) for s, v in dmas1.items() if v > dmas0.get(s, 0)]

        def run(e):
            value = e.value_load(count, min_val=0, max_val=512)
            with e.If(value > limit):
                for op in body:
                    op(e)
            with e.Else():
                for s, v0, _ in owed:
                    if v0:
                        e.wait_ge(s, v0)
                for s, _, d in owed:
                    if s in self.soft:
                        e.inc_swdge_sem([s], [d], mode="add")
                    else:
                        e.sem_inc(s, d)

        self.ops.append(run)

    def play(self, e):
        for op in self.ops:
            op(e)


NRAW = 4
SUB = 1024
NSPLIT = 5
AHEAD = NSPLIT - 1


def build(nc, A, out, consts, decay, plan):
    with ExitStack() as ctx:
        def sb(name, shape, dt=F32):
            return ctx.enter_context(nc.sbuf_tensor(name, shape, dt))

        def sem(name):
            return ctx.enter_context(nc.semaphore(name))

        RAW = sb("RAW", [P, NRAW, 2048])
        HI = sb("HI", [P, NSPLIT, SUB], F32R)
        LO = sb("LO", [P, NSPLIT, SUB], F32R)
        FR = sb("FR", [P, 8192], F32R)
        CS = sb("CS", [P, 8, P], F32R)
        XL = sb("XL", [P, 2, D])
        XC = sb("XC", [P, 2, D])
        HB = sb("HB", [P, 2, D])
        GB = sb("GB", [P, 2, D])
        SC = sb("SC", [P, 13700])
        CN = sb("CN", [P, sum(w for _, w in CONSTS)])
        SM = sb("SM", [P, 1300])
        CNT = sb("CNT", [P, 17], U32)
        IDX = sb("IDX", [P, 72], U32)
        PS = [ctx.enter_context(nc.psum_tensor(f"PS{i}", [P, 512], F32)) for i in range(8)]
        HD = nc.dram_tensor("HD", [512, D], F32, kind="Internal").ap()
        MOD = nc.dram_tensor("MOD", [2, 2, 4, 3072], F32, kind="Internal").ap()
        YD = nc.dram_tensor("YD", [NE * 512, D], F32, kind="Internal").ap()

        pe, act, dve, pool, sp = (Queue(sem(n)) for n in ("s_pe", "s_act", "s_dve", "s_pool", "s_sp"))
        s_raw = [sem(f"s_raw{i}") for i in range(NRAW)]
        s_hd, s_yd, s_xg, s_yg = ([sem(f"{n}{i}") for i in range(2)] for n in ("s_hd", "s_yd", "s_xg", "s_yg"))
        s_mod = [sem(f"s_mod{i}") for i in range(2)]
        s_gain = [sem(f"s_gain{i}") for i in range(2)]
        s_const, s_ctx, s_r, s_fill, s_out = (sem(n) for n in (
            "s_const", "s_ctx", "s_r", "s_fill", "s_out"))

        C, at = {}, 0
        for n, w in CONSTS:
            C[n] = CN[:, at:at + w]
            at += w
        ident = C["ident"]

        bank_free = [None] * 8
        buf_free = {}

        class Banks:
            def __init__(self, ids):
                self.ids, self.i = ids, 0

            def take(self):
                b = self.ids[self.i % len(self.ids)]
                self.i += 1
                return b

        def mm(o, l, r, start, stop, tr=False, skip=False):
            return lambda e: e.matmul(o, l, r, start=start, stop=stop, is_transpose=True) if tr else \
                e.matmul(o, l, r, start=start, stop=stop)

        def pe_group(items, *tickets):
            pe.wait(*tickets)
            for it in items[:-1]:
                pe.quiet(it)
            return pe(items[-1])

        n_const = [0]

        def const_load(q, o, i):
            n_const[0] += 1
            q.dma(o, i, s_const, n_const[0])

        class Small:
            def __init__(self):
                self.at = 0

            def __call__(self, n):
                self.at += n
                assert self.at <= 1300, self.at
                return SM[:, self.at - n:self.at]

        small = Small()
        const_load(act, CN[:, :], consts)
        const_load(act, XL[:, :, :], A["x"][0].rearrange("(t p) d -> p t d", p=P))
        XCF = XC[:, :, :].rearrange("p t d -> p (t d)")
        dec = XCF[:, 0:1024].rearrange("p (h b c) -> p h b c", h=4, b=2)
        const_load(act, XCF[:, 0:1024], decay)
        rnorm = [XCF[:, 1024 + 512 * i:1536 + 512 * i] for i in range(2)]
        bfor = [small(8) for _ in range(2)]
        for l in range(2):
            const_load(act, rnorm[l], A["ret_norm"][l:l + 1, :].partition_broadcast(P).rearrange("p a n -> p (a n)"))
            const_load(act, bfor[l], A["b_forget"][l:l + 1, :].partition_broadcast(P).rearrange("p a n -> p (a n)"))
        sink = small(16)
        const_load(act, sink, A["sink_a_2"][0:1, :].partition_broadcast(P).rearrange("p a n -> p (a n)"))
        subln = small(128)
        const_load(act, subln, A["subln_b_2"][0:1, :].partition_broadcast(P).rearrange("p a n -> p (a n)"))
        rbias = small(16)
        const_load(act, rbias, A["router_bias_2"].rearrange("(a n) -> a n", a=1).partition_broadcast(P)
                   .rearrange("p a n -> p (a n)"))
        lamb = small(256)
        const_load(act, lamb, A["lambda_b_2"][0].rearrange("a n -> (a n)").rearrange("(a n) -> a n", a=1)
                   .partition_broadcast(P).rearrange("p a n -> p (a n)"))
        crow = small(128)
        const_load(act, crow[0:8, :], A["c_2"][0].rearrange("(k p) -> k p", p=P))
        const_load(act, crow[8:16, :], A["c_ctx_2"].rearrange("(k p) -> k p", p=P))
        stat = small(512)
        loaded = (s_const, 16 * n_const[0])
        for q in (pe, act, dve, pool):
            q.wait(loaded)

        class Weights:
            def __init__(self):
                self.log, self.part = [], 0
                self.loaded = self.split = self.used = 0
                self.arrival, self.freed, self.ready, self.spent = {}, {}, {}, {}
                self.parts = []
                for n, (_, nk, ncol, region) in enumerate(plan or []):
                    ks = max(1, SUB // ncol)
                    for k in range(0, nk, ks):
                        self.parts.append((n, k, min(ks, nk - k), region))

            def load(self):
                while self.loaded < len(plan) and plan[self.loaded][3] == self.part and \
                        (self.loaded < NRAW or self.loaded - NRAW in self.freed):
                    n = self.loaded
                    at_, nk, ncol, _ = plan[n]
                    raw = RAW[:, n % NRAW, 0:nk * ncol].rearrange("p (k c) -> p k c", k=nk)
                    self.arrival[n] = sp.dma(raw, chunk_ap(*at_), s_raw[n % NRAW], n // NRAW + 1,
                                             self.freed.get(n - NRAW))
                    self.loaded += 1

            def split_next(self):
                m = self.split
                n, k, nk, _ = self.parts[m]
                ncol, s = plan[n][2], m % NSPLIT
                w = nk * ncol
                raw = RAW[:, n % NRAW, k * ncol:k * ncol + w]
                free = self.spent.get(m - NSPLIT)
                hi = act.activation(HI[:, s, 0:w], raw, ACT.Copy, after=[self.arrival[n], free])
                self.ready[m] = dve.tensor_tensor(LO[:, s, 0:w], raw, HI[:, s, 0:w].bitcast(F32), ALU.subtract,
                                                  after=[hi, free])
                if k + nk == plan[n][1]:
                    self.freed[n] = self.ready[m]
                self.split += 1

            def chunk(self, at_, nk, ncol):
                n = len(self.log)
                self.log.append((at_, nk, ncol, self.part))
                assert plan is None or plan[n] == self.log[n]
                ks = max(1, SUB // ncol)
                for k in range(0, nk, ks):
                    m = self.used
                    self.used += 1
                    if plan is not None:
                        self.load()
                        while self.split <= min(m + AHEAD, len(self.parts) - 1) and \
                                self.parts[self.split][3] == self.part:
                            self.split_next()
                            self.load()
                    kk = min(ks, nk - k)
                    hi, lo = (X[:, m % NSPLIT, 0:kk * ncol].rearrange("p (k c) -> p k c", k=kk) for X in (HI, LO))
                    yield k, kk, hi, lo, self.ready.get(m), m

        W = Weights()
        engines = (sp, pool, act, dve, pe)

        def begin():
            W.part += 1
            for q in engines:
                q.begin()

        def end(count, limit):
            W.part += 1
            for q in engines:
                q.end(count, limit)

        def rows(w, k0, nk, c0, ncol):
            return (w, k0, nk, c0, ncol)

        def chunk_ap(w, k0, nk, c0, ncol):
            a = A[w[0]]
            for i in w[1:]:
                a = a[i]
            return a[k0 * P:(k0 + nk) * P, c0:c0 + ncol].rearrange("(k p) c -> p k c", p=P)

        def gemm(w, k0, nk, c0, ncol, xh, xl, tiles, banks, first, last, *tickets):
            pe.wait(*tickets)
            for k, kk, hi, lo, ready, m in W.chunk(rows(w, k0, nk, c0, ncol), nk, ncol):
                pe.wait(ready)
                done = []
                for i, t in enumerate(tiles):
                    b = banks[i]
                    if first and k == 0:
                        pe.wait(bank_free[b])
                    o = PS[b][:, 0:ncol]
                    items = []
                    for q in range(kk):
                        h, ll = xh[:, k + q, t * P:(t + 1) * P], xl[:, k + q, t * P:(t + 1) * P]
                        items += [mm(o, h, hi[:, q, :], first and k + q == 0, False),
                                  mm(o, h, lo[:, q, :], False, False),
                                  mm(o, ll, hi[:, q, :], False, last and k + q == nk - 1)]
                    done.append(pe_group(items))
                W.spent[m] = done[-1]
            return done

        def proj(w, c0, ncol, xh, xl, tiles, banks, *tickets):
            if ncol > 256:
                gemm(w, 0, 4, c0, ncol, xh[:, 0:4, :], xl[:, 0:4, :], tiles, banks, True, False, *tickets)
                return gemm(w, 4, 4, c0, ncol, xh[:, 4:8, :], xl[:, 4:8, :], tiles, banks, False, True)
            return gemm(w, 0, 8, c0, ncol, xh, xl, tiles, banks, True, True, *tickets)

        def to_T(src, nk, hi, lo, rot, ready, free=None):
            last = None
            for g in range(0, nk, 4):
                m = min(4, nk - g)
                b = rot.take()
                t = pe_group([mm(PS[b][:, k * P:(k + 1) * P], src[:, (g + k) * P:(g + k + 1) * P], ident, True, True,
                                 tr=True) for k in range(m)], ready, bank_free[b])
                v = PS[b][:, 0:m * P].rearrange("p (k c) -> p k c", k=m)
                a = act.activation(hi[:, g:g + m, :], v, ACT.Copy, after=[t, free])
                last = dve.tensor_tensor(lo[:, g:g + m, :], v, hi[:, g:g + m, :].bitcast(F32), ALU.subtract,
                    after=[a, free])
                bank_free[b] = last
            return last

        def to_T32(srcs, dst, rot, ready, free=None, eng=None):
            m = len(srcs)
            b = rot.take()
            t = pe_group([mm(PS[b][:, k * P:(k + 1) * P], s, ident, True, True, tr=True)
                          for k, s in enumerate(srcs)], ready, bank_free[b])
            v = PS[b][:, 0:m * P].rearrange("p (k c) -> p k c", k=m)
            if eng is dve:
                bank_free[b] = dve.tensor_copy(dst, v, after=[t, free])
            else:
                bank_free[b] = act.activation(dst, v, ACT.Copy, after=[t, free])
            return bank_free[b]

        n_gain = [0]
        gain_use = [None, None]

        def load_gain(row):
            i = n_gain[0] % 2
            n_gain[0] += 1
            t = sp.dma(GB[:, i, :], row.partition_broadcast(P).rearrange("p a n -> p (a n)"), s_gain[i],
                       (n_gain[0] + 1) // 2, gain_use[i])
            return GB[:, i, :], t, i

        def rstd_of(ss, n, eps, scale, ready):
            v = dve.tensor_scalar(ss, ss, scale, eps, ALU.mult, ALU.add, after=[ready])
            return pool.tensor_tensor(ss, ss, C["half"].to_broadcast([P, n]), ALU.pow, after=[v])

        def rms(src, dst, gain, col, ready, free=None):
            g, garr, slot = gain
            ss = stat[:, col:col + 1]
            a = act.activation(dst, src, ACT.Square, accum_out=ss, after=[ready, free])
            r = rstd_of(ss, 1, EPS, 1.0 / D, a)
            return dve.scalar_tensor_tensor(dst, src, ss, g, ALU.mult, ALU.mult, after=[r, garr])

        XTh = FR[:, 0:2048].rearrange("p (k t) -> p k t", k=8)
        XTl = FR[:, 2048:4096].rearrange("p (k t) -> p k t", k=8)

        h_free = [None, None]
        x_ready = [None, None]
        xt_free = [None]

        def norm_T(gain, rot):
            done = []
            for t in range(2):
                r = rms(XL[:, t, :], HB[:, t, :], gain, t, x_ready[t], h_free[t])
                d = to_T(HB[:, t, :], 8, XTh[:, :, t * P:(t + 1) * P], XTl[:, :, t * P:(t + 1) * P], rot, r, xt_free[0])
                h_free[t] = d
                gain_use[gain[2]] = r
                done.append(d)
            return done

        def swiglu_unit(xh, xl, tiles, rot, wa, wb, wo, blocks, sbuf, gbuf, gts, flush, ready):
            pend = None
            T = len(tiles)
            for j, blk in enumerate(list(blocks) + [None]):
                if pend is not None:
                    pj, pc, gr = pend
                    nk = pc // P
                    gh, gl = gts[pj % 2]
                    tl = []
                    for i in range(T):
                        d = to_T(gbuf[pj % 2][:, i, 0:pc], nk, gh[:, 0:nk, i * P:(i + 1) * P],
                                 gl[:, 0:nk, i * P:(i + 1) * P], rot, gr[i], buf_free.get(("gt", pj % 2)))
                        tl.append(d)
                    buf_free[("g", pj % 2)] = tl[-1]
                if blk is not None:
                    fill_rows()
                    c0, ncol = blk
                    ba = [rot.take() for _ in range(T)]
                    ra = proj(wa[0], wa[1] + c0, ncol, xh, xl, tiles, ba, ready)
                    bb = [rot.take() for _ in range(T)]
                    sr = []
                    for i in range(T):
                        sr.append(act.activation(sbuf[j % 2][:, i, 0:ncol], PS[ba[i]][:, 0:ncol], ACT.Silu,
                            after=[ra[i], buf_free.get(("s", j % 2))]))
                        bank_free[ba[i]] = sr[i]
                    rb = proj(wb[0], wb[1] + c0, ncol, xh, xl, tiles, bb)
                    gr = []
                    for i in range(T):
                        gr.append(dve.tensor_tensor(gbuf[j % 2][:, i, 0:ncol], sbuf[j % 2][:, i, 0:ncol],
                            PS[bb[i]][:, 0:ncol], ALU.mult, after=[rb[i], sr[i], buf_free.get(("g", j % 2))]))
                        bank_free[bb[i]] = gr[i]
                    buf_free[("s", j % 2)] = gr[-1]
                if pend is not None:
                    buf_free[("gt", pj % 2)] = flush(pj, pc, gts[pj % 2], tl)
                pend = (j, ncol, gr) if blk is not None else None

        SC0 = [0]

        def sc(n):
            SC0[0] += n
            assert SC0[0] <= 13700, SC0[0]
            return SC[:, SC0[0] - n:SC0[0]]

        ffn_gt = [(FR[:, 4096 + 2048 * i:4096 + 2048 * i + 1024].rearrange("p (k t) -> p k t", k=4),
                   FR[:, 4096 + 2048 * i + 1024:4096 + 2048 * i + 2048].rearrange("p (k t) -> p k t", k=4))
                  for i in range(2)]

        n_fill = [0]

        def fill_rows():
            r = NE * P + 256 * n_fill[0]
            n_fill[0] += 1
            act.dma(YD[r:r + 256, :].rearrange("(n p) d -> p n d", p=P),
                    CN[:, 0:D].unsqueeze(1).to_broadcast([P, 2, D]), s_fill, n_fill[0])

        def ffn(l, w_in, w_out, gain):
            rot = Banks([0, 1, 2, 3])
            SC0[0] = 0
            sbuf = [sc(1024).rearrange("p (t c) -> p t c", t=2) for _ in range(2)]
            gbuf = [sc(1024).rearrange("p (t c) -> p t c", t=2) for _ in range(2)]
            ready = norm_T(gain, rot)
            blocks = [(512 * j, 512) for j in range(5)] + [(2560, 256)]
            fin = []

            def flush(j, pc, gt, tl):
                gh, gl = gt
                c0 = 512 * j
                last = j == 5
                d = None
                for k in range(0, pc // P, 2):
                    for q, _, hi, lo, rdy, m in W.chunk(rows(w_out, c0 // P + k, 2, 0, D), 2, D):
                        pe.wait(rdy, tl)
                        st, fl = j == 0 and k + q == 0, last and k + q == pc // P - 1
                        for t in range(2):
                            a, b = gh[:, k + q, t * P:(t + 1) * P], gl[:, k + q, t * P:(t + 1) * P]
                            for h in range(2):
                                o = PS[4 + 2 * t + h][:, :]
                                if st:
                                    pe.wait(bank_free[4 + 2 * t + h])
                                hh, ll = hi[:, 0, 512 * h:512 * h + 512], lo[:, 0, 512 * h:512 * h + 512]
                                d = pe_group([mm(o, a, hh, st, False), mm(o, a, ll, False, False),
                                              mm(o, b, hh, False, fl)])
                                if fl:
                                    fin.append(d)
                        W.spent[m] = d
                return d

            swiglu_unit(XTh, XTl, [0, 1], rot, (w_in, 0), (w_in, FF), None, blocks, sbuf, gbuf, ffn_gt, flush, ready)
            for t in range(2):
                for h in range(2):
                    b = 4 + 2 * t + h
                    xs = XL[:, t, 512 * h:512 * h + 512]
                    x_ready[t] = bank_free[b] = dve.scalar_tensor_tensor(xs, PS[b][:, :], 0.5, xs, ALU.mult, ALU.add,
                        after=[fin[2 * t + h]])
            xt_free[0] = fin[-1]

        OFF = {"rq": 0, "rk": 512, "rv": 1024, "rg": 1536, "fq": 2048, "fk": 2560, "fv": 3072, "ff": 3584,
               "gr": 3592, "gf": 4616}

        def sigmoid_from(psrc, dst, ready, free=None):
            a = act.activation(dst, psrc, ACT.Exp, scale=-1.0, after=[ready, free])
            b = dve.tensor_scalar(dst, dst, 1.0, None, ALU.add, after=[a])
            return dve.reciprocal(dst, dst, after=[b]), a

        def attend(units, rot, pbuf, ptbuf, fill):
            n = len(units)
            st = [None] * n
            later = {}
            for i in range(n + 5):
                if 0 <= i - 2 < n:
                    u = units[i - 2]
                    k = u["w"] // P
                    wt, pb, _ = st[i - 2]
                    pt = ptbuf[i % len(ptbuf)]
                    st[i - 2][2] = to_T32([pb[:, P * j:P * j + P] for j in range(k)],
                                          pt[:, 0:k * P].rearrange("p (k c) -> p k c", k=k), rot, wt,
                                          buf_free.get(("pt", i % len(ptbuf))), dve if i % 2 else act)
                    buf_free["p", (i - 2) % len(pbuf)] = st[i - 2][2]
                if i < n:
                    u = units[i]
                    w = u["w"]
                    pb = pbuf[i % len(pbuf)]
                    es = []
                    for m, qk in enumerate(u["qk"]):
                        b = rot.take()
                        pe.wait(bank_free[b])
                        s = pe_group(qk(PS[b]), u["ready"])
                        nm = u["nm"][m]
                        x = dve.reduce_max(nm, PS[b][:, 0:w], AX, negate=True, after=[s])
                        if "negsink" in u:
                            x = dve.tensor_tensor(nm, nm, u["negsink"], ALU.min, after=[x])
                        y = bank_free[b] = act.activation(pb[:, 512 * m:512 * m + w], PS[b][:, 0:w], ACT.Exp, bias=nm,
                                                          accum_out=u["ss"][m],
                                                          after=[x, buf_free.get(("p", i % len(pbuf)))])
                        es.append(y)
                    st[i] = [u["weigh"](pb, es) if "weigh" in u else es[-1], pb, None]
                if i < n + 3:
                    next(fill, None)
                if 0 <= i - 3 < n:
                    u = units[i - 3]
                    k = u["w"] // P
                    pt = ptbuf[(i - 1) % len(ptbuf)]
                    if "out_free" in u:
                        pe.wait(u["out_free"]())
                    d = pe_group([mm(u["out"], pt[:, P * j:P * j + P], u["v"][j], j == 0, j == k - 1)
                                  for j in range(k)], st[i - 3][2])
                    buf_free["pt", (i - 1) % len(ptbuf)] = d
                    if "then" in u:
                        later[i + 2] = u["then"](d)
                if later.get(i) is not None:
                    later[i]()

        def split_heads(t, n):
            return t.rearrange("p (h d) -> p h d", h=n)

        def mixer(l, gain, sections):
            w = ("w_in", l)
            rot = Banks([0, 1, 2, 3])
            ready = norm_T(gain, rot)
            stage = [HB[0:4, t, 0:512] for t in range(2)]
            fill = ada(sections, [4, 5], stage, h_free)
            SC0[0] = 0
            qT, kT, v, rg, fqT, fkT, fv = (sc(1024) for _ in range(7))
            tok = [sc(512) for _ in range(2)]
            tA, tB = sc(512), sc(512)
            pbuf = [sc(512) for _ in range(3)]
            ptbuf = [sc(256) for _ in range(2)]
            lfB = sc(2048).rearrange("p (t h c) -> p t h c", t=2, h=8)
            lf = sc(64)
            v3 = lambda a, t: a[:, 512 * t:512 * t + 512]
            tok_free = [None, None]
            fin = {}
            for name, dst in (("rq", qT), ("rk", kT)):
                bb = [rot.take(), rot.take()]
                r = proj(w, OFF[name], 512, XTh, XTl, [0, 1], bb, ready)
                for t in range(2):
                    cos = C["cos1"][:, 64 * t:64 * t + 64]
                    sin = C["sin1"][:, 64 * t:64 * t + 64]
                    src = PS[bb[t]][:, :].rearrange("p (h a d) -> p h a d", h=4, a=2)
                    a4 = tA.rearrange("p (h a d) -> p h a d", h=4, a=2)
                    b4 = tB.rearrange("p (h a d) -> p h a d", h=4, a=2)
                    o4 = tok[t].rearrange("p (h a d) -> p h a d", h=4, a=2)
                    fr = buf_free.get("rope")
                    x1 = dve.tensor_tensor(a4, src, cos.unsqueeze(1).unsqueeze(1).to_broadcast([P, 4, 2, 64]),
                        ALU.mult, after=[r[t], fr])
                    x2 = dve.tensor_tensor(b4[:, :, 0, :], src[:, :, 1, :], sin.unsqueeze(1).to_broadcast([P, 4, 64]),
                        ALU.mult, after=[fr])
                    x3 = dve.tensor_tensor(b4[:, :, 1, :], src[:, :, 0, :], sin.unsqueeze(1).to_broadcast([P, 4, 64]),
                        ALU.mult)
                    bank_free[bb[t]] = x3
                    pool.tensor_tensor(o4[:, :, 0, :], a4[:, :, 0, :], b4[:, :, 0, :], ALU.subtract,
                        after=[x3, tok_free[t]])
                    y = pool.tensor_tensor(o4[:, :, 1, :], a4[:, :, 1, :], b4[:, :, 1, :], ALU.add)
                    buf_free["rope"] = y
                    fin[name, t] = to_T32([tok[t][:, P * h:P * h + P] for h in range(4)],
                                          dst.rearrange("p (h c) -> p h c", h=4)[:, :, t * P:t * P + P], rot, y,
                                          eng=act)
                    tok_free[t] = fin[name, t]
            for name, dst in (("rv", v), ("fv", fv)):
                bb = [rot.take(), rot.take()]
                r = proj(w, OFF[name], 512, XTh, XTl, [0, 1], bb)
                for t in range(2):
                    fin[name, t] = bank_free[bb[t]] = act.activation(v3(dst, t), PS[bb[t]][:, :], ACT.Copy,
                        after=[r[t]])
            bb = [rot.take(), rot.take()]
            r = proj(w, OFF["rg"], 512, XTh, XTl, [0, 1], bb)
            for t in range(2):
                s, _ = sigmoid_from(PS[bb[t]][:, :], v3(rg, t), r[t])
                fin["rg", t] = bank_free[bb[t]] = dve.tensor_tensor(v3(rg, t), v3(rg, t), PS[bb[t]][:, :], ALU.mult,
                    after=[s])
            for name, dst, sca in (("fq", fqT, 0.125), ("fk", fkT, 1.0)):
                bb = [rot.take(), rot.take()]
                r = proj(w, OFF[name], 512, XTh, XTl, [0, 1], bb)
                for t in range(2):
                    y = bank_free[bb[t]] = act.activation(tok[t], PS[bb[t]][:, :], ACT.Copy, scale=sca,
                        after=[r[t], tok_free[t]])
                    fin[name, t] = to_T32([tok[t][:, P * h:P * h + P] for h in range(4)],
                                          dst.rearrange("p (h c) -> p h c", h=4)[:, :, t * P:t * P + P], rot, y,
                                          eng=act)
                    tok_free[t] = fin[name, t]
            bb = [rot.take(), rot.take()]
            r = proj(w, OFF["ff"], 8, XTh, XTl, [0, 1], bb)
            for t in range(2):
                z, e1, e2 = lf[:, 24 * t:24 * t + 8], lf[:, 24 * t + 8:24 * t + 16], lf[:, 24 * t + 16:24 * t + 24]
                x = bank_free[bb[t]] = dve.tensor_tensor(z, PS[bb[t]][:, 0:8], bfor[l], ALU.add, after=[r[t]])
                x1 = dve.tensor_scalar(e1, z, -1.0, None, ALU.mult, after=[x])
                x1 = dve.tensor_tensor(e1, e1, z, ALU.min, after=[x1])
                x2 = act.activation(e1, e1, ACT.Exp, after=[x1])
                x2 = dve.tensor_scalar(e1, e1, 1.0, None, ALU.add, after=[x2])
                x2 = act.activation(e2, e1, ACT.Ln, after=[x2])
                x3 = dve.tensor_scalar(z, z, 0.0, None, ALU.min, after=[x1])
                x3 = dve.tensor_tensor(z, z, e2, ALU.subtract, after=[x3, x2])
                fin["lf", t] = dve.tensor_copy(lfB[:, t, :, :], z.unsqueeze(2).to_broadcast([P, 8, P]), after=[x3])
            prev = None
            rr = [fin["rq", 0], fin["rq", 1], fin["rk", 0], fin["rk", 1], fin["rv", 0], fin["rv", 1]]
            rdone = []
            for h in range(5):
                if h < 4:
                    b = rot.take()
                    q, k = qT[:, 256 * h:256 * h + 256], kT[:, 256 * h:256 * h + 256]
                    s = pe_group([mm(PS[b][:, 0:256], k[:, 0:P], q, True, True),
                                  mm(PS[b][:, 256:384], k[:, P:256], q[:, P:256], True, True)], rr, bank_free[b])
                    pb = pbuf[h % 3]
                    x = dve.tensor_tensor(pb[:, 0:256], PS[b][:, 0:256],
                        dec[:, h, :, :].rearrange("p b c -> p (b c)"), ALU.mult,
                        after=[s, buf_free.get(("p", h % 3))])
                    x = bank_free[b] = dve.tensor_tensor(pb[:, 256:384], PS[b][:, 256:384], dec[:, h, 0, :], ALU.mult,
                        after=[s])
                if prev is not None:
                    ph, ppb, px = prev
                    vv = [v3(v, t)[:, P * ph:P * ph + P] for t in range(2)]
                    if ph == 0:
                        pe.wait(bank_free[6], bank_free[7])
                    d = pe_group([mm(PS[6][:, P * ph:P * ph + P], ppb[:, 0:P], vv[0], True, True),
                                  mm(PS[7][:, P * ph:P * ph + P], ppb[:, P:256], vv[0], True, False),
                                  mm(PS[7][:, P * ph:P * ph + P], ppb[:, 256:384], vv[1], False, True)], px)
                    buf_free[("p", ph % 3)] = d
                prev = (h, pb, x) if h < 4 else None
                next(fill, None)
            RTh, RTl = (FR[:, 4096 + 1024 * i:5120 + 1024 * i].rearrange("p (k t) -> p k t", k=4) for i in range(2))
            FTh, FTl = (FR[:, 6144 + 1024 * i:7168 + 1024 * i].rearrange("p (k t) -> p k t", k=4) for i in range(2))
            rT = []
            for t in range(2):
                ra, rb = tA, tB
                ss = stat[:, 16 + 4 * t:20 + 4 * t]
                y = bank_free[6 + t] = act.activation(tok[t], PS[6 + t][:, :], ACT.Copy, after=[d, tok_free[t]])
                y1 = dve.tensor_tensor(tA, tok[t], tok[t], ALU.mult, after=[y, buf_free.get("rope")])
                y2 = dve.reduce_sum(ss, split_heads(tA, 4), AX, after=[y1])
                y3 = rstd_of(ss, 4, EPS, 1.0 / 128, y2)
                y4 = dve.tensor_tensor(split_heads(tok[t], 4), split_heads(tok[t], 4),
                    ss.unsqueeze(2).to_broadcast([P, 4, P]), ALU.mult, after=[y3])
                y5 = pool.tensor_tensor(v3(rg, t), v3(rg, t), rnorm[l], ALU.mult, after=[fin["rg", t]])
                y6 = dve.tensor_tensor(tok[t], tok[t], v3(rg, t), ALU.mult, after=[y4, y5])
                rT.append(to_T(tok[t], 4, RTh[:, :, t * P:t * P + P], RTl[:, :, t * P:t * P + P], rot, y6, xt_free[0]))
                tok_free[t] = rT[-1]
            units, fT = [], [None, None]
            fr = [fin[n, t] for n in ("fq", "fk", "fv", "lf") for t in range(2)]
            nms, sums = stat[:, 64:80], stat[:, 80:96]

            def fox_out(d, t):
                r = sums[:, 8 * t:8 * t + 8]
                y = dve.reciprocal(r, r, after=[d])
                y = bank_free[6 + t] = dve.tensor_tensor(split_heads(tok[t], 8), split_heads(PS[6 + t][:, :], 8),
                    r.unsqueeze(2).to_broadcast([P, 8, 64]), ALU.mult, after=[y, tok_free[t]])

                def turn():
                    fT[t] = tok_free[t] = to_T(tok[t], 4, FTh[:, :, t * P:t * P + P], FTl[:, :, t * P:t * P + P], rot,
                                               y, xt_free[0])
                return turn

            for t in range(2):
                for h in range(8):
                    o = 64 * (h % 2)
                    q = fqT[o:o + 64, 256 * (h // 2):256 * (h // 2) + 256]
                    k = fkT[o:o + 64, 256 * (h // 2):256 * (h // 2) + 256]

                    def qk(B, h=h, t=t, q=q, k=k):
                        if t == 0:
                            return [mm(B[:, 0:P], q[:, 0:P], k[:, 0:P], True, False),
                                    mm(B[:, 0:P], lfB[:, 0, h, :], C["negtri"], False, False),
                                    mm(B[:, 0:P], ident, C["cmask"], False, True)]
                        return [mm(B[:, 0:256], q[:, P:256], k, True, False),
                                mm(B[:, 0:P], lfB[:, 0, h, :], C["negtri"], False, False),
                                mm(B[:, P:256], lfB[:, 0, h, :], C["negones"], False, False),
                                mm(B[:, P:256], lfB[:, 1, h, :], C["negtri"], False, False),
                                mm(B[:, P:256], ident, C["cmask"], False, True)]
                    i = 8 * t + h
                    u = {"w": 128 * (t + 1), "qk": [qk], "ready": fr, "nm": [nms[:, i:i + 1]], "ss": [sums[:, i:i + 1]],
                         "out": PS[6 + t][:, 64 * h:64 * h + 64],
                         "v": [v3(fv, s)[:, 64 * h:64 * h + 64] for s in range(2)]}
                    if h == 0:
                        u["out_free"] = lambda t=t: bank_free[6 + t]
                    if h == 7:
                        u["then"] = lambda d, t=t: fox_out(d, t)
                    units.append(u)
            attend(units, rot, pbuf, ptbuf, fill)
            for _ in fill:
                pass
            mg_ready = {}
            for h in range(2):
                for wo, go, xh, xl_, rd in ((("w_o_ret", l), "gr", RTh, RTl, rT), (("w_o_fox", l), "gf", FTh, FTl, fT)):
                    bb = [rot.take(), rot.take()]
                    r = proj(w, OFF[go] + 512 * h, 512, XTh, XTl, [0, 1], bb)
                    sg = []
                    for t in range(2):
                        dst = (tA, tB)[t]
                        s, a = sigmoid_from(PS[bb[t]][:, :], dst, r[t], buf_free.get(("sg", t)))
                        bank_free[bb[t]] = a
                        sg.append(s)
                    yb = [rot.take(), rot.take()]
                    r = gemm(wo, 0, 4, 512 * h, 512, xh, xl_, [0, 1], yb, True, True, rd)
                    for t in range(2):
                        dst = (tA, tB)[t]
                        m = HB[:, t, 512 * h:512 * h + 512]
                        if go == "gr":
                            y = dve.tensor_tensor(m, dst, PS[yb[t]][:, :], ALU.mult, after=[r[t], sg[t], h_free[t]])
                            bank_free[yb[t]] = y
                            buf_free["sg", t] = y
                        else:
                            y = dve.tensor_tensor(dst, dst, PS[yb[t]][:, :], ALU.mult, after=[r[t], sg[t]])
                            bank_free[yb[t]] = y
                            y = dve.tensor_tensor(m, m, dst, ALU.add, after=[y, mg_ready[t, h]])
                            buf_free["sg", t] = y
                        mg_ready[t, h] = y
            xt_done = r[-1]
            mT = []
            for t in range(2):
                mT.append(to_T(HB[:, t, :], 8, XTh[:, :, t * P:t * P + P], XTl[:, :, t * P:t * P + P], rot,
                               [mg_ready[t, 0], mg_ready[t, 1]], xt_done))
                h_free[t] = mT[-1]
            for h in range(2):
                bb = [rot.take(), rot.take()]
                r = proj(("w_out", l), 512 * h, 512, XTh, XTl, [0, 1], bb, mT)
                for t in range(2):
                    xs = XL[:, t, 512 * h:512 * h + 512]
                    x_ready[t] = bank_free[bb[t]] = dve.tensor_tensor(xs, PS[bb[t]][:, :], xs, ALU.add, after=[r[t]])
            xt_free[0] = r[-1]
            buf_free["rope"] = None

        def conditioning():
            cs_z = dve.memset(CS[:, :, :].bitcast(F32), 0.0)
            ccol, csig = small(16), small(16)
            x = pe_group([mm(PS[0][:, 0:16], crow[0:16, :], ident[0:16, 0:16], True, True, tr=True)], bank_free[0])
            y = act.activation(ccol, PS[0][:, 0:16], ACT.Copy, after=[x])
            s, a = sigmoid_from(PS[0][:, 0:16], csig, x)
            bank_free[0] = [y, a]
            y = dve.tensor_tensor(ccol, ccol, csig, ALU.mult, after=[y, s])
            cv = ccol.rearrange("p (v k) -> p k v", v=2)
            cs4 = CS[:, :, 0:4].rearrange("p k (v a) -> p k v a", a=2)
            y = act.activation(cs4[:, :, :, 0], cv, ACT.Copy, after=[y, cs_z])
            cs_ready = dve.tensor_tensor(cs4[:, :, :, 1], cv, cs4[:, :, :, 0].bitcast(F32), ALU.subtract, after=[y])
            return cs_ready

        n_mod = [0, 0]
        mod_ready = {}

        def ada(sections, banks, stage, free):
            turn = 0
            for l, sec in sections:
                for c in range(6):
                    b = banks[c % 2]
                    for hk in range(2):
                        for k, kk, hi, lo, rdy, m in W.chunk(rows(("w_ada_2", l), 4 * hk, 4, 3072 * sec + 512 * c, 512),
                                                             4, 512):
                            pe.wait(rdy, cs_ready)
                            if hk == 0 and k == 0:
                                pe.wait(bank_free[b])
                            items = []
                            for q in range(kk):
                                cs = CS[:, 4 * hk + k + q, :]
                                items += [mm(PS[b][:, :], cs, hi[:, q, :], hk == 0 and k + q == 0, False),
                                          mm(PS[b][:, :], cs, lo[:, q, :], False, hk == 1 and k + q == 3)]
                            d = W.spent[m] = pe_group(items)
                            if hk == 1 and k + kk == 4:
                                i = turn % 2
                                turn += 1
                                y = bank_free[b] = act.activation(stage[i], PS[b][0:4, :], ACT.Copy, after=[d, free[i]])
                                n_mod[i] += 1
                                free[i] = act.dma(MOD[l, sec, :, 512 * c:512 * c + 512], stage[i], s_mod[i], n_mod[i], y)
                                mod_ready[l, sec] = both(s_mod, n_mod)
                            yield

        def both(sems, counts):
            return [(sems[i], 16 * counts[i]) for i in range(2) if counts[i]]

        g_next = load_gain(A["norm_ffn1"][0:1, :])
        for l in range(2):
            g, g_next = g_next, load_gain(A["norm_mix"][l:l + 1, :])
            ffn(l, ("w_ffn1_in", l), ("w_ffn1_out", l), g)
            if l == 0:
                cs_ready = conditioning()
            g, g_next = g_next, load_gain(A["norm_ffn2"][l:l + 1, :])
            mixer(l, g, [(0, l)])
            g, g_next = g_next, load_gain(A["norm_ffn1"][1:2, :] if l == 0 else
                                          A["norm_final"].rearrange("(a n) -> a n", a=1))
            ffn(l, ("w_ffn2_in", l), ("w_ffn2_out", l), g)
        for t in range(2):
            x_ready[t] = rms(XL[:, t, :], HB[:, t, :], g_next, t, x_ready[t], h_free[t])
            gain_use[g_next[2]] = x_ready[t]
            x_ready[t] = act.activation(XL[:, t, :], HB[:, t, :], ACT.Copy, after=[x_ready[t]])
            h_free[t] = x_ready[t]

        lt, l2 = small(128), small(2)
        y = dve.tensor_tensor(lt.rearrange("p (a n) -> p a n", a=2),
            lamb.rearrange("p (a b n) -> p a b n", a=2, b=2)[:, :, 0, :],
            lamb.rearrange("p (a b n) -> p a b n", a=2, b=2)[:, :, 1, :], ALU.mult)
        y = dve.reduce_sum(l2, lt.rearrange("p (a n) -> p a n", a=2), AX, after=[y])
        y = act.activation(l2, l2, ACT.Exp, after=[y])
        neglam = small(1)
        y = dve.tensor_tensor(neglam, l2[:, 1:2], l2[:, 0:1], ALU.subtract, after=[y])
        lam_ready = dve.tensor_scalar(neglam, neglam, -LAM_INIT, None, ALU.add, after=[y])
        negsink = small(16)
        sink_ready = dve.tensor_scalar(negsink, sink, -1.0, None, ALU.mult)
        subs_ready = dve.tensor_scalar(subln, subln, 1.0 - LAM_INIT, None, ALU.mult)

        n_r = [0]
        r_free = [None]
        RR = SC[0:5, 10628:13700]
        r_ready = [None]

        def load_mod(l, sec):
            n_r[0] += 2
            sp.dma(RR[4:5, :], A["b_ada_2"][l:l + 1, 3072 * sec:3072 * sec + 3072], s_r, n_r[0] - 1, r_free[0])
            r_ready[0] = sp.dma(RR[0:4, :], MOD[l, sec], s_r, n_r[0], mod_ready[l, sec])

        def spread(which, col, rot):
            b = rot.take()
            m = C["bl" if which == 0 else "bc"][0:5, :]
            t = pe_group([mm(PS[b][:, :], m, RR[:, col:col + 512], True, True)], r_ready[0], bank_free[b])
            r_free[0] = t
            return b, t

        def modulate(x, which, tiles, dsts, rot, ready, free):
            done = [None] * len(tiles)
            for h in range(2):
                bs, ts = spread(which, 1024 + 512 * h, rot)
                bh, th = spread(which, 512 * h, rot)
                for i, t in enumerate(tiles):
                    o = dsts[i][:, 512 * h:512 * h + 512]
                    xs = x[:, t, 512 * h:512 * h + 512]
                    y = dve.scalar_tensor_tensor(o, PS[bs][:, :], 1.0, xs, ALU.add, ALU.mult,
                        after=[ts, ready[i], free[i]])
                    bank_free[bs] = y
                    y = bank_free[bh] = dve.tensor_tensor(o, o, PS[bh][:, :], ALU.add, after=[y, th])
                    done[i] = y
            return done

        r_free[0] = x_ready
        ctx_in = sp.dma(XC[:, :, :], A["ctx_2"][0].rearrange("(t p) d -> p t d", p=P), s_ctx, 1, x_ready)
        c_ready = [ctx_in, ctx_in]

        def add_half(x, h, u, src, gate, col, ready, free=None):
            c = slice(512 * h, 512 * h + 512)
            y = dve.tensor_tensor(u, src, gate[:, c], ALU.mult, after=[ready, free])
            f = dve.scalar_tensor_tensor(x[:, c], x[:, c], ALPHA, u, ALU.mult, ALU.add, after=[y])
            return y, f, dve.bn_stats(stat[:, col + 6 * h:col + 6 * h + 6], x[:, c], after=[f])

        def layer_norm(x, gt, bt, col, ready):
            mv = stat[:, col + 12:col + 14]
            y = dve.bn_aggr(mv, stat[:, col:col + 12], after=[ready])
            y = rstd_of(mv[:, 1:2], 1, EPS, 1.0, y)
            y = dve.scalar_tensor_tensor(x, x, mv[:, 0:1], gt[0], ALU.subtract, ALU.mult, after=[y, gt[1]])
            y = dve.scalar_tensor_tensor(x, x, mv[:, 1:2], bt[0], ALU.mult, ALU.add, after=[y, bt[1]])
            gain_use[gt[2]] = gain_use[bt[2]] = y
            return y

        def gate_tile(which, dst, rot, free=None):
            y = None
            for h in range(2):
                b, t = spread(which, 2048 + 512 * h, rot)
                y = bank_free[b] = act.activation(dst[:, 512 * h:512 * h + 512], PS[b][:, :], ACT.Copy,
                    after=[t, free])
            return y

        X4h = FR[:, 0:4096].rearrange("p (k t) -> p k t", k=8)
        X4l = FR[:, 4096:8192].rearrange("p (k t) -> p k t", k=8)

        def hidden_T(nctx, rot, to_dram=None):
            done = []
            for which in range(2 if nctx else 1):
                x = XC if which else XL
                rd = c_ready if which else x_ready
                hs = modulate(x, which, [0, 1], [HB[:, 0, :], HB[:, 1, :]], rot, rd, h_free)
                for t in range(2):
                    g = 2 * which + t
                    fr = []
                    if to_dram is not None:
                        fr = [to_dram(g, HB[:, t, :], hs[t])]
                    d = to_T(HB[:, t, :], 8, X4h[:, :, g * P:g * P + P], X4l[:, :, g * P:g * P + P], rot, hs[t],
                             xt_free[0])
                    done.append(d)
                    h_free[t] = [d] + fr
            return done

        def rope2(src, dst, t, nh, ready, tmp, free, pairs=False):
            cos, sin = C["cos2"][:, 64 * t:64 * t + 64], C["sin2"][:, 64 * t:64 * t + 64]
            a, bq = tmp[0][:, 0:64 * nh], tmp[1][:, 0:64 * nh]
            v5 = lambda z: z.rearrange("p (h b a d) -> p h b a d", h=nh, b=2, a=2)
            s4 = sin.rearrange("p (b a d) -> p b a d", b=2, a=2)
            fr = buf_free.get("rope")
            x = dve.tensor_tensor(split_heads(a, nh), split_heads(src, nh),
                cos.unsqueeze(1).to_broadcast([P, nh, 64]), ALU.mult, after=[ready, fr])
            for half in range(2):
                x = dve.tensor_tensor(v5(bq)[:, :, :, half, :], v5(src)[:, :, :, 1 - half, :],
                    s4[:, :, half, :].unsqueeze(1).to_broadcast([P, nh, 2, 16]), ALU.mult, after=[fr])
            if pairs:
                dst, a, bq = paired(dst), a.rearrange("p (v g d) -> p v g d", v=2, g=4), \
                    bq.rearrange("p (v g d) -> p v g d", v=2, g=4)
            y = pool.tensor_tensor(dst, a, bq, ALU.add, after=[x, free])
            buf_free["rope"] = y
            return y, x

        def paired(dst):
            return dst.rearrange("p (g v d) -> p v g d", g=4, v=2)

        def attn_a(rot):
            SC0[0] = 0
            qT, kT, v = sc(4096), sc(1024), sc(1024)
            tok = [sc(512) for _ in range(2)]
            pbuf = [sc(512) for _ in range(3)]
            ptbuf = [sc(512) for _ in range(2)]
            st_ = sc(900)
            stage = [st_[0:4, 0:512], tok[0][0:4, :]]
            tmp = pbuf[0:2]
            assert SC0[0] <= 10628
            w = ("wqkv_a_2", 0)
            ready = hidden_T(True, rot)
            q4 = qT.rearrange("p (n t) -> p n t", n=8)
            k4 = kT.rearrange("p (n t) -> p n t", n=2)
            fin = []
            tf = [None, None]
            ti = 0
            for blk in (2, 0, 1):
                bb = [rot.take() for _ in range(4)]
                r = proj(w, 512 * blk, 512, X4h, X4l, [0, 1, 2, 3], bb, ready)
                for t in range(4):
                    src = PS[bb[t]][:, :]
                    dst = tok[ti % 2]
                    if blk == 2:
                        if t < 2:
                            y, x = rope2(src[:, 0:256], dst[:, 0:256], t, 4, r[t], tmp, tf[ti % 2])
                        else:
                            y = x = act.activation(dst[:, 0:256], src[:, 0:256], ACT.Copy, after=[r[t], tf[ti % 2]])
                        z = act.activation(v[:, 256 * t:256 * t + 256], src[:, 256:512], ACT.Copy, after=[r[t], x])
                        bank_free[bb[t]] = [x, z]
                        fin.append(z)
                        tf[ti % 2] = to_T32([dst[:, P * n:P * n + P] for n in range(2)],
                                            k4[:, :, t * P:t * P + P], rot2, y, eng=act)
                    else:
                        if t < 2:
                            y, x = rope2(src, dst, t, 8, r[t], tmp, tf[ti % 2], pairs=True)
                        else:
                            y = x = act.activation(paired(dst), src.rearrange("p (v g d) -> p v g d", v=2, g=4),
                                ACT.Copy, after=[r[t], tf[ti % 2]])
                        bank_free[bb[t]] = x
                        tf[ti % 2] = to_T32([dst[:, P * g:P * g + P] for g in range(4)],
                                            q4[:, 4 * blk:4 * blk + 4, t * P:t * P + P], rot2, y, eng=act)
                    fin.append(tf[ti % 2])
                    ti += 1
            xt_free[0] = r[-1]
            oT = [None] * 4
            buf_free["p", 0] = buf_free["p", 1] = buf_free["rope"]
            rot3 = Banks([0, 1, 2, 3])
            qs = dve.tensor_scalar(qT, qT, 0.125, None, ALU.mult, after=[fin])
            nms, sums, snk = stat[:, 64:128], stat[:, 128:192], stat[:, 192:256]
            stage_free = [fin, fin]
            fill = ada([(1, 0), (1, 1)], [4, 5], stage, stage_free)
            units = []
            act.wait(sink_ready)

            def half(d, t, hh):
                cols = slice(16 * t + 8 * hh, 16 * t + 8 * hh + 8)
                hb = HB[:, t % 2, 512 * hh:512 * hh + 512]
                y = dve.tensor_tensor(snk[:, cols], nms[:, cols], sink[:, 8 * hh:8 * hh + 8], ALU.add, after=[d])
                y = act.activation(snk[:, cols], snk[:, cols], ACT.Exp, after=[y])
                y = dve.tensor_tensor(sums[:, cols], sums[:, cols], snk[:, cols], ALU.add, after=[y])
                y = dve.reciprocal(sums[:, cols], sums[:, cols], after=[y])
                y = bank_free[6 + hh] = dve.tensor_tensor(split_heads(hb, 8), split_heads(PS[6 + hh][:, :], 8),
                    sums[:, cols].unsqueeze(2).to_broadcast([P, 8, 64]), ALU.mult, after=[y, h_free[t % 2]])
                if hh == 0:
                    return None

                def turn():
                    h_free[t % 2] = oT[t] = to_T(HB[:, t % 2, :], 8, X4h[:, :, t * P:t * P + P],
                                                 X4l[:, :, t * P:t * P + P], rot3, y, xt_free[0])
                return turn

            for t in range(4):
                for h in range(16):
                    kv, g = h // 4, h % 4
                    o = 64 * (kv % 2)
                    q = q4[o:o + 64, 4 * (kv // 2) + g, t * P:t * P + P]
                    k = k4[o:o + 64, kv // 2, :]
                    if t < 2:
                        def qk(B, q=q, k=k, t=t):
                            m = (B[:, P:256], C["cmask"]) if t == 0 else (B[:, 0:P], C["wmask"])
                            return [mm(B[:, 0:512], q, k, True, False), mm(m[0], ident, m[1], False, True)]
                        vt = [0, 1, 2, 3]
                    else:
                        def qk(B, q=q, k=k):
                            return [mm(B[:, 0:256], q, k[:, 256:512], True, True)]
                        vt = [2, 3]
                    i = 16 * t + h
                    u = {"w": P * len(vt), "qk": [qk], "ready": [qs] + fin, "nm": [nms[:, i:i + 1]],
                         "ss": [sums[:, i:i + 1]], "negsink": negsink[:, h:h + 1],
                         "out": PS[6 + h // 8][:, 64 * (h % 8):64 * (h % 8) + 64],
                         "v": [v[:, 256 * s + 64 * kv:256 * s + 64 * kv + 64] for s in vt]}
                    if h % 8 == 0:
                        u["out_free"] = lambda h=h: bank_free[6 + h // 8]
                    if h % 8 == 7:
                        u["then"] = lambda d, t=t, h=h: half(d, t, h // 8)
                    units.append(u)
            attend(units, rot3, pbuf, ptbuf, fill)
            for _ in fill:
                pass
            return oT + stage_free

        def attn_b(rot):
            SC0[0] = 0
            qT, kT, v = sc(2048), sc(4096), None
            tok2 = sc(1024)
            tok = [tok2[:, 0:512], tok2[:, 512:1024]]
            pbuf = [sc(1024) for _ in range(2)] + [tok2]
            ptbuf = [sc(512) for _ in range(2)]
            tmp = [pbuf[0][:, 0:512], pbuf[1][:, 0:512]]
            assert SC0[0] <= 10628
            w = ("wqkv_b_2", 0)
            ready = hidden_T(True, rot)
            q4 = qT.rearrange("p (n t) -> p n t", n=8)
            k4 = kT.rearrange("p (n t) -> p n t", n=8)
            vt = [XC[:, 0, :], XC[:, 1, :], VX[:, 0:1024], VX[:, 1024:2048]]
            fin, tf, ti = [], [None, None], 0
            ctx_dead = ready
            for blk in range(6):
                tiles = [0, 1] if blk < 2 else [0, 1, 2, 3]
                bb = [rot.take() for _ in tiles]
                r = proj(w, 512 * blk, 512, X4h, X4l, tiles, bb, ready)
                for t in tiles:
                    src, dst = PS[bb[t]][:, :], tok[ti % 2]
                    if blk >= 4:
                        z = bank_free[bb[t]] = act.activation(vt[t][:, 512 * (blk - 4):512 * (blk - 4) + 512], src,
                            ACT.Copy, after=[r[t], ctx_dead])
                        fin.append(z)
                        continue
                    if t < 2:
                        y, x = rope2(src, dst, t, 8, r[t], tmp, tf[ti % 2])
                    else:
                        y = x = act.activation(dst, src, ACT.Copy, after=[r[t], tf[ti % 2]])
                    bank_free[bb[t]] = x
                    dd = (q4 if blk < 2 else k4)[:, 4 * (blk % 2):4 * (blk % 2) + 4, t * P:t * P + P]
                    tf[ti % 2] = to_T32([dst[:, P * n:P * n + P] for n in range(4)], dd, rot2, y, eng=act)
                    fin.append(tf[ti % 2])
                    ti += 1
            xt_free[0] = r[-1]
            buf_free["p", 0] = buf_free["p", 1] = buf_free["rope"]
            rot3 = Banks([0, 1, 2, 3, 4, 5])
            qs = dve.tensor_scalar(qT, qT, 0.125, None, ALU.mult, after=[fin])
            nms, sums, ratio = stat[:, 64:96], stat[:, 96:128], stat[:, 128:144]
            units, oT = [], [None, None]
            out_y = {}

            def half(d, t, hh):
                hb = HB[:, t, 512 * hh:512 * hh + 512]
                r = sums[:, 16 * t + 8 * hh:16 * t + 8 * hh + 8].rearrange("p (h m) -> p h m", m=2)[:, :, 0]
                y = dve.reciprocal(r, r, after=[d])
                y = bank_free[6 + hh] = dve.tensor_tensor(split_heads(hb, 4), split_heads(PS[6 + hh][:, :], 4),
                    r.unsqueeze(2).to_broadcast([P, 4, P]), ALU.mult, after=[y, h_free[t]])
                sq = GB[:, t, 512 * hh:512 * hh + 512]
                ss = stat[:, 480 + 8 * t + 4 * hh:484 + 8 * t + 4 * hh]
                x = dve.tensor_tensor(sq, hb, hb, ALU.mult, after=[y, gain_use[t]])
                x = dve.reduce_sum(ss, split_heads(sq, 4), AX, after=[x])
                x = rstd_of(ss, 4, 1e-5, 1.0 / 128, x)
                out_y[hh] = x
                if hh == 0:
                    return None
                ss, hb = stat[:, 480 + 8 * t:488 + 8 * t], HB[:, t, :]
                y = dve.tensor_tensor(split_heads(hb, 8), split_heads(hb, 8), ss.unsqueeze(2).to_broadcast([P, 8, P]),
                    ALU.mult, after=[y, out_y[0], x])
                gain_use[t] = y
                y = dve.tensor_tensor(split_heads(hb, 8), split_heads(hb, 8),
                    subln.unsqueeze(1).to_broadcast([P, 8, P]), ALU.mult, after=[y, subs_ready])

                def turn():
                    h_free[t] = oT[t] = to_T(HB[:, t, :], 8, X4h[:, :, t * P:t * P + P], X4l[:, :, t * P:t * P + P],
                                             rot3, y, xt_free[0])
                return turn

            for t in range(2):
                for h in range(8):
                    qks = []
                    for m in range(2):
                        qks.append(lambda B, h=h, m=m, t=t: [mm(
                            B[:, 0:512], q4[64 * m:64 * m + 64, h, t * P:t * P + P], k4[64 * m:64 * m + 64, h, :],
                            True, True)])
                    i = 8 * t + h
                    s0, s1, ra = sums[:, 2 * i:2 * i + 1], sums[:, 2 * i + 1:2 * i + 2], ratio[:, i:i + 1]

                    def weigh(pb, es, s0=s0, s1=s1, ra=ra):
                        y = dve.reciprocal(s1, s1, after=[es[1]])
                        y = dve.scalar_tensor_tensor(ra, s0, neglam, s1, ALU.mult, ALU.mult, after=[y, es, lam_ready])
                        return dve.scalar_tensor_tensor(pb[:, 0:512], pb[:, 512:1024], ra, pb[:, 0:512], ALU.mult,
                            ALU.add, after=[y])
                    u = {"w": 512, "qk": qks, "ready": [qs] + fin, "nm": [nms[:, 2 * i + m:2 * i + m + 1] for m in range(2)],
                         "ss": [s0, s1], "weigh": weigh, "out": PS[6 + h // 4][:, P * (h % 4):P * (h % 4) + P],
                         "v": [vt[s][:, P * h:P * h + P] for s in range(4)]}
                    if h % 4 == 0:
                        u["out_free"] = lambda h=h: bank_free[6 + h // 4]
                    if h % 4 == 3:
                        u["then"] = lambda d, t=t, h=h: half(d, t, h // 4)
                    units.append(u)
            attend(units, rot3, pbuf, ptbuf, iter(()))
            return oT

        VX = SC[:, 10240:12288]

        def attn_out(l, wo, tiles, oT, rot):
            gl = load_gain(A["ln_attn_g_2"][l:l + 1, :])
            bl = load_gain(A["ln_attn_b_2"][l:l + 1, :])
            SC0[0] = 0
            gates = [sc(1024), sc(1024)]
            u = [sc(1024) for _ in range(4)]
            gr = [gate_tile(w, gates[w], rot, oT) for w in range(2 if len(tiles) > 2 else 1)]
            ur = {}
            for h in range(2):
                bb = [rot.take() for _ in tiles]
                r = proj(wo, 512 * h, 512, X4h, X4l, tiles, bb, oT)
                for i, t in enumerate(tiles):
                    x, rd = (XL, x_ready) if t < 2 else (XC, c_ready)
                    bank_free[bb[i]], f, ur[t] = add_half(x[:, t % 2, :], h, u[t][:, 512 * h:512 * h + 512],
                                                          PS[bb[i]][:, :], gates[t // 2], 16 * t,
                                                          [r[i], oT, gr[t // 2], rd[t % 2]])
            xt_free[0] = r[-1]
            for t in tiles:
                x, rd = (XL, x_ready) if t < 2 else (XC, c_ready)
                rd[t % 2] = layer_norm(x[:, t % 2, :], gl, bl, 16 * t, ur[t])

        filled = (s_fill, 16 * n_fill[0])
        n_hd, n_yd, n_xg, n_yg = [0, 0], [0, 0], [0, 0], [0, 0]

        hd_free = [None]
        yd_free = [None]

        def top(b, n, ranks, tmp, lim, ready):
            big = tmp[0].rearrange("p (g i j) -> p g i j", i=4, j=4)[:, 0:n, :, :]
            eq = tmp[1].rearrange("p (g i j) -> p g i j", i=4, j=4)[:, 0:n, :, :]
            bj = b.unsqueeze(2).to_broadcast([P, n, 4, 4])
            bi = b.unsqueeze(3).to_broadcast([P, n, 4, 4])
            lt = C["lt4"].rearrange("p (i j) -> p i j", i=4).unsqueeze(1).to_broadcast([P, n, 4, 4])
            x = dve.tensor_tensor(big, bj, bi, ALU.is_gt, after=[ready])
            y = dve.tensor_tensor(eq, bj, bi, ALU.is_equal, after=[ready])
            y = dve.tensor_tensor(eq, eq, lt, ALU.mult, after=[y])
            y = dve.tensor_tensor(big, big, eq, ALU.add, after=[x, y])
            y = dve.reduce_sum(ranks, big, AX, after=[y])
            return dve.tensor_scalar(ranks, ranks, lim, None, ALU.is_lt, after=[y])

        def moe(l, NT):
            gl = load_gain(A["ln_ffn_g_2"][l:l + 1, :])
            bl = load_gain(A["ln_ffn_b_2"][l:l + 1, :])
            rot = Banks(list(range(8)))
            rows_out = []

            def to_dram(g, h, rd):
                n_hd[g % 2] += 1
                return sp.dma(HD[g * P:g * P + P, :], h, s_hd[g % 2], n_hd[g % 2], rd, hd_free[0])

            ready = hidden_T(NT == 4, rot, to_dram)
            hd_ready = both(s_hd, n_hd)
            SC0[0] = 0
            N16 = NT * 16
            z = [sc(64)[:, 0:N16] for _ in range(10)]
            tmp = [sc(256), sc(256)]
            gs, gsel, s2 = sc(16)[:, 0:NT * 4], sc(16)[:, 0:NT * 4], sc(64)
            xg = [sc(1024) for _ in range(2)]
            ysb = [sc(1024) for _ in range(2)]
            sbuf = [sc(512) for _ in range(2)]
            gbuf = [sc(512) for _ in range(2)]
            pe_b = [sc(128) for _ in range(4)]
            assert SC0[0] <= 10628, SC0[0]
            b = rot.take()
            for _, _, hi, lo, rdy, m in W.chunk(rows(("w_router_2",), 0, 8, 0, 16), 8, 16):
                pe.wait(rdy, ready, bank_free[b])
                o = PS[b][0:16, 0:NT * P]
                it = []
                for k in range(8):
                    h, ll = X4h[:, k, 0:NT * P], X4l[:, k, 0:NT * P]
                    it += [mm(o, hi[:, k, :], h, k == 0, False), mm(o, lo[:, k, :], h, False, False),
                           mm(o, hi[:, k, :], ll, False, k == 7)]
                d = W.spent[m] = pe_group(it)
            lgT = ysb[0][0:16, 0:NT * P]
            y = bank_free[b] = act.activation(lgT, PS[b][0:16, 0:NT * P], ACT.Copy, after=[d])
            b = rot.take()
            d = buf_free["y", 0] = pe_group([mm(PS[b][:, 16 * t:16 * t + 16], lgT[:, t * P:t * P + P], ident[0:16, 0:16],
                                                True, True, tr=True) for t in range(NT)], y, bank_free[b])
            xt_free[0] = d
            s, bb, ing, sel, wgt, posm, slot, t0, t1, t2 = z
            y, a = sigmoid_from(PS[b][:, 0:N16], s, d)
            bank_free[b] = a
            v3 = lambda q: q.rearrange("p (t e) -> p t e", t=NT)
            g4 = lambda q: q.rearrange("p (g j) -> p g j", j=4)
            y = dve.tensor_tensor(v3(bb), v3(s), rbias.unsqueeze(1).to_broadcast([P, NT, 16]), ALU.add, after=[y])
            y = top(g4(bb), NT * 4, g4(ing), tmp, 1.5, y)
            y = dve.tensor_tensor(t0, bb, ing, ALU.mult, after=[y])
            y = dve.reduce_sum(gs, g4(t0), AX, after=[y])
            y = top(g4(gs), NT, g4(gsel), tmp, 0.5, y)
            y = dve.tensor_tensor(g4(sel), g4(ing), gsel.unsqueeze(2).to_broadcast([P, NT * 4, 4]), ALU.mult,
                after=[y])
            sel_r = y
            y = dve.tensor_tensor(t0, s, sel, ALU.mult, after=[y])
            den, sl0, sl1, w0, w1 = (s2[:, 4 * i:4 * i + NT] for i in range(5))
            y = dve.reduce_sum(den, v3(t0), AX, after=[y])
            y = dve.reciprocal(den, den, after=[y])
            wr = dve.tensor_tensor(v3(wgt), v3(t0), den.unsqueeze(2).to_broadcast([P, NT, 16]), ALU.mult, after=[y])
            b = rot.take()
            pe.wait(bank_free[b], sel_r)
            for t in range(NT):
                d = pe_group([mm(PS[b][:, 16 * t:16 * t + 16], C["negtri" if u == t else "negones"],
                                 v3(sel)[:, u, :], u == 0, u == t) for u in range(t + 1)])
            d = pe_group([mm(PS[b][:, 64:80], C["negones"], v3(sel)[:, u, :], u == 0, u == NT - 1) for u in range(NT)])
            cf = s2[:, 32:49]
            y = dve.tensor_scalar(cf[:, 0:16], PS[b][:, 64:80], -1.0, None, ALU.mult, after=[d])
            y = dve.reduce_max(cf[:, 16:17], cf[:, 0:16], AX, after=[y])
            cnt_r = dve.tensor_copy(CNT[:, :], cf, after=[y])
            y = dve.tensor_scalar(posm, sel, -4096.0, 4095.0, ALU.mult, ALU.add, after=[sel_r])
            pos_r = dve.tensor_tensor(posm, posm, PS[b][:, 0:N16], ALU.subtract, after=[y, d])
            y = dve.tensor_tensor(v3(slot), C["eoff"].unsqueeze(1).to_broadcast([P, NT, 16]),
                v3(PS[b][:, 0:N16]), ALU.subtract, after=[d])
            for j in range(1, NT):
                y1 = dve.tensor_scalar(t0, PS[b][:, 0:N16], -(P * j + 1.0), float(NE * P - P), ALU.is_le, ALU.mult,
                                       after=[y, wr])
                y = dve.tensor_tensor(slot, slot, t0, ALU.add, after=[y1])
            bank_free[b] = y
            y1 = dve.tensor_tensor(t1, slot, sel, ALU.mult, after=[y])
            y1 = dve.reduce_max(sl1, v3(t1), AX, after=[y1])
            y2 = dve.tensor_scalar(t2, slot, -1.0, BIG, ALU.mult, ALU.add, after=[y])
            y2 = dve.tensor_tensor(t2, t2, sel, ALU.mult, after=[y2])
            y2 = dve.reduce_max(sl0, v3(t2), AX, after=[y2])
            y2 = dve.tensor_scalar(sl0, sl0, -1.0, BIG, ALU.mult, ALU.add, after=[y2])
            for sl, ww, yy, tt in ((sl0, w0, y2, t1), (sl1, w1, y1, t2)):
                y = dve.tensor_tensor(v3(tt), v3(slot), sl.unsqueeze(2).to_broadcast( [P, NT, 16]), ALU.is_equal,
                    after=[yy, y1, y2])
                y = dve.tensor_tensor(tt, tt, wgt, ALU.mult, after=[y, wr])
                w_r = dve.reduce_sum(ww, v3(tt), AX, after=[y])
            sidx = IDX[:, 64:64 + 2 * NT].rearrange("p (k t) -> p k t", k=2)
            dve.tensor_copy(sidx[:, 0, :], sl0, after=[y2])
            sidx_r = dve.tensor_copy(sidx[:, 1, :], sl1, after=[y1])

            def indices(e_list, j, icol, rdy):
                b = rot.take()
                pe.wait(bank_free[b])
                d = None
                for i, e_ in enumerate(e_list):
                    for t in range(NT):
                        q = (i * NT + t) % 4
                        col = posm[:, 16 * t + e_:16 * t + e_ + 1]
                        y = dve.tensor_scalar(pe_b[q], C["iota"], float(P * j), col, ALU.add, ALU.is_equal,
                            after=[rdy, buf_free.get(("pe", q))])
                        d = buf_free["pe", q] = pe_group([mm(PS[b][:, 2 * i:2 * i + 1], pe_b[q],
                                                             C["tid"][:, t:t + 1], t == 0, t == NT - 1)], y)
                m = len(e_list)
                r = bank_free[b] = dve.tensor_copy(IDX[:, icol:icol + m],
                    PS[b][:, 0:2 * m].rearrange("p (m a) -> p m a", a=2)[:, :, 0],
                    after=[d, buf_free.get(("idx", icol))])
                return r

            xts = [(FR[:, 2048 * i:2048 * i + 1024].rearrange("p (k t) -> p k t", k=8),
                    FR[:, 2048 * i + 1024:2048 * i + 2048].rearrange("p (k t) -> p k t", k=8)) for i in range(2)]
            gts = [(FR[:, 4096 + 1024 * i:4096 + 1024 * i + 512].rearrange("p (k t) -> p k t", k=4),
                    FR[:, 4608 + 1024 * i:4608 + 1024 * i + 512].rearrange("p (k t) -> p k t", k=4)) for i in range(2)]
            buf_free["xt", 0] = buf_free["xt", 1] = buf_free["gt", 0] = buf_free["gt", 1] = d

            def gather(i, icol, rdy):
                n_xg[i % 2] += 1
                return pool.gather_rows(xg[i % 2], HD[:, :], IDX[:, icol:icol + 1], s_xg[i % 2], n_xg[i % 2],
                                        after=[rdy, hd_ready, buf_free.get(("xg", i % 2))])

            xt_r, g_t = {}, {}

            def fetch(i, e_, j, rdy):
                g_t[i] = gather(i, 16 * j + e_, rdy)

            def prep(i):
                xh, xl_ = xts[i % 2]
                xt_r[i] = to_T(xg[i % 2], 8, xh, xl_, rot, g_t[i], buf_free["xt", i % 2])
                buf_free["xg", i % 2] = xt_r[i]

            def up(i, e_):
                xh, xl_ = xts[i % 2]
                ba, bb_ = rot.take(), rot.take()
                ra = proj(("w_gate_2", l, e_), 0, DE, xh, xl_, [0], [ba], xt_r[i])
                sr = bank_free[ba] = act.activation(sbuf[i % 2], PS[ba][:, :], ACT.Silu,
                                                    after=[ra, buf_free.get(("s", i % 2))])
                rb = proj(("w_up_2", l, e_), 0, DE, xh, xl_, [0], [bb_])
                buf_free["xt", i % 2] = rb[0]
                gr = bank_free[bb_] = dve.tensor_tensor(gbuf[i % 2], sbuf[i % 2], PS[bb_][:, :], ALU.mult,
                                                        after=[rb, sr, buf_free.get(("g", i % 2))])
                buf_free["s", i % 2] = gr
                return gr

            def turn(i, gr):
                gh, gw = gts[i % 2]
                buf_free["g", i % 2] = to_T(gbuf[i % 2], 4, gh, gw, rot, gr, buf_free["gt", i % 2])
                return buf_free["g", i % 2]

            def down(i, e_, j, tl):
                gh, gw = gts[i % 2]
                for h in range(2):
                    by = rot.take()
                    r = gemm(("w_down_2", l, e_), 0, 4, 512 * h, 512, gh, gw, [0], [by], True, True, tl)
                    y = bank_free[by] = act.activation(ysb[i % 2][:, 512 * h:512 * h + 512], PS[by][:, :], ACT.Copy,
                                                       after=[r, buf_free.get(("y", i % 2))])
                buf_free["gt", i % 2] = r[0]
                n_yd[i % 2] += 1
                base = (j * NE + e_) * P
                buf_free["y", i % 2] = act.dma(YD[base:base + P, :], ysb[i % 2], s_yd[i % 2], n_yd[i % 2], y, yd_free[0],
                                             filled)

            rdy = {0: indices([0], 0, 0, pos_r), 1: indices([1], 0, 1, pos_r)}
            fetch(0, 0, 0, rdy[0])
            prep(0)
            gr = [None] * NE
            for i in range(NE + 1):
                if i + 1 < NE:
                    fetch(i + 1, i + 1, 0, rdy[i + 1])
                if i:
                    tl = turn(i - 1, gr[i - 1])
                if i < NE:
                    gr[i] = up(i, i)
                    if i + 2 < NE:
                        rdy[i + 2] = indices([i + 2], 0, i + 2, pos_r)
                if i + 1 < NE:
                    prep(i + 1)
                if i:
                    down(i - 1, i - 1, 0, tl)
            for q in engines:
                q.wait(cnt_r)
            i = NE
            for j in range(1, NT):
                begin()
                for e_ in range(NE):
                    begin()
                    fetch(i, e_, j, indices([e_], j, 16 * j + e_, pos_r))
                    prep(i)
                    down(i, e_, j, turn(i, up(i, e_)))
                    end(CNT[0:1, e_:e_ + 1], P * j)
                    i += 1
                end(CNT[0:1, 16:17], P * j)
            r = [(pe.sem, pe.n)]
            xt_free[0] = buf_free["gt", 0] = buf_free["gt", 1] = r[0]
            hd_free[0] = both(s_xg, n_xg)
            yd_all = both(s_yd, n_yd)
            gates = [HB[:, 0, :], HB[:, 1, :]]
            gr = [gate_tile(w, gates[w], rot, h_free[w]) for w in range(2 if NT == 4 else 1)]
            ya = [(xg[0], xg[1]), (ysb[0], ysb[1])]
            yfree = [[buf_free["xg", 0], buf_free["xg", 1]], [yd_all]]
            for t in range(NT):
                pr = ya[t % 2]
                for k in range(2):
                    n_yg[t % 2] += 1
                    got = pool.gather_rows(pr[k], YD[0:NT * NE * P, :], sidx[:, k, t:t + 1], s_yg[t % 2], n_yg[t % 2],
                                           after=[yd_all, filled, sidx_r, yfree[t % 2]])
                y = dve.tensor_scalar(pr[0], pr[0], w0[:, t:t + 1], None, ALU.mult, after=[got, w_r])
                y = dve.scalar_tensor_tensor(pr[0], pr[1], w1[:, t:t + 1], pr[0], ALU.mult, ALU.add, after=[y])
                x, rd = (XL, x_ready) if t < 2 else (XC, c_ready)
                for h in range(2):
                    us = pr[0][:, 512 * h:512 * h + 512]
                    _, f, st_ = add_half(x[:, t % 2, :], h, us, us, gates[t // 2], 16 * t, [y, gr[t // 2], rd[t % 2]])
                rd[t % 2] = layer_norm(x[:, t % 2, :], gl, bl, 16 * t, st_)
                fr = f
                yfree[t % 2] = [fr]
                h_free[t // 2] = [fr]
            yd_free[0] = both(s_yg, n_yg)

        r4 = Banks([0, 1, 2, 3, 4, 5])
        rot2 = Banks([4, 5, 6, 7])
        for l in range(2):
            rotp = Banks([0, 1, 2, 3])
            load_mod(l, 0)
            oT = (attn_a if l == 0 else attn_b)(rotp)
            attn_out(l, ("wo_a_2" if l == 0 else "wo_b_2", 0), [0, 1, 2, 3] if l == 0 else [0, 1], oT,
                     Banks(list(range(8))))
            load_mod(l, 1)
            moe(l, 4 if l == 0 else 2)
        fin = sp.dma(out[0].rearrange("(t p) d -> p t d", p=P), XL[:, :, :], s_out, 1, x_ready[0], x_ready[1])
        sp.wait(fin, both(s_hd, n_hd), both(s_yd, n_yd))

        if plan is None:
            return W.log
        assert len(plan) == len(W.log) and W.split == len(W.parts)
        block = ctx.enter_context(nc.Block())

        @block.sync
        def _(e):
            sp.play(e)

        @block.gpsimd
        def _(e):
            pool.play(e)

        @block.scalar
        def _(e):
            act.play(e)

        @block.vector
        def _(e):
            dve.play(e)

        @block.tensor
        def _(e):
            pe.play(e)


_INS = ["x", "norm_ffn1", "w_ffn1_in", "w_ffn1_out", "norm_mix", "w_in", "b_forget", "ret_norm", "w_o_ret", "w_o_fox",
        "w_out", "norm_ffn2", "w_ffn2_in", "w_ffn2_out", "norm_final", "c_2", "ctx_2", "c_ctx_2", "w_ada_2", "b_ada_2",
        "wqkv_a_2", "wo_a_2", "sink_a_2", "wqkv_b_2", "wo_b_2", "lambda_b_2", "subln_b_2", "ln_attn_g_2",
        "ln_attn_b_2", "ln_ffn_g_2", "ln_ffn_b_2", "w_router_2", "router_bias_2", "w_gate_2", "w_up_2", "w_down_2"]


def kernel(**inputs):
    import concourse.bacc as _bacc
    from concourse.bass_utils import run_bass_kernel_spmd as _run

    arrays = {f"in_{n}": np.ascontiguousarray(inputs[n]) for n in _INS}
    arrays["consts"], arrays["decay"] = constants()

    def program(plan):
        nc = _bacc.Bacc("TRN2", target_bir_lowering=False, num_devices=1)
        ap = {n: nc.dram_tensor(n, a.shape, mybir.dt.from_np(a.dtype), kind="ExternalInput").ap()
              for n, a in arrays.items()}
        out = nc.dram_tensor("out_0", (1, 256, D), F32, kind="ExternalOutput").ap()
        return nc, build(nc, {n: ap[f"in_{n}"] for n in _INS}, out, ap["consts"], ap["decay"], plan)

    _, plan = program(None)
    nc, _ = program(plan)
    r = _run(nc, [arrays], core_ids=[0])
    return r.results[0]["out_0"]
```

```python
from contextlib import ExitStack

import numpy as np

import concourse.bass as bass
from concourse import mybir

P = 128
D = 1024
FF = 2816
NE = 16
DE = 512
ALU = mybir.AluOpType
ACT = mybir.ActivationFunctionType
F32 = mybir.dt.float32
F32R = mybir.dt.float32r
U32 = mybir.dt.uint32
AX = mybir.AxisListType.X
EPS = 1e-6
ALPHA = 4.0 ** 0.25
LAM_INIT = 0.8 - 0.6 * float(np.exp(-0.3))
BIG = 16384.0

CONSTS = [("ident", 128), ("half", 1), ("negtri", 128), ("negones", 128), ("cmask", 128), ("wmask", 128),
          ("cos1", 128), ("sin1", 128), ("cos2", 128), ("sin2", 128), ("iota", 128), ("tid", 4), ("lt4", 16),
          ("eoff", 16), ("bl", 128), ("bc", 128)]


def constants():
    i = np.arange(P, dtype=np.float64)
    t = {}
    t["ident"] = np.eye(P)
    t["negtri"] = -(i[:, None] <= i[None, :]).astype(np.float64)
    t["negones"] = -np.ones((P, P))
    t["cmask"] = np.where(i[None, :] > i[:, None], -1e30, 0.0)
    t["wmask"] = np.where(i[None, :] < i[:, None], -1e30, 0.0)
    dec = np.zeros((P, 4, 2, P))
    for h in range(4):
        lg = np.log1p(-np.exp2(-5.0 - h))
        d = i[None, :] - i[:, None]
        dec[:, h, 0] = np.where(d >= 0, np.exp(lg * np.maximum(d, 0)), 0.0) * 128 ** -0.5
        dec[:, h, 1] = np.exp(lg * (128 + d)) * 128 ** -0.5
    tok = (np.arange(2)[None, :] * P + i[:, None]).astype(np.float32)
    inv = np.power(np.float32(10000.0), -np.arange(0, 128, 2, dtype=np.float32) / np.float32(128))
    ang = (tok[:, :, None] * inv).astype(np.float32).astype(np.float64)
    t["cos1"] = np.cos(ang).reshape(P, 128)
    t["sin1"] = np.sin(ang).reshape(P, 128)
    inv2 = np.power(np.float32(10000.0), -np.arange(16, dtype=np.float32) / np.float32(16))
    ar = ((tok // 64)[:, :, None] * inv2).astype(np.float32).astype(np.float64)
    ac = ((tok % 64)[:, :, None] * inv2).astype(np.float32).astype(np.float64)
    t["cos2"] = np.concatenate([np.cos(ar), np.cos(ar), np.cos(ac), np.cos(ac)], -1).reshape(P, 128)
    t["sin2"] = np.concatenate([-np.sin(ar), np.sin(ar), -np.sin(ac), np.sin(ac)], -1).reshape(P, 128)
    t["iota"] = np.broadcast_to(i[None, :], (P, P))
    t["tid"] = np.arange(4)[None, :] * P + i[:, None]
    t["lt4"] = np.broadcast_to((np.arange(4)[None, :] < np.arange(4)[:, None]).reshape(1, 16), (P, 16))
    t["eoff"] = np.broadcast_to(np.arange(16)[None, :] * P - 1.0, (P, 16))
    t["bl"] = np.where(np.isin(np.arange(P), (0, 1, 4))[:, None], 1.0, 0.0) * np.ones((P, P))
    t["bc"] = np.where(np.isin(np.arange(P), (2, 3, 4))[:, None], 1.0, 0.0) * np.ones((P, P))
    t["half"] = np.full((P, 1), -0.5)
    return (np.concatenate([np.asarray(t[n], np.float32).reshape(P, w) for n, w in CONSTS], 1),
            dec.reshape(P, 1024).astype(np.float32))


class Queue:

    def __init__(self, sem):
        self.sem, self.n, self.ops, self.met = sem, 0, [], {}
        self.dmas, self.open, self.soft = {}, [], set()

    def wait(self, *tickets):
        for t in tickets:
            if t is None:
                continue
            if isinstance(t, list):
                self.wait(*t)
                continue
            s, v = t
            if self.met.get(id(s), 0) < v:
                self.met[id(s)] = v
                self.ops.append(lambda e, s=s, v=v: e.wait_ge(s, v))

    def quiet(self, fn, *tickets):
        self.wait(*tickets)
        self.ops.append(fn)

    def __call__(self, fn, *tickets):
        self.wait(*tickets)
        self.n += 1
        self.ops.append(lambda e: fn(e).then_inc(self.sem, 1))
        return (self.sem, self.n)

    def activation(self, o, i, func, bias=0.0, scale=1.0, accum_out=None, after=()):
        return self(lambda e: e.activation(o, i, func, bias=bias, scale=scale, accum_out=accum_out), *after)

    def tensor_tensor(self, o, a, b, op, after=()):
        return self(lambda e: e.tensor_tensor(o, a, b, op), *after)

    def tensor_scalar(self, o, a, s1, s2, op0, op1=ALU.bypass, after=()):
        return self(lambda e: e.tensor_scalar(o, a, s1, s2, op0, op1), *after)

    def scalar_tensor_tensor(self, o, a, s, b, op0, op1, after=()):
        return self(lambda e: e.scalar_tensor_tensor(o, a, s, b, op0, op1), *after)

    def tensor_copy(self, o, i, after=()):
        return self(lambda e: e.tensor_copy(o, i), *after)

    def reciprocal(self, o, i, after=()):
        return self(lambda e: e.reciprocal(o, i), *after)

    def reduce_max(self, o, i, ax, negate=False, after=()):
        return self(lambda e: e.reduce_max(o, i, ax, negate=negate), *after)

    def reduce_sum(self, o, i, ax, after=()):
        return self(lambda e: e.reduce_sum(o, i, ax), *after)

    def bn_stats(self, o, i, after=()):
        return self(lambda e: e.bn_stats(o, i), *after)

    def bn_aggr(self, o, i, after=()):
        return self(lambda e: e.bn_aggr(o, i), *after)

    def memset(self, o, value, after=()):
        return self(lambda e: e.memset(o, value), *after)

    def gather_rows(self, o, table, index, sem, count, after=()):
        self.quiet(lambda e: e.indirect_dma_start(
            out=o, out_offset=None, in_=table,
            in_offset=bass.IndirectOffsetOnAxis(ap=index, axis=0)).then_inc(sem, 16), *after)
        self.soft.add(sem)
        self.dmas[sem] = 16 * count
        return (sem, 16 * count)

    def dma(self, out, in_, sem, count, *tickets):
        self.wait(*tickets)
        self.ops.append(lambda e: e.dma_start(out, in_).then_inc(sem, 16))
        self.dmas[sem] = 16 * count
        return (sem, 16 * count)

    def begin(self):
        self.open.append((self.ops, dict(self.met), self.n, dict(self.dmas)))
        self.ops = []

    def end(self, count, limit):
        body, n1, dmas1 = self.ops, self.n, dict(self.dmas)
        self.ops, self.met, n0, dmas0 = self.open.pop()
        owed = [(self.sem, n0, n1 - n0)] if n1 > n0 else []
        owed += [(s, dmas0.get(s, 0), v - dmas0.get(s, 0)) for s, v in dmas1.items() if v > dmas0.get(s, 0)]

        def run(e):
            value = e.value_load(count, min_val=0, max_val=512)
            with e.If(value > limit):
                for op in body:
                    op(e)
            with e.Else():
                for s, v0, _ in owed:
                    if v0:
                        e.wait_ge(s, v0)
                for s, _, d in owed:
                    if s in self.soft:
                        e.inc_swdge_sem([s], [d], mode="add")
                    else:
                        e.sem_inc(s, d)

        self.ops.append(run)

    def play(self, e):
        for op in self.ops:
            op(e)


NRAW = 4
SUB = 1024
NSPLIT = 5
AHEAD = NSPLIT - 1


def build(nc, A, out, consts, decay, plan):
    with ExitStack() as ctx:
        def sb(name, shape, dt=F32):
            return ctx.enter_context(nc.sbuf_tensor(name, shape, dt))

        def sem(name):
            return ctx.enter_context(nc.semaphore(name))

        RAW = sb("RAW", [P, NRAW, 2048])
        HI = sb("HI", [P, NSPLIT, SUB], F32R)
        LO = sb("LO", [P, NSPLIT, SUB], F32R)
        FR = sb("FR", [P, 8192], F32R)
        CS = sb("CS", [P, 8, P], F32R)
        XL = sb("XL", [P, 2, D])
        XC = sb("XC", [P, 2, D])
        HB = sb("HB", [P, 2, D])
        GB = sb("GB", [P, 2, D])
        SC = sb("SC", [P, 13700])
        CN = sb("CN", [P, sum(w for _, w in CONSTS)])
        SM = sb("SM", [P, 1340])
        CNT = sb("CNT", [P, 17], U32)
        IDX = sb("IDX", [P, 72], U32)
        PS = [ctx.enter_context(nc.psum_tensor(f"PS{i}", [P, 512], F32)) for i in range(8)]
        HD = nc.dram_tensor("HD", [512, D], F32, kind="Internal").ap()
        MOD = nc.dram_tensor("MOD", [2, 2, 4, 3072], F32, kind="Internal").ap()
        YD = nc.dram_tensor("YD", [NE * 512, D], F32, kind="Internal").ap()

        pe, act, dve, pool, sp = (Queue(sem(n)) for n in ("s_pe", "s_act", "s_dve", "s_pool", "s_sp"))
        s_raw = [sem(f"s_raw{i}") for i in range(NRAW)]
        s_hd, s_yd, s_xg, s_yg = ([sem(f"{n}{i}") for i in range(2)] for n in ("s_hd", "s_yd", "s_xg", "s_yg"))
        s_mod = [sem(f"s_mod{i}") for i in range(2)]
        s_gain = [sem(f"s_gain{i}") for i in range(2)]
        s_x = [sem(f"s_x{i}") for i in range(2)]
        s_first, s_const, s_ctx, s_r, s_fill, s_out = (sem(n) for n in (
            "s_first", "s_const", "s_ctx", "s_r", "s_fill", "s_out"))

        C, at = {}, 0
        for n, w in CONSTS:
            C[n] = CN[:, at:at + w]
            at += w
        ident = C["ident"]

        bank_free = [None] * 8
        buf_free = {}

        class Banks:
            def __init__(self, ids):
                self.ids, self.i = ids, 0

            def take(self):
                b = self.ids[self.i % len(self.ids)]
                self.i += 1
                return b

        def mm(o, l, r, start, stop, tr=False):
            return lambda e: e.matmul(o, l, r, start=start, stop=stop, is_transpose=True) if tr else \
                e.matmul(o, l, r, start=start, stop=stop)

        def pe_group(items, *tickets):
            pe.wait(*tickets)
            for it in items[:-1]:
                pe.quiet(it)
            return pe(items[-1])

        const_todo = []

        def const_load(o, i):
            const_todo.append((o, i))

        def load_consts():
            for n, (o, i) in enumerate(const_todo):
                sp.dma(o, i, s_const, n + 1)
            const_todo.clear()

        class Small:
            def __init__(self):
                self.at = 0

            def __call__(self, n):
                self.at += n
                assert self.at <= 1340, self.at
                return SM[:, self.at - n:self.at]

        small = Small()
        grow, gcol = SC[:, 13000:13128], small(48)
        sp.dma(CN[:, 0:129], consts[:, 0:129], s_first, 1)
        for i, n in enumerate(("norm_ffn1", "norm_mix", "norm_ffn2")):
            first_in = sp.dma(grow[16 * i:16 * i + 16, :], A[n].rearrange("l (k p) -> (l k) p", p=P), s_first, i + 2)
        x_in = [sp.dma(XL[:, t, :], A["x"][0, t * P:t * P + P, :], s_x[t], 1) for t in range(2)]
        const_load(CN[:, 129:], consts[:, 129:])
        XCF = XC[:, :, :].rearrange("p t d -> p (t d)")
        dec = XCF[:, 0:1024].rearrange("p (h b c) -> p h b c", h=4, b=2)
        const_load(XCF[:, 0:1024], decay)
        rnorm = [XCF[:, 1024 + 512 * i:1536 + 512 * i] for i in range(2)]
        bfor = [small(8) for _ in range(2)]
        for l in range(2):
            const_load(rnorm[l], A["ret_norm"][l:l + 1, :].partition_broadcast(P).rearrange("p a n -> p (a n)"))
            const_load(bfor[l], A["b_forget"][l:l + 1, :].partition_broadcast(P).rearrange("p a n -> p (a n)"))
        sink = small(16)
        const_load(sink, A["sink_a_2"][0:1, :].partition_broadcast(P).rearrange("p a n -> p (a n)"))
        subln = small(128)
        const_load(subln, A["subln_b_2"][0:1, :].partition_broadcast(P).rearrange("p a n -> p (a n)"))
        rbias = small(16)
        const_load(rbias, A["router_bias_2"].rearrange("(a n) -> a n", a=1).partition_broadcast(P)
                   .rearrange("p a n -> p (a n)"))
        lamb = small(256)
        const_load(lamb, A["lambda_b_2"][0].rearrange("a n -> (a n)").rearrange("(a n) -> a n", a=1)
                   .partition_broadcast(P).rearrange("p a n -> p (a n)"))
        crow = small(128)
        const_load(crow[0:8, :], A["c_2"][0].rearrange("(k p) -> k p", p=P))
        const_load(crow[8:16, :], A["c_ctx_2"].rearrange("(k p) -> k p", p=P))
        stat = small(512)
        loaded = (s_const, 16 * len(const_todo))
        for q in (pe, act, dve, pool):
            q.wait(first_in)
        x = pe_group([mm(PS[0][:, 0:48], grow[0:48, :], ident[0:48, 0:48], True, True, tr=True)])
        gcol_ready = bank_free[0] = act.activation(gcol, PS[0][:, 0:48], ACT.Copy, after=[x])

        class Weights:
            def __init__(self):
                self.log, self.part = [], 0
                self.loaded = self.split = self.used = 0
                self.arrival, self.freed, self.ready, self.spent = {}, {}, {}, {}
                self.parts, self.pending = [], None
                for n, (_, nk, ncol, region, _) in enumerate(plan or []):
                    ks = max(1, SUB // ncol)
                    for k in range(0, nk, ks):
                        self.parts.append((n, k, min(ks, nk - k), region))

            def load(self):
                while self.loaded < len(plan) and plan[self.loaded][3] == self.part and \
                        (self.loaded < NRAW or self.loaded - NRAW in self.freed):
                    n = self.loaded
                    at_, nk, ncol = plan[n][:3]
                    raw = RAW[:, n % NRAW, 0:nk * ncol].rearrange("p (k c) -> p k c", k=nk)
                    self.arrival[n] = sp.dma(raw, chunk_ap(*at_), s_raw[n % NRAW], n // NRAW + 1,
                                             self.freed.get(n - NRAW))
                    self.loaded += 1

            def split_next(self):
                m = self.split
                n, k, nk, _ = self.parts[m]
                ncol, s, gain = plan[n][2], m % NSPLIT, plan[n][4]
                w = nk * ncol
                raw = RAW[:, n % NRAW, k * ncol:k * ncol + w]
                after = [self.arrival[n], self.spent.get(m - NSPLIT), gcol_ready]
                if gain is None:
                    cuts = [(slice(0, w), None)]
                else:
                    g0 = 8 * gain + plan[n][0][1] + k
                    cuts = [(slice(ncol * q, ncol * q + ncol), gcol[:, g0 + q:g0 + q + 1]) for q in range(nk)]
                todo = [(c, g, act.activation(HI[:, s, c], raw[:, c], ACT.Copy, scale=1.0 if g is None else g, after=after))
                        for c, g in cuts]
                self.low_parts()
                self.pending = (m, raw, todo, after)
                self.split += 1

            def low_parts(self):
                if self.pending is None:
                    return
                (m, raw, todo, after), self.pending = self.pending, None
                n, k, nk, _ = self.parts[m]
                s = m % NSPLIT
                for c, g, hi in todo:
                    h = HI[:, s, c].bitcast(F32)
                    if g is None:
                        t = dve.tensor_tensor(LO[:, s, c], raw[:, c], h, ALU.subtract, after=[hi, after])
                    else:
                        t = dve.scalar_tensor_tensor(LO[:, s, c], raw[:, c], g, h, ALU.mult, ALU.subtract,
                                                     after=[hi, after])
                self.ready[m] = t
                if k + nk == plan[n][1]:
                    self.freed[n] = t

            def ahead(self):
                if plan is None:
                    return
                self.load()
                while self.split < min(self.used + NSPLIT, len(self.parts)) and self.parts[self.split][3] == self.part:
                    self.split_next()
                    self.load()
                self.low_parts()
                self.load()

            def chunk(self, at_, nk, ncol, gain=None):
                n = len(self.log)
                self.log.append((at_, nk, ncol, self.part, gain))
                assert plan is None or plan[n] == self.log[n]
                ks = max(1, SUB // ncol)
                for k in range(0, nk, ks):
                    m = self.used
                    self.used += 1
                    if plan is not None:
                        self.load()
                        while self.split <= min(m + AHEAD, len(self.parts) - 1) and \
                                self.parts[self.split][3] == self.part:
                            self.split_next()
                            self.load()
                        if m not in self.ready:
                            self.low_parts()
                            self.load()
                    kk = min(ks, nk - k)
                    hi, lo = (X[:, m % NSPLIT, 0:kk * ncol].rearrange("p (k c) -> p k c", k=kk) for X in (HI, LO))
                    yield k, kk, hi, lo, self.ready.get(m), m

        W = Weights()
        engines = (sp, pool, act, dve, pe)

        def begin():
            W.part += 1
            for q in engines:
                q.begin()

        def end(count, limit):
            W.part += 1
            for q in engines:
                q.end(count, limit)

        def rows(w, k0, nk, c0, ncol):
            return (w, k0, nk, c0, ncol)

        def chunk_ap(w, k0, nk, c0, ncol):
            a = A[w[0]]
            for i in w[1:]:
                a = a[i]
            return a[k0 * P:(k0 + nk) * P, c0:c0 + ncol].rearrange("(k p) c -> p k c", p=P)

        def gemm(w, k0, nk, c0, ncol, xh, xl, tiles, banks, first, last, *tickets, gain=None):
            pe.wait(*tickets)
            for k, kk, hi, lo, ready, m in W.chunk(rows(w, k0, nk, c0, ncol), nk, ncol, gain):
                pe.wait(ready)
                done = []
                for i, t in enumerate(tiles):
                    b = banks[i]
                    if first and k == 0:
                        pe.wait(bank_free[b])
                    o = PS[b][:, 0:ncol]
                    items = []
                    for q in range(kk):
                        h, ll = xh[:, k + q, t * P:(t + 1) * P], xl[:, k + q, t * P:(t + 1) * P]
                        items += [mm(o, h, hi[:, q, :], first and k + q == 0, False),
                                  mm(o, h, lo[:, q, :], False, False),
                                  mm(o, ll, hi[:, q, :], False, last and k + q == nk - 1)]
                    done.append(pe_group(items))
                W.spent[m] = done[-1]
            return done

        def proj(w, c0, ncol, xh, xl, tiles, banks, *tickets, gain=None):
            if ncol > 256:
                gemm(w, 0, 4, c0, ncol, xh[:, 0:4, :], xl[:, 0:4, :], tiles, banks, True, False, *tickets, gain=gain)
                return gemm(w, 4, 4, c0, ncol, xh[:, 4:8, :], xl[:, 4:8, :], tiles, banks, False, True, gain=gain)
            return gemm(w, 0, 8, c0, ncol, xh, xl, tiles, banks, True, True, *tickets, gain=gain)

        def to_T(src, nk, hi, lo, rot, ready, free=None, by_four=None):
            last = None
            for g in range(0, nk, 4):
                m = min(4, nk - g)
                b = rot.take()
                t = pe_group([mm(PS[b][:, k * P:(k + 1) * P], src[:, (g + k) * P:(g + k + 1) * P], ident, True, True,
                                 tr=True) for k in range(m)], by_four[g // 4] if by_four else ready, bank_free[b])
                v = PS[b][:, 0:m * P].rearrange("p (k c) -> p k c", k=m)
                a = act.activation(hi[:, g:g + m, :], v, ACT.Copy, after=[t, free])
                last = dve.tensor_tensor(lo[:, g:g + m, :], v, hi[:, g:g + m, :].bitcast(F32), ALU.subtract,
                    after=[a, free])
                bank_free[b] = last
            return last

        def to_T32(srcs, dst, rot, ready, free=None, eng=None):
            m = len(srcs)
            b = rot.take()
            t = pe_group([mm(PS[b][:, k * P:(k + 1) * P], s, ident, True, True, tr=True)
                          for k, s in enumerate(srcs)], ready, bank_free[b])
            v = PS[b][:, 0:m * P].rearrange("p (k c) -> p k c", k=m)
            if eng is dve:
                bank_free[b] = dve.tensor_copy(dst, v, after=[t, free])
            else:
                bank_free[b] = act.activation(dst, v, ACT.Copy, after=[t, free])
            return bank_free[b]

        n_gain = [0]
        gain_use = [None, None]

        def load_gain(row):
            i = n_gain[0] % 2
            n_gain[0] += 1
            t = sp.dma(GB[:, i, :], row.partition_broadcast(P).rearrange("p a n -> p (a n)"), s_gain[i],
                       (n_gain[0] + 1) // 2, gain_use[i])
            return GB[:, i, :], t, i

        def rstd_of(ss, n, eps, scale, ready):
            v = dve.tensor_scalar(ss, ss, scale, eps, ALU.mult, ALU.add, after=[ready])
            return pool.tensor_tensor(ss, ss, C["half"].to_broadcast([P, n]), ALU.pow, after=[v])

        def rms(src, dst, gain, col, ready, free=None):
            g, garr, slot = gain
            ss = stat[:, col:col + 1]
            a = act.activation(dst, src, ACT.Square, accum_out=ss, after=[ready, free])
            r = rstd_of(ss, 1, EPS, 1.0 / D, a)
            return dve.scalar_tensor_tensor(dst, src, ss, g, ALU.mult, ALU.mult, after=[r, garr])

        XTh = FR[:, 0:2048].rearrange("p (k t) -> p k t", k=8)
        XTl = FR[:, 2048:4096].rearrange("p (k t) -> p k t", k=8)

        h_free = [None, None]
        x_ready = [None, None]
        xt_free = [None]

        x_half = [[x_in[t]] * 2 for t in range(2)]
        rs = [stat[:, t:t + 1] for t in range(2)]
        rs_ready = [None, None]

        def norm_T(rot):
            done = [to_T(XL[:, t, :], 8, XTh[:, :, t * P:(t + 1) * P], XTl[:, :, t * P:(t + 1) * P], rot, None,
                         xt_free[0], by_four=x_half[t]) for t in range(2)]
            for t in range(2):
                h_free[t] = act.activation(HB[:, t, :], XL[:, t, :], ACT.Square, accum_out=rs[t],
                                           after=[x_half[t], h_free[t]])
                rs_ready[t] = rstd_of(rs[t], 1, EPS, 1.0 / D, h_free[t])
            return done

        def swiglu_unit(xh, xl, tiles, rot, wa, wb, gain, blocks, sbuf, gbuf, gts, flush, ready):
            pend = None
            T = len(tiles)
            for j, blk in enumerate(list(blocks) + [None]):
                if pend is not None:
                    pj, pc, gr = pend
                    nk = pc // P
                    gh, gl = gts[pj % 2]
                    tl = []
                    for i in range(T):
                        d = to_T(gbuf[pj % 2][:, i, 0:pc], nk, gh[:, 0:nk, i * P:(i + 1) * P],
                                 gl[:, 0:nk, i * P:(i + 1) * P], rot, gr[i], buf_free.get(("gt", pj % 2)))
                        tl.append(d)
                    buf_free[("g", pj % 2)] = tl[-1]
                if blk is not None:
                    c0, ncol = blk
                    ba = [rot.take() for _ in range(T)]
                    ra = proj(wa[0], wa[1] + c0, ncol, xh, xl, tiles, ba, ready, gain=gain)
                    bb = [rot.take() for _ in range(T)]
                    sr = []
                    for i in range(T):
                        sr.append(act.activation(sbuf[j % 2][:, i, 0:ncol], PS[ba[i]][:, 0:ncol], ACT.Silu, scale=rs[i],
                            after=[ra[i], rs_ready[i], buf_free.get(("s", j % 2))]))
                        bank_free[ba[i]] = sr[i]
                    rb = proj(wb[0], wb[1] + c0, ncol, xh, xl, tiles, bb, gain=gain)
                    gr = []
                    for i in range(T):
                        gr.append(dve.scalar_tensor_tensor(gbuf[j % 2][:, i, 0:ncol], PS[bb[i]][:, 0:ncol], rs[i],
                            sbuf[j % 2][:, i, 0:ncol], ALU.mult, ALU.mult,
                            after=[rb[i], sr[i], rs_ready[i], buf_free.get(("g", j % 2))]))
                        bank_free[bb[i]] = gr[i]
                    buf_free[("s", j % 2)] = gr[-1]
                if pend is not None:
                    buf_free[("gt", pj % 2)] = flush(pj, pc, gts[pj % 2], tl)
                pend = (j, ncol, gr) if blk is not None else None
                if j == 0:
                    load_consts()
                for _ in range((0, 2, 1, 1, 1, 1, 0)[j]):
                    fill_rows()

        SC0 = [0]

        def sc(n):
            SC0[0] += n
            assert SC0[0] <= 13700, SC0[0]
            return SC[:, SC0[0] - n:SC0[0]]

        ffn_gt = [(FR[:, 4096 + 2048 * i:4096 + 2048 * i + 1024].rearrange("p (k t) -> p k t", k=4),
                   FR[:, 4096 + 2048 * i + 1024:4096 + 2048 * i + 2048].rearrange("p (k t) -> p k t", k=4))
                  for i in range(2)]

        n_fill = [0]

        def fill_rows():
            r = NE * P + 256 * n_fill[0]
            n_fill[0] += 1
            act.dma(YD[r:r + 256, :].rearrange("(n p) d -> p n d", p=P),
                    CN[:, 0:D].unsqueeze(1).to_broadcast([P, 2, D]), s_fill, n_fill[0], loaded)

        def ffn(w_in, w_out, gain):
            rot = Banks([0, 1, 2, 3])
            SC0[0] = 0
            sbuf = [sc(1024).rearrange("p (t c) -> p t c", t=2) for _ in range(2)]
            gbuf = [sc(1024).rearrange("p (t c) -> p t c", t=2) for _ in range(2)]
            ready = norm_T(rot)
            blocks = [(512 * j, 512) for j in range(5)] + [(2560, 256)]
            fin = []

            def flush(j, pc, gt, tl):
                gh, gl = gt
                c0 = 512 * j
                last = j == 5
                d = None
                for k in range(0, pc // P, 2):
                    for q, _, hi, lo, rdy, m in W.chunk(rows(w_out, c0 // P + k, 2, 0, D), 2, D):
                        pe.wait(rdy, tl)
                        st, fl = j == 0 and k + q == 0, last and k + q == pc // P - 1
                        for t in range(2):
                            a, b = gh[:, k + q, t * P:(t + 1) * P], gl[:, k + q, t * P:(t + 1) * P]
                            for h in range(2):
                                o = PS[4 + 2 * t + h][:, :]
                                if st:
                                    pe.wait(bank_free[4 + 2 * t + h])
                                hh, ll = hi[:, 0, 512 * h:512 * h + 512], lo[:, 0, 512 * h:512 * h + 512]
                                d = pe_group([mm(o, a, hh, st, False), mm(o, a, ll, False, False),
                                              mm(o, b, hh, False, fl)])
                                if fl:
                                    fin.append(d)
                        W.spent[m] = d
                return d

            swiglu_unit(XTh, XTl, [0, 1], rot, (w_in, 0), (w_in, FF), gain, blocks, sbuf, gbuf, ffn_gt, flush, ready)
            for t in range(2):
                for h in range(2):
                    b = 4 + 2 * t + h
                    xs = XL[:, t, 512 * h:512 * h + 512]
                    x_ready[t] = x_half[t][h] = bank_free[b] = dve.scalar_tensor_tensor(xs, PS[b][:, :], 0.5, xs,
                        ALU.mult, ALU.add, after=[fin[2 * t + h], h_free[t]])
            xt_free[0] = fin[-1]

        OFF = {"rq": 0, "rk": 512, "rv": 1024, "rg": 1536, "fq": 2048, "fk": 2560, "fv": 3072, "ff": 3584,
               "gr": 3592, "gf": 4616}

        def sigmoid_by_exp(psrc, dst, ready):
            a = act.activation(dst, psrc, ACT.Exp, scale=-1.0, after=[ready])
            b = dve.tensor_scalar(dst, dst, 1.0, None, ALU.add, after=[a])
            return dve.reciprocal(dst, dst, after=[b]), a

        def attend(units, rot, pbuf, ptbuf, fill, later):
            n = len(units)
            st = [None] * n
            for i in range(n + 5):
                if i < n + 3:
                    next(fill, None)
                if 0 <= i - 2 < n:
                    u = units[i - 2]
                    k = u["w"] // P
                    wt, pb, _ = st[i - 2]
                    pt = ptbuf[i % len(ptbuf)]
                    st[i - 2][2] = to_T32([pb[:, P * j:P * j + P] for j in range(k)],
                                          pt[:, 0:k * P].rearrange("p (k c) -> p k c", k=k), rot, wt,
                                          buf_free.get(("pt", i % len(ptbuf))), dve if i % 2 and "weigh" not in u else act)
                    buf_free["p", (i - 2) % len(pbuf)] = st[i - 2][2]
                if 0 <= i - 1 < n and "weigh" in units[i - 1]:
                    es, pb, _ = st[i - 1]
                    st[i - 1][0] = units[i - 1]["weigh"](pb, es)
                if i < n:
                    u = units[i]
                    w = u["w"]
                    pb = pbuf[i % len(pbuf)]
                    es = []
                    for m, qk in enumerate(u["qk"]):
                        b = rot.take()
                        pe.wait(bank_free[b])
                        s = pe_group(qk(PS[b]), u["ready"])
                        nm = u["nm"][m]
                        x = dve.reduce_max(nm, PS[b][:, 0:w], AX, negate=True, after=[s])
                        if "negsink" in u:
                            x = dve.tensor_tensor(nm, nm, u["negsink"], ALU.min, after=[x])
                        y = bank_free[b] = act.activation(pb[:, 512 * m:512 * m + w], PS[b][:, 0:w], ACT.Exp, bias=nm,
                                                          accum_out=u["ss"][m],
                                                          after=[x, buf_free.get(("p", i % len(pbuf)))])
                        es.append(y)
                    st[i] = [es, pb, None]
                if 0 <= i - 3 < n:
                    u = units[i - 3]
                    k = u["w"] // P
                    pt = ptbuf[(i - 1) % len(ptbuf)]
                    if "out_free" in u:
                        pe.wait(u["out_free"]())
                    d = pe_group([mm(u["out"], pt[:, P * j:P * j + P], u["v"][j], j == 0, j == k - 1)
                                  for j in range(k)], st[i - 3][2])
                    buf_free["pt", (i - 1) % len(ptbuf)] = d
                    if "then" in u:
                        later.setdefault(i + 2, []).append(u["then"](d))
                for step in later.get(i, ()):
                    if step is not None:
                        step()

        def split_heads(t, n):
            return t.rearrange("p (h d) -> p h d", h=n)

        def mixer(l, gain, sections):
            w = ("w_in", l)
            rot = Banks([0, 1, 2, 3])
            ready = norm_T(rot)
            stage = [HB[0:4, t, 0:512] for t in range(2)]
            norm_free = list(h_free)
            fill = ada(sections, [4, 5], stage, h_free)
            SC0[0] = 0
            qT, kT, v, rg, fqT, fkT, fv = (sc(1024) for _ in range(7))
            tok = [sc(512) for _ in range(2)]
            tA, tB = sc(512), sc(512)
            pbuf = [sc(512) for _ in range(3)]
            ptbuf = [sc(256) for _ in range(2)]
            lfB = sc(2048).rearrange("p (t h c) -> p t h c", t=2, h=8)
            lf = sc(64)
            v3 = lambda a, t: a[:, 512 * t:512 * t + 512]
            tok_free = [None, None]
            pend = []

            def turn_heads(name, dst, t, y):
                fin[name, t] = tok_free[t] = to_T32([tok[t][:, P * h:P * h + P] for h in range(4)],
                                                    dst.rearrange("p (h c) -> p h c", h=4)[:, :, t * P:t * P + P], rot,
                                                    y, eng=act)

            def turn_pending():
                for a in pend:
                    turn_heads(*a)
                pend.clear()

            fin, turns, cs_r = {}, [], []
            for t in range(2):
                ct = sc(128)
                turns.append(ct)
                dve.tensor_scalar(ct[:, 0:64], C["cos1"][:, 64 * t:64 * t + 64], rs[t], None, ALU.mult,
                                  after=[rs_ready[t]])
                cs_r.append(dve.tensor_scalar(ct[:, 64:128], C["sin1"][:, 64 * t:64 * t + 64], rs[t], None, ALU.mult))
            for name, dst in (("rq", qT), ("rk", kT)):
                bb = [rot.take(), rot.take()]
                r = proj(w, OFF[name], 512, XTh, XTl, [0, 1], bb, ready, gain=gain)
                turn_pending()
                for t in range(2):
                    cos, sin = turns[t][:, 0:64], turns[t][:, 64:128]
                    src = PS[bb[t]][:, :].rearrange("p (h a d) -> p h a d", h=4, a=2)
                    a4 = tA.rearrange("p (h a d) -> p h a d", h=4, a=2)
                    b4 = tB.rearrange("p (h a d) -> p h a d", h=4, a=2)
                    o4 = tok[t].rearrange("p (h a d) -> p h a d", h=4, a=2)
                    fr = buf_free.get("rope")
                    x1 = dve.tensor_tensor(a4, src, cos.unsqueeze(1).unsqueeze(1).to_broadcast([P, 4, 2, 64]),
                        ALU.mult, after=[r[t], fr, cs_r[t]])
                    x2 = dve.tensor_tensor(b4[:, :, 0, :], src[:, :, 1, :], sin.unsqueeze(1).to_broadcast([P, 4, 64]),
                        ALU.mult, after=[fr])
                    x3 = dve.tensor_tensor(b4[:, :, 1, :], src[:, :, 0, :], sin.unsqueeze(1).to_broadcast([P, 4, 64]),
                        ALU.mult)
                    bank_free[bb[t]] = x3
                    pool.tensor_tensor(o4[:, :, 0, :], a4[:, :, 0, :], b4[:, :, 0, :], ALU.subtract,
                        after=[x3, tok_free[t]])
                    y = pool.tensor_tensor(o4[:, :, 1, :], a4[:, :, 1, :], b4[:, :, 1, :], ALU.add)
                    buf_free["rope"] = y
                    pend.append((name, dst, t, y))
            for name, dst in (("rv", v), ("fv", fv)):
                bb = [rot.take(), rot.take()]
                r = proj(w, OFF[name], 512, XTh, XTl, [0, 1], bb, gain=gain)
                turn_pending()
                for t in range(2):
                    fin[name, t] = bank_free[bb[t]] = act.activation(v3(dst, t), PS[bb[t]][:, :], ACT.Copy, scale=rs[t],
                        after=[r[t], rs_ready[t]])
            bb = [rot.take(), rot.take()]
            r = proj(w, OFF["rg"], 512, XTh, XTl, [0, 1], bb, gain=gain)
            for t in range(2):
                fin["rg", t] = bank_free[bb[t]] = act.activation(v3(rg, t), PS[bb[t]][:, :], ACT.Silu, scale=rs[t],
                                                                   after=[r[t], rs_ready[t]])
            rq8 = [stat[:, 2 + t:3 + t] for t in range(2)]
            sc_ready = [dve.tensor_scalar(rq8[t], rs[t], 0.125, None, ALU.mult, after=[rs_ready[t]]) for t in range(2)]
            for name, dst, sca in (("fq", fqT, rq8), ("fk", fkT, rs)):
                bb = [rot.take(), rot.take()]
                r = proj(w, OFF[name], 512, XTh, XTl, [0, 1], bb, gain=gain)
                turn_pending()
                for t in range(2):
                    y = bank_free[bb[t]] = act.activation(tok[t], PS[bb[t]][:, :], ACT.Copy, scale=sca[t],
                        after=[r[t], tok_free[t], sc_ready[t]])
                    pend.append((name, dst, t, y))
            bb = [rot.take(), rot.take()]
            r = proj(w, OFF["ff"], 8, XTh, XTl, [0, 1], bb, gain=gain)
            turn_pending()
            for t in range(2):
                z, e1, e2 = lf[:, 24 * t:24 * t + 8], lf[:, 24 * t + 8:24 * t + 16], lf[:, 24 * t + 16:24 * t + 24]
                x = bank_free[bb[t]] = dve.scalar_tensor_tensor(z, PS[bb[t]][:, 0:8], rs[t], bfor[l], ALU.mult, ALU.add,
                                                               after=[r[t], rs_ready[t]])
                x1 = dve.tensor_scalar(e1, z, -1.0, None, ALU.mult, after=[x])
                x1 = dve.tensor_tensor(e1, e1, z, ALU.min, after=[x1])
                x2 = act.activation(e1, e1, ACT.Exp, after=[x1])
                x2 = dve.tensor_scalar(e1, e1, 1.0, None, ALU.add, after=[x2])
                x2 = act.activation(e2, e1, ACT.Ln, after=[x2])
                x3 = dve.tensor_scalar(z, z, 0.0, None, ALU.min, after=[x1])
                x3 = dve.tensor_tensor(z, z, e2, ALU.subtract, after=[x3, x2])
                fin["lf", t] = dve.tensor_copy(lfB[:, t, :, :], z.unsqueeze(2).to_broadcast([P, 8, P]), after=[x3])
            prev = None
            rr = [fin["rq", 0], fin["rq", 1], fin["rk", 0], fin["rk", 1], fin["rv", 0], fin["rv", 1]]
            rdone = []
            for h in range(5):
                if h < 4:
                    b = rot.take()
                    q, k = qT[:, 256 * h:256 * h + 256], kT[:, 256 * h:256 * h + 256]
                    s = pe_group([mm(PS[b][:, 0:256], k[:, 0:P], q, True, True),
                                  mm(PS[b][:, 256:384], k[:, P:256], q[:, P:256], True, True)], rr, bank_free[b])
                    pb = pbuf[h % 3]
                    x = dve.tensor_tensor(pb[:, 0:256], PS[b][:, 0:256],
                        dec[:, h, :, :].rearrange("p b c -> p (b c)"), ALU.mult,
                        after=[s, buf_free.get(("p", h % 3))])
                    x = bank_free[b] = dve.tensor_tensor(pb[:, 256:384], PS[b][:, 256:384], dec[:, h, 0, :], ALU.mult,
                        after=[s])
                if prev is not None:
                    ph, ppb, px = prev
                    vv = [v3(v, t)[:, P * ph:P * ph + P] for t in range(2)]
                    if ph == 0:
                        pe.wait(bank_free[6], bank_free[7])
                    d = pe_group([mm(PS[6][:, P * ph:P * ph + P], ppb[:, 0:P], vv[0], True, True),
                                  mm(PS[7][:, P * ph:P * ph + P], ppb[:, P:256], vv[0], True, False),
                                  mm(PS[7][:, P * ph:P * ph + P], ppb[:, 256:384], vv[1], False, True)], px)
                    buf_free[("p", ph % 3)] = d
                prev = (h, pb, x) if h < 4 else None
                next(fill, None)
            RTh, RTl = (FR[:, 4096 + 1024 * i:5120 + 1024 * i].rearrange("p (k t) -> p k t", k=4) for i in range(2))
            FTh, FTl = (FR[:, 6144 + 1024 * i:7168 + 1024 * i].rearrange("p (k t) -> p k t", k=4) for i in range(2))
            rT = [None, None]
            ret_y = {}

            def ret_norm(t):
                ss = stat[:, 16 + 4 * t:20 + 4 * t]
                y = bank_free[6 + t] = act.activation(tok[t], PS[6 + t][:, :], ACT.Copy, after=[d, tok_free[t]])
                sq = HB[:, t, 512:1024]
                y1 = dve.tensor_tensor(sq, tok[t], tok[t], ALU.mult, after=[y, norm_free[t]])
                y2 = dve.reduce_sum(ss, split_heads(sq, 4), AX, after=[y1])
                h_free[t] = [h_free[t], y2]
                ret_y[t] = rstd_of(ss, 4, EPS, 1.0 / 128, y2)

            def ret_gate(t):
                ss = stat[:, 16 + 4 * t:20 + 4 * t]
                y4 = dve.tensor_tensor(split_heads(tok[t], 4), split_heads(tok[t], 4),
                    ss.unsqueeze(2).to_broadcast([P, 4, P]), ALU.mult, after=[ret_y[t]])
                y5 = pool.tensor_tensor(v3(rg, t), v3(rg, t), rnorm[l], ALU.mult, after=[fin["rg", t]])
                ret_y[t] = dve.tensor_tensor(tok[t], tok[t], v3(rg, t), ALU.mult, after=[y4, y5])

            def ret_turn(t):
                rT[t] = tok_free[t] = to_T(tok[t], 4, RTh[:, :, t * P:t * P + P], RTl[:, :, t * P:t * P + P], rot,
                                           ret_y[t], xt_free[0])

            later = {1: [lambda: ret_norm(0)], 3: [lambda: ret_gate(0), lambda: ret_norm(1)],
                     5: [lambda: ret_turn(0), lambda: ret_gate(1)], 7: [lambda: ret_turn(1)]}
            units, fT = [], [None, None]
            fr = [fin[n, t] for n in ("fq", "fk", "fv", "lf") for t in range(2)]
            nms, sums = stat[:, 64:80], stat[:, 80:96]

            def fox_out(d, t):
                r = sums[:, 8 * t:8 * t + 8]
                y = dve.reciprocal(r, r, after=[d])
                fo = (tA, tB)[t]
                y = bank_free[6 + t] = dve.tensor_tensor(split_heads(fo, 8), split_heads(PS[6 + t][:, :], 8),
                    r.unsqueeze(2).to_broadcast([P, 8, 64]), ALU.mult, after=[y, buf_free.get("rope")])

                def turn():
                    fT[t] = to_T(fo, 4, FTh[:, :, t * P:t * P + P], FTl[:, :, t * P:t * P + P], rot, y, xt_free[0])
                    buf_free["sg", t] = fT[t]
                return turn

            for t in range(2):
                for h in range(8):
                    o = 64 * (h % 2)
                    q = fqT[o:o + 64, 256 * (h // 2):256 * (h // 2) + 256]
                    k = fkT[o:o + 64, 256 * (h // 2):256 * (h // 2) + 256]

                    def qk(B, h=h, t=t, q=q, k=k):
                        if t == 0:
                            return [mm(B[:, 0:P], q[:, 0:P], k[:, 0:P], True, False),
                                    mm(B[:, 0:P], lfB[:, 0, h, :], C["negtri"], False, False),
                                    mm(B[:, 0:P], ident, C["cmask"], False, True)]
                        return [mm(B[:, 0:256], q[:, P:256], k, True, False),
                                mm(B[:, 0:P], lfB[:, 0, h, :], C["negtri"], False, False),
                                mm(B[:, P:256], lfB[:, 0, h, :], C["negones"], False, False),
                                mm(B[:, P:256], lfB[:, 1, h, :], C["negtri"], False, False),
                                mm(B[:, P:256], ident, C["cmask"], False, True)]
                    i = 8 * t + h
                    u = {"w": 128 * (t + 1), "qk": [qk], "ready": fr, "nm": [nms[:, i:i + 1]], "ss": [sums[:, i:i + 1]],
                         "out": PS[6 + t][:, 64 * h:64 * h + 64],
                         "v": [v3(fv, s)[:, 64 * h:64 * h + 64] for s in range(2)]}
                    if h == 0:
                        u["out_free"] = lambda t=t: bank_free[6 + t]
                    if h == 7:
                        u["then"] = lambda d, t=t: fox_out(d, t)
                    units.append(u)
            attend(units, rot, pbuf, ptbuf, fill, later)
            for _ in fill:
                pass
            mg_ready = {}
            for h in range(2):
                for wo, go, xh, xl_, rd in ((("w_o_ret", l), "gr", RTh, RTl, rT), (("w_o_fox", l), "gf", FTh, FTl, fT)):
                    bb = [rot.take(), rot.take()]
                    r = proj(w, OFF[go] + 512 * h, 512, XTh, XTl, [0, 1], bb, gain=gain)
                    sg = []
                    for t in range(2):
                        dst = (tA, tB)[t]
                        s = bank_free[bb[t]] = act.activation(dst, PS[bb[t]][:, :], ACT.Sigmoid, scale=rs[t],
                                                             after=[r[t], rs_ready[t], buf_free.get(("sg", t))])
                        sg.append(s)
                    yb = [rot.take(), rot.take()]
                    r = gemm(wo, 0, 4, 512 * h, 512, xh, xl_, [0, 1], yb, True, True, rd)
                    for t in range(2):
                        dst = (tA, tB)[t]
                        m = HB[:, t, 512 * h:512 * h + 512]
                        if go == "gr":
                            y = dve.tensor_tensor(m, dst, PS[yb[t]][:, :], ALU.mult, after=[r[t], sg[t], h_free[t]])
                            bank_free[yb[t]] = y
                            buf_free["sg", t] = y
                        else:
                            y = dve.tensor_tensor(dst, dst, PS[yb[t]][:, :], ALU.mult, after=[r[t], sg[t]])
                            bank_free[yb[t]] = y
                            y = dve.tensor_tensor(m, m, dst, ALU.add, after=[y, mg_ready[t, h]])
                            buf_free["sg", t] = y
                        mg_ready[t, h] = y
            xt_done = r[-1]
            mT = []
            for t in range(2):
                mT.append(to_T(HB[:, t, :], 8, XTh[:, :, t * P:t * P + P], XTl[:, :, t * P:t * P + P], rot,
                               [mg_ready[t, 0], mg_ready[t, 1]], xt_done))
                h_free[t] = mT[-1]
            for h in range(2):
                bb = [rot.take(), rot.take()]
                r = proj(("w_out", l), 512 * h, 512, XTh, XTl, [0, 1], bb, mT)
                for t in range(2):
                    xs = XL[:, t, 512 * h:512 * h + 512]
                    x_ready[t] = x_half[t][h] = bank_free[bb[t]] = dve.tensor_tensor(xs, PS[bb[t]][:, :], xs, ALU.add, after=[r[t]])
            xt_free[0] = r[-1]
            buf_free["rope"] = None

        def conditioning():
            cs_z = dve.memset(CS[:, :, :].bitcast(F32), 0.0)
            ccol, csig = small(16), small(16)
            x = pe_group([mm(PS[0][:, 0:16], crow[0:16, :], ident[0:16, 0:16], True, True, tr=True)], bank_free[0])
            y = act.activation(ccol, PS[0][:, 0:16], ACT.Copy, after=[x])
            s, a = sigmoid_by_exp(PS[0][:, 0:16], csig, x)
            bank_free[0] = [y, a]
            y = dve.tensor_tensor(ccol, ccol, csig, ALU.mult, after=[y, s])
            cv = ccol.rearrange("p (v k) -> p k v", v=2)
            cs4 = CS[:, :, 0:4].rearrange("p k (v a) -> p k v a", a=2)
            y = act.activation(cs4[:, :, :, 0], cv, ACT.Copy, after=[y, cs_z])
            cs_ready = dve.tensor_tensor(cs4[:, :, :, 1], cv, cs4[:, :, :, 0].bitcast(F32), ALU.subtract, after=[y])
            return cs_ready

        n_mod = [0, 0]
        mod_ready = {}

        def ada(sections, banks, stage, free):
            turn = 0
            for l, sec in sections:
                for c in range(6):
                    b = banks[c % 2]
                    for hk in range(2):
                        for k, kk, hi, lo, rdy, m in W.chunk(rows(("w_ada_2", l), 4 * hk, 4, 3072 * sec + 512 * c, 512),
                                                             4, 512):
                            pe.wait(rdy, cs_ready)
                            if hk == 0 and k == 0:
                                pe.wait(bank_free[b])
                            items = []
                            for q in range(kk):
                                cs = CS[:, 4 * hk + k + q, :]
                                items += [mm(PS[b][:, :], cs, hi[:, q, :], hk == 0 and k + q == 0, False),
                                          mm(PS[b][:, :], cs, lo[:, q, :], False, hk == 1 and k + q == 3)]
                            d = W.spent[m] = pe_group(items)
                            if hk == 1 and k + kk == 4:
                                i = turn % 2
                                turn += 1
                                y = bank_free[b] = act.activation(stage[i], PS[b][0:4, :], ACT.Copy, after=[d, free[i]])
                                n_mod[i] += 1
                                free[i] = act.dma(MOD[l, sec, :, 512 * c:512 * c + 512], stage[i], s_mod[i], n_mod[i], y)
                                mod_ready[l, sec] = both(s_mod, n_mod)
                            yield

        def both(sems, counts):
            return [(sems[i], 16 * counts[i]) for i in range(2) if counts[i]]

        n_r = [0]
        r_free = [None]
        RR = SC[0:5, 10628:13700]
        r_ready = [None]

        def load_mod(l, sec):
            n_r[0] += 2
            act.dma(RR[4:5, :], A["b_ada_2"][l:l + 1, 3072 * sec:3072 * sec + 3072], s_r, n_r[0] - 1, r_free[0])
            r_ready[0] = act.dma(RR[0:4, :], MOD[l, sec], s_r, n_r[0], mod_ready[l, sec])

        for l in range(2):
            ffn(("w_ffn1_in", l), ("w_ffn1_out", l), l)
            if l == 0:
                for q in (pe, act, dve, pool):
                    q.wait(loaded)
                cs_ready = conditioning()
            mixer(l, 2 + l, [(0, l)])
            if l == 1:
                r_free[0] = [(q.sem, q.n) for q in (pe, act, dve, pool)]
                load_mod(0, 0)
                ctx_in = act.dma(XC[:, :, :], A["ctx_2"][0].rearrange("(t p) d -> p t d", p=P), s_ctx, 1, r_free[0])
                c_ready = [ctx_in, ctx_in]
                g_final = load_gain(A["norm_final"].rearrange("(a n) -> a n", a=1))
            ffn(("w_ffn2_in", l), ("w_ffn2_out", l), 4 + l)
        for t in range(2):
            x_ready[t] = rms(XL[:, t, :], HB[:, t, :], g_final, t, x_ready[t], h_free[t])
            gain_use[g_final[2]] = x_ready[t]
            x_ready[t] = act.activation(XL[:, t, :], HB[:, t, :], ACT.Copy, after=[x_ready[t]])
            h_free[t] = x_ready[t]

        lt, l2 = small(128), small(2)
        y = dve.tensor_tensor(lt.rearrange("p (a n) -> p a n", a=2),
            lamb.rearrange("p (a b n) -> p a b n", a=2, b=2)[:, :, 0, :],
            lamb.rearrange("p (a b n) -> p a b n", a=2, b=2)[:, :, 1, :], ALU.mult)
        y = dve.reduce_sum(l2, lt.rearrange("p (a n) -> p a n", a=2), AX, after=[y])
        y = act.activation(l2, l2, ACT.Exp, after=[y])
        neglam = small(1)
        y = dve.tensor_tensor(neglam, l2[:, 1:2], l2[:, 0:1], ALU.subtract, after=[y])
        lam_ready = dve.tensor_scalar(neglam, neglam, -LAM_INIT, None, ALU.add, after=[y])
        negsink = small(16)
        sink_ready = dve.tensor_scalar(negsink, sink, -1.0, None, ALU.mult)
        subs_ready = dve.tensor_scalar(subln, subln, 1.0 - LAM_INIT, None, ALU.mult)

        def spread(which, col, rot):
            b = rot.take()
            m = C["bl" if which == 0 else "bc"][0:5, :]
            t = pe_group([mm(PS[b][:, :], m, RR[:, col:col + 512], True, True)], r_ready[0], bank_free[b])
            r_free[0] = t
            return b, t

        def modulate(x, which, tiles, dsts, rot, ready, free):
            done = [None] * len(tiles)
            for h in range(2):
                bs, ts = spread(which, 1024 + 512 * h, rot)
                bh, th = spread(which, 512 * h, rot)
                for i, t in enumerate(tiles):
                    o = dsts[i][:, 512 * h:512 * h + 512]
                    xs = x[:, t, 512 * h:512 * h + 512]
                    y = dve.scalar_tensor_tensor(o, PS[bs][:, :], 1.0, xs, ALU.add, ALU.mult,
                        after=[ts, ready[i], free[i]])
                    bank_free[bs] = y
                    y = bank_free[bh] = dve.tensor_tensor(o, o, PS[bh][:, :], ALU.add, after=[y, th])
                    done[i] = y
            return done


        def add_half(x, h, u, src, gate, col, ready, free=None):
            c = slice(512 * h, 512 * h + 512)
            y = dve.tensor_tensor(u, src, gate[:, c], ALU.mult, after=[ready, free])
            f = dve.scalar_tensor_tensor(x[:, c], x[:, c], ALPHA, u, ALU.mult, ALU.add, after=[y])
            return y, f, dve.bn_stats(stat[:, col + 6 * h:col + 6 * h + 6], x[:, c], after=[f])

        def ln_stats(col, ready):
            mv = stat[:, col + 12:col + 14]
            y = dve.bn_aggr(mv, stat[:, col:col + 12], after=[ready])
            return rstd_of(mv[:, 1:2], 1, EPS, 1.0, y)

        def ln_apply(x, gt, bt, col, ready):
            mv = stat[:, col + 12:col + 14]
            y = dve.scalar_tensor_tensor(x, x, mv[:, 0:1], gt[0], ALU.subtract, ALU.mult, after=[ready, gt[1]])
            y = dve.scalar_tensor_tensor(x, x, mv[:, 1:2], bt[0], ALU.mult, ALU.add, after=[y, bt[1]])
            gain_use[gt[2]] = gain_use[bt[2]] = y
            return y

        def gate_tile(which, dst, rot, free=None):
            y = None
            for h in range(2):
                b, t = spread(which, 2048 + 512 * h, rot)
                y = bank_free[b] = act.activation(dst[:, 512 * h:512 * h + 512], PS[b][:, :], ACT.Copy,
                    after=[t, free])
            return y

        X4h = FR[:, 0:4096].rearrange("p (k t) -> p k t", k=8)
        X4l = FR[:, 4096:8192].rearrange("p (k t) -> p k t", k=8)

        folded, norm_last = {}, []

        def fold(which, gt, bt, dst, rot, free):
            G, B = dst
            for h in range(2):
                c = slice(512 * h, 512 * h + 512)
                bs, ts = spread(which, 1024 + 512 * h, rot)
                bh, th = spread(which, 512 * h, rot)
                dve.scalar_tensor_tensor(G[:, c], PS[bs][:, :], 1.0, gt[0][:, c], ALU.add, ALU.mult,
                                         after=[ts, gt[1], free])
                y = bank_free[bs] = dve.scalar_tensor_tensor(B[:, c], PS[bs][:, :], 1.0, bt[0][:, c], ALU.add, ALU.mult,
                                                             after=[bt[1]])
                y = bank_free[bh] = dve.tensor_tensor(B[:, c], B[:, c], PS[bh][:, :], ALU.add, after=[y, th])
            folded[which] = (G, B, y)

        def modulate_folded(x, which, dsts, stats, free):
            G, B, rdy = folded.pop(which)
            done = []
            for t in range(2):
                mv = stat[:, 16 * (2 * which + t) + 12:16 * (2 * which + t) + 14]
                y = dve.scalar_tensor_tensor(dsts[t], x[:, t, :], mv[:, 0:1], G, ALU.subtract, ALU.mult,
                                             after=[stats[2 * which + t], rdy, free[t]])
                done.append(dve.scalar_tensor_tensor(dsts[t], dsts[t], mv[:, 1:2], B, ALU.mult, ALU.add, after=[y]))
            return done

        def hidden_part(which, rot, to_dram=None, dsts=None):
            done = []
            x = XC if which else XL
            rd = c_ready if which else x_ready
            dsts = dsts or [HB[:, 0, :], HB[:, 1, :]]
            if which in folded:
                hs = modulate_folded(x, which, dsts, norm_last[0][0], h_free)
            else:
                hs = modulate(x, which, [0, 1], dsts, rot, rd, h_free)
            for t in range(2):
                g = 2 * which + t
                fr = []
                if to_dram is not None:
                    fr = [to_dram(g, dsts[t], hs[t])]
                d = to_T(dsts[t], 8, X4h[:, :, g * P:g * P + P], X4l[:, :, g * P:g * P + P], rot, hs[t], xt_free[0])
                done.append(d)
                h_free[t] = [d, h_free[t]] + fr
            return done

        def hidden_T(nctx, rot, to_dram=None):
            done = [d for which in range(2 if nctx else 1) for d in hidden_part(which, rot, to_dram)]
            norm_now()
            return done

        def norm_now():
            if norm_last:
                stats, gt, bt, tiles = norm_last.pop()
                for t in tiles:
                    x, rd = (XL, x_ready) if t < 2 else (XC, c_ready)
                    rd[t % 2] = ln_apply(x[:, t % 2, :], gt, bt, 16 * t, stats[t])

        def rope2(src, dst, t, nh, ready, tmp, free, pairs=False):
            cos, sin = C["cos2"][:, 64 * t:64 * t + 64], C["sin2"][:, 64 * t:64 * t + 64]
            a, bq = tmp[0][:, 0:64 * nh], tmp[1][:, 0:64 * nh]
            v5 = lambda z: z.rearrange("p (h b a d) -> p h b a d", h=nh, b=2, a=2)
            s4 = sin.rearrange("p (b a d) -> p b a d", b=2, a=2)
            fr = buf_free.get("rope")
            x = dve.tensor_tensor(split_heads(a, nh), split_heads(src, nh),
                cos.unsqueeze(1).to_broadcast([P, nh, 64]), ALU.mult, after=[ready, fr])
            for half in range(2):
                x = dve.tensor_tensor(v5(bq)[:, :, :, half, :], v5(src)[:, :, :, 1 - half, :],
                    s4[:, :, half, :].unsqueeze(1).to_broadcast([P, nh, 2, 16]), ALU.mult, after=[fr])
            if pairs:
                dst, a, bq = paired(dst), a.rearrange("p (v g d) -> p v g d", v=2, g=4), \
                    bq.rearrange("p (v g d) -> p v g d", v=2, g=4)
            y = pool.tensor_tensor(dst, a, bq, ALU.add, after=[x, free])
            buf_free["rope"] = y
            return y, x

        def paired(dst):
            return dst.rearrange("p (g v d) -> p v g d", g=4, v=2)

        def attn_a(rot):
            SC0[0] = 0
            qT, kT, v = sc(4096), sc(1024), sc(1024)
            tok = [sc(512) for _ in range(2)]
            pbuf = [sc(512) for _ in range(3)]
            ptbuf = [sc(512) for _ in range(2)]
            st_ = sc(900)
            stage = [st_[0:4, 0:512], tok[0][0:4, :]]
            tmp = pbuf[0:2]
            tok = tok + ptbuf
            assert SC0[0] <= 10628
            w = ("wqkv_a_2", 0)
            ready = hidden_T(True, rot)
            q4 = qT.rearrange("p (n t) -> p n t", n=8)
            k4 = kT.rearrange("p (n t) -> p n t", n=2)
            fin = []
            tf = [None] * 4
            pend = []

            def turn_pending():
                for q, n, dst, y in pend:
                    tf[q] = to_T32([tok[q][:, P * g:P * g + P] for g in range(n)], dst, rot2, y, eng=act)
                    fin.append(tf[q])
                pend.clear()

            for blk in (2, 0, 1):
                bb = [rot.take() for _ in range(4)]
                r = proj(w, 512 * blk, 512, X4h, X4l, [0, 1, 2, 3], bb, ready)
                turn_pending()
                for t in range(4):
                    src = PS[bb[t]][:, :]
                    dst = tok[t]
                    if blk == 2:
                        if t < 2:
                            y, x = rope2(src[:, 0:256], dst[:, 0:256], t, 4, r[t], tmp, tf[t])
                        else:
                            y = x = act.activation(dst[:, 0:256], src[:, 0:256], ACT.Copy, after=[r[t], tf[t]])
                        z = act.activation(v[:, 256 * t:256 * t + 256], src[:, 256:512], ACT.Copy, after=[r[t], x])
                        bank_free[bb[t]] = [x, z]
                        fin.append(z)
                        pend.append((t, 2, k4[:, :, t * P:t * P + P], y))
                    else:
                        if t < 2:
                            y, x = rope2(src, dst, t, 8, r[t], tmp, tf[t], pairs=True)
                        else:
                            y = x = act.activation(paired(dst), src.rearrange("p (v g d) -> p v g d", v=2, g=4),
                                ACT.Copy, after=[r[t], tf[t]])
                        bank_free[bb[t]] = x
                        pend.append((t, 4, q4[:, 4 * blk:4 * blk + 4, t * P:t * P + P], y))
            turn_pending()
            xt_free[0] = r[-1]
            oT = [None] * 4
            buf_free["p", 0] = buf_free["p", 1] = buf_free["rope"]
            rot3 = Banks([0, 1, 2, 3])
            qs = dve.tensor_scalar(qT, qT, 0.125, None, ALU.mult, after=[fin])
            nms, sums, snk = stat[:, 64:128], stat[:, 128:192], stat[:, 192:256]
            stage_free = [fin, fin]
            fill = ada([(1, 0), (1, 1)], [4, 5], stage, stage_free)
            units = []
            act.wait(sink_ready)

            def half(d, t, hh):
                cols = slice(16 * t + 8 * hh, 16 * t + 8 * hh + 8)
                hb = HB[:, t % 2, 512 * hh:512 * hh + 512]
                y = dve.tensor_tensor(snk[:, cols], nms[:, cols], sink[:, 8 * hh:8 * hh + 8], ALU.add, after=[d])
                y = act.activation(snk[:, cols], snk[:, cols], ACT.Exp, after=[y])
                y = dve.tensor_tensor(sums[:, cols], sums[:, cols], snk[:, cols], ALU.add, after=[y])
                y = dve.reciprocal(sums[:, cols], sums[:, cols], after=[y])
                y = bank_free[6 + hh] = dve.tensor_tensor(split_heads(hb, 8), split_heads(PS[6 + hh][:, :], 8),
                    sums[:, cols].unsqueeze(2).to_broadcast([P, 8, 64]), ALU.mult, after=[y, h_free[t % 2]])
                if hh == 0:
                    return None

                def turn():
                    h_free[t % 2] = oT[t] = to_T(HB[:, t % 2, :], 8, X4h[:, :, t * P:t * P + P],
                                                 X4l[:, :, t * P:t * P + P], rot3, y, xt_free[0])
                return turn

            for t in range(4):
                for h in range(16):
                    kv, g = h // 4, h % 4
                    o = 64 * (kv % 2)
                    q = q4[o:o + 64, 4 * (kv // 2) + g, t * P:t * P + P]
                    k = k4[o:o + 64, kv // 2, :]
                    if t < 2:
                        def qk(B, q=q, k=k, t=t):
                            m = (B[:, P:256], C["cmask"]) if t == 0 else (B[:, 0:P], C["wmask"])
                            return [mm(B[:, 0:512], q, k, True, False), mm(m[0], ident, m[1], False, True)]
                        vt = [0, 1, 2, 3]
                    else:
                        def qk(B, q=q, k=k):
                            return [mm(B[:, 0:256], q, k[:, 256:512], True, True)]
                        vt = [2, 3]
                    i = 16 * t + h
                    u = {"w": P * len(vt), "qk": [qk], "ready": [qs] + fin, "nm": [nms[:, i:i + 1]],
                         "ss": [sums[:, i:i + 1]], "negsink": negsink[:, h:h + 1],
                         "out": PS[6 + h // 8][:, 64 * (h % 8):64 * (h % 8) + 64],
                         "v": [v[:, 256 * s + 64 * kv:256 * s + 64 * kv + 64] for s in vt]}
                    if h % 8 == 0:
                        u["out_free"] = lambda h=h: bank_free[6 + h // 8]
                    if h % 8 == 7:
                        u["then"] = lambda d, t=t, h=h: half(d, t, h // 8)
                    units.append(u)
            attend(units, rot3, pbuf, ptbuf, fill, {})
            for _ in fill:
                pass
            return oT + stage_free

        def attn_b(rot, add_up):
            SC0[0] = 0
            qT, kT, v = sc(2048), sc(4096), None
            tok2 = sc(1024)
            tok = [tok2[:, 0:512], tok2[:, 512:1024]]
            pbuf = [sc(1024) for _ in range(2)] + [tok2]
            ptbuf = [sc(512) for _ in range(2)]
            tmp = [pbuf[1][:, 0:512], pbuf[1][:, 512:1024]]
            tok = tok + ptbuf
            assert SC0[0] <= 10628
            w = ("wqkv_b_2", 0)
            ready = hidden_part(0, rot, dsts=[HB[:, 0, :], SC[:, 0:1024]])
            W.ahead()
            q4 = qT.rearrange("p (n t) -> p n t", n=8)
            k4 = kT.rearrange("p (n t) -> p n t", n=8)
            vt = [XC[:, 0, :], XC[:, 1, :], VX[:, 0:1024], VX[:, 1024:2048]]
            fin, tf, pend = [], [None] * 4, []

            def turn_pending():
                for q, dst, y in pend:
                    tf[q] = to_T32([tok[q][:, P * n:P * n + P] for n in range(4)], dst, rot2, y, eng=act)
                    fin.append(tf[q])
                pend.clear()

            for blk in range(6):
                tiles = [0, 1] if blk < 2 else [0, 1, 2, 3]
                if blk == 2:
                    ready = ctx_dead = hidden_part(1, rot2)
                    norm_now()
                if blk < 2:
                    add_up(2 + blk)
                bb = [rot.take() for _ in tiles]
                r = proj(w, 512 * blk, 512, X4h, X4l, tiles, bb, ready)
                turn_pending()
                for t in tiles:
                    src, dst = PS[bb[t]][:, :], tok[t]
                    if blk >= 4:
                        z = bank_free[bb[t]] = act.activation(vt[t][:, 512 * (blk - 4):512 * (blk - 4) + 512], src,
                            ACT.Copy, after=[r[t], ctx_dead])
                        fin.append(z)
                        continue
                    if t < 2:
                        y, x = rope2(src, dst, t, 8, r[t], tmp, tf[t])
                    else:
                        y = x = act.activation(dst, src, ACT.Copy, after=[r[t], tf[t]])
                    bank_free[bb[t]] = x
                    dd = (q4 if blk < 2 else k4)[:, 4 * (blk % 2):4 * (blk % 2) + 4, t * P:t * P + P]
                    pend.append((t, dd, y))
            xt_free[0] = r[-1]
            buf_free["p", 0] = buf_free["p", 1] = buf_free["rope"]
            rot3 = Banks([0, 1, 2, 3, 4, 5])
            qs = dve.tensor_scalar(qT, qT, 0.125, None, ALU.mult, after=[fin])
            nms, sums, ratio = stat[:, 64:96], stat[:, 96:128], stat[:, 128:144]
            units, oT = [], [None, None]
            out_y = {}

            def half(d, t, hh):
                hb = HB[:, t, 512 * hh:512 * hh + 512]
                r = sums[:, 16 * t + 8 * hh:16 * t + 8 * hh + 8].rearrange("p (h m) -> p h m", m=2)[:, :, 0]
                y = dve.reciprocal(r, r, after=[d])
                y = bank_free[6 + hh] = dve.tensor_tensor(split_heads(hb, 4), split_heads(PS[6 + hh][:, :], 4),
                    r.unsqueeze(2).to_broadcast([P, 4, P]), ALU.mult, after=[y, h_free[t]])
                sq = GB[:, t, 512 * hh:512 * hh + 512]
                ss = stat[:, 480 + 8 * t + 4 * hh:484 + 8 * t + 4 * hh]
                x = dve.tensor_tensor(sq, hb, hb, ALU.mult, after=[y, gain_use[t]])
                x = dve.reduce_sum(ss, split_heads(sq, 4), AX, after=[x])
                x = rstd_of(ss, 4, 1e-5, 1.0 / 128, x)
                out_y[hh] = x
                if hh == 0:
                    return None
                ss, hb = stat[:, 480 + 8 * t:488 + 8 * t], HB[:, t, :]
                y = dve.tensor_tensor(split_heads(hb, 8), split_heads(hb, 8), ss.unsqueeze(2).to_broadcast([P, 8, P]),
                    ALU.mult, after=[y, out_y[0], x])
                gain_use[t] = y
                y = dve.tensor_tensor(split_heads(hb, 8), split_heads(hb, 8),
                    subln.unsqueeze(1).to_broadcast([P, 8, P]), ALU.mult, after=[y, subs_ready])

                def turn():
                    h_free[t] = oT[t] = to_T(HB[:, t, :], 8, X4h[:, :, t * P:t * P + P], X4l[:, :, t * P:t * P + P],
                                             rot3, y, xt_free[0])
                return turn

            for t in range(2):
                for h in range(8):
                    qks = []
                    for m in range(2):
                        qks.append(lambda B, h=h, m=m, t=t: [mm(
                            B[:, 0:512], q4[64 * m:64 * m + 64, h, t * P:t * P + P], k4[64 * m:64 * m + 64, h, :],
                            True, True)])
                    i = 8 * t + h
                    s0, s1, ra = sums[:, 2 * i:2 * i + 1], sums[:, 2 * i + 1:2 * i + 2], ratio[:, i:i + 1]

                    def weigh(pb, es, s0=s0, s1=s1, ra=ra):
                        y = dve.reciprocal(s1, s1, after=[es[1]])
                        y = dve.scalar_tensor_tensor(ra, s0, neglam, s1, ALU.mult, ALU.mult, after=[y, es, lam_ready])
                        return dve.scalar_tensor_tensor(pb[:, 0:512], pb[:, 512:1024], ra, pb[:, 0:512], ALU.mult,
                            ALU.add, after=[y])
                    u = {"w": 512, "qk": qks, "ready": [qs] + fin, "nm": [nms[:, 2 * i + m:2 * i + m + 1] for m in range(2)],
                         "ss": [s0, s1], "weigh": weigh, "out": PS[6 + h // 4][:, P * (h % 4):P * (h % 4) + P],
                         "v": [vt[s][:, P * h:P * h + P] for s in range(4)]}
                    if h % 4 == 0:
                        u["out_free"] = lambda h=h: bank_free[6 + h // 4]
                    if h % 4 == 3:
                        u["then"] = lambda d, t=t, h=h: half(d, t, h // 4)
                    units.append(u)
            attend(units, rot3, pbuf, ptbuf, iter(()), {})
            return oT

        VX = SC[:, 10240:12288]

        def attn_out(l, wo, tiles, oT, rot):
            gl = load_gain(A["ln_attn_g_2"][l:l + 1, :])
            bl = load_gain(A["ln_attn_b_2"][l:l + 1, :])
            SC0[0] = 0
            gates = [sc(1024), sc(1024)]
            u = [sc(1024) for _ in range(4)]
            gr = [gate_tile(w, gates[w], rot, oT) for w in range(2 if len(tiles) > 2 else 1)]
            load_mod(l, 1)
            ur = {}
            for h in range(2):
                bb = [rot.take() for _ in tiles]
                r = proj(wo, 512 * h, 512, X4h, X4l, tiles, bb, oT)
                for i, t in enumerate(tiles):
                    x, rd = (XL, x_ready) if t < 2 else (XC, c_ready)
                    bank_free[bb[i]], f, ur[t] = add_half(x[:, t % 2, :], h, u[t][:, 512 * h:512 * h + 512],
                                                          PS[bb[i]][:, :], gates[t // 2], 16 * t,
                                                          [r[i], oT, gr[t // 2], rd[t % 2]])
                if h == 0:
                    for which in range(len(tiles) // 2):
                        fold(which, gl, bl, (sc(1024), sc(1024)), rot, oT)
            xt_free[0] = r[-1]
            norm_last.append(({t: ln_stats(16 * t, ur[t]) for t in tiles}, gl, bl, tiles))

        filled = (s_fill, 16 * n_fill[0])
        n_hd, n_yd, n_xg, n_yg = [0, 0], [0, 0], [0, 0], [0, 0]

        hd_free = [None]
        yd_free = [None]

        def top(b, n, ranks, tmp, lim, ready):
            big = tmp[0].rearrange("p (g i j) -> p g i j", i=4, j=4)[:, 0:n, :, :]
            eq = tmp[1].rearrange("p (g i j) -> p g i j", i=4, j=4)[:, 0:n, :, :]
            bj = b.unsqueeze(2).to_broadcast([P, n, 4, 4])
            bi = b.unsqueeze(3).to_broadcast([P, n, 4, 4])
            lt = C["lt4"].rearrange("p (i j) -> p i j", i=4).unsqueeze(1).to_broadcast([P, n, 4, 4])
            x = dve.tensor_tensor(big, bj, bi, ALU.is_gt, after=[ready])
            y = dve.tensor_tensor(eq, bj, bi, ALU.is_equal, after=[ready])
            y = dve.tensor_tensor(eq, eq, lt, ALU.mult, after=[y])
            y = dve.tensor_tensor(big, big, eq, ALU.add, after=[x, y])
            y = dve.reduce_sum(ranks, big, AX, after=[y])
            return dve.tensor_scalar(ranks, ranks, lim, None, ALU.is_lt, after=[y])

        def moe(l, NT):
            rot = Banks(list(range(8)))
            rows_out = []

            def to_dram(g, h, rd):
                n_hd[g % 2] += 1
                return sp.dma(HD[g * P:g * P + P, :], h, s_hd[g % 2], n_hd[g % 2], rd, hd_free[0])

            ready = hidden_T(NT == 4, rot, to_dram)
            hd_ready = both(s_hd, n_hd)
            gl = load_gain(A["ln_ffn_g_2"][l:l + 1, :])
            bl = load_gain(A["ln_ffn_b_2"][l:l + 1, :])
            SC0[0] = 0
            N16 = NT * 16
            z = [sc(64)[:, 0:N16] for _ in range(10)]
            tmp = [sc(256), sc(256)]
            gs, gsel = sc(16)[:, 0:NT * 4], sc(16)[:, 0:NT * 4]
            pe_b = [sc(128) for _ in range(4)]
            SC0[0] = 2048
            xg = [sc(1024) for _ in range(2)]
            ysb = [sc(1024) for _ in range(2)]
            fold_to = [sc(1024) for _ in range(4)]
            sbuf, gbuf = ([fold_to[a][:, 512 * b:512 * b + 512] for b in range(2)] for a in (1, 3))
            s2 = sc(64)
            assert SC0[0] <= 10628, SC0[0]
            b = rot.take()
            for _, _, hi, lo, rdy, m in W.chunk(rows(("w_router_2",), 0, 8, 0, 16), 8, 16):
                pe.wait(rdy, ready, bank_free[b])
                o = PS[b][0:16, 0:NT * P]
                it = []
                for k in range(8):
                    h, ll = X4h[:, k, 0:NT * P], X4l[:, k, 0:NT * P]
                    it += [mm(o, hi[:, k, :], h, k == 0, False), mm(o, lo[:, k, :], h, False, False),
                           mm(o, hi[:, k, :], ll, False, k == 7)]
                d = W.spent[m] = pe_group(it)
            lgT = ysb[0][0:16, 0:NT * P]
            y = bank_free[b] = act.activation(lgT, PS[b][0:16, 0:NT * P], ACT.Copy, after=[d])
            b = rot.take()
            d = buf_free["y", 0] = pe_group([mm(PS[b][:, 16 * t:16 * t + 16], lgT[:, t * P:t * P + P], ident[0:16, 0:16],
                                                True, True, tr=True) for t in range(NT)], y, bank_free[b])
            xt_free[0] = d
            s, bb, ing, sel, wgt, posm, slot, t0, t1, t2 = z
            y, a = sigmoid_by_exp(PS[b][:, 0:N16], s, d)
            bank_free[b] = a
            v3 = lambda q: q.rearrange("p (t e) -> p t e", t=NT)
            g4 = lambda q: q.rearrange("p (g j) -> p g j", j=4)
            y = dve.tensor_tensor(v3(bb), v3(s), rbias.unsqueeze(1).to_broadcast([P, NT, 16]), ALU.add, after=[y])
            y = top(g4(bb), NT * 4, g4(ing), tmp, 1.5, y)
            y = dve.tensor_tensor(t0, bb, ing, ALU.mult, after=[y])
            y = dve.reduce_sum(gs, g4(t0), AX, after=[y])
            y = top(g4(gs), NT, g4(gsel), tmp, 0.5, y)
            y = dve.tensor_tensor(g4(sel), g4(ing), gsel.unsqueeze(2).to_broadcast([P, NT * 4, 4]), ALU.mult,
                after=[y])
            sel_r = y
            y = dve.tensor_tensor(t0, s, sel, ALU.mult, after=[y])
            den, sl0, sl1, w0, w1 = (s2[:, 4 * i:4 * i + NT] for i in range(5))
            y = dve.reduce_sum(den, v3(t0), AX, after=[y])
            y = dve.reciprocal(den, den, after=[y])
            wr = dve.tensor_tensor(v3(wgt), v3(t0), den.unsqueeze(2).to_broadcast([P, NT, 16]), ALU.mult, after=[y])
            b = rot.take()
            pe.wait(bank_free[b], sel_r)
            for t in range(NT):
                d = pe_group([mm(PS[b][:, 16 * t:16 * t + 16], C["negtri" if u == t else "negones"],
                                 v3(sel)[:, u, :], u == 0, u == t) for u in range(t + 1)])
            d = pe_group([mm(PS[b][:, 64:80], C["negones"], v3(sel)[:, u, :], u == 0, u == NT - 1) for u in range(NT)])
            cf = s2[:, 32:49]
            y = dve.tensor_scalar(cf[:, 0:16], PS[b][:, 64:80], -1.0, None, ALU.mult, after=[d])
            y = dve.reduce_max(cf[:, 16:17], cf[:, 0:16], AX, after=[y])
            cnt_r = dve.tensor_copy(CNT[:, :], cf, after=[y])
            y = dve.tensor_scalar(posm, sel, -4096.0, 4095.0, ALU.mult, ALU.add, after=[sel_r])
            pos_r = dve.tensor_tensor(posm, posm, PS[b][:, 0:N16], ALU.subtract, after=[y, d])
            y = dve.tensor_tensor(v3(slot), C["eoff"].unsqueeze(1).to_broadcast([P, NT, 16]),
                v3(PS[b][:, 0:N16]), ALU.subtract, after=[d])
            for j in range(1, NT):
                y1 = dve.tensor_scalar(t0, PS[b][:, 0:N16], -(P * j + 1.0), float(NE * P - P), ALU.is_le, ALU.mult,
                                       after=[y, wr])
                y = dve.tensor_tensor(slot, slot, t0, ALU.add, after=[y1])
            bank_free[b] = y
            y1 = dve.tensor_tensor(t1, slot, sel, ALU.mult, after=[y])
            y1 = dve.reduce_max(sl1, v3(t1), AX, after=[y1])
            y2 = dve.tensor_scalar(t2, slot, -1.0, BIG, ALU.mult, ALU.add, after=[y])
            y2 = dve.tensor_tensor(t2, t2, sel, ALU.mult, after=[y2])
            y2 = dve.reduce_max(sl0, v3(t2), AX, after=[y2])
            y2 = dve.tensor_scalar(sl0, sl0, -1.0, BIG, ALU.mult, ALU.add, after=[y2])
            for sl, ww, yy, tt in ((sl0, w0, y2, t1), (sl1, w1, y1, t2)):
                y = dve.tensor_tensor(v3(tt), v3(slot), sl.unsqueeze(2).to_broadcast( [P, NT, 16]), ALU.is_equal,
                    after=[yy, y1, y2])
                y = dve.tensor_tensor(tt, tt, wgt, ALU.mult, after=[y, wr])
                w_r = dve.reduce_sum(ww, v3(tt), AX, after=[y])
            sidx = IDX[:, 64:64 + 2 * NT].rearrange("p (k t) -> p k t", k=2)
            dve.tensor_copy(sidx[:, 0, :], sl0, after=[y2])
            sidx_r = dve.tensor_copy(sidx[:, 1, :], sl1, after=[y1])

            def places(e_, j, rdy):
                return [dve.tensor_scalar(pe_b[t], C["iota"], float(P * j), posm[:, 16 * t + e_:16 * t + e_ + 1], ALU.add,
                                          ALU.is_equal, after=[rdy, buf_free.get(("pe", t))]) for t in range(NT)]

            def indices(e_, j, ys):
                b = rot.take()
                c = 16 * j + e_
                d = pe_group([mm(PS[b][:, 0:1], pe_b[t], C["tid"][:, t:t + 1], t == 0, t == NT - 1) for t in range(NT)],
                             bank_free[b], ys)
                for t in range(NT):
                    buf_free["pe", t] = d
                bank_free[b] = dve.tensor_copy(IDX[:, c:c + 1], PS[b][:, 0:1], after=[d])
                return bank_free[b]

            xts = [(FR[:, 2048 * i:2048 * i + 1024].rearrange("p (k t) -> p k t", k=8),
                    FR[:, 2048 * i + 1024:2048 * i + 2048].rearrange("p (k t) -> p k t", k=8)) for i in range(2)]
            gts = [(FR[:, 4096 + 1024 * i:4096 + 1024 * i + 512].rearrange("p (k t) -> p k t", k=4),
                    FR[:, 4608 + 1024 * i:4608 + 1024 * i + 512].rearrange("p (k t) -> p k t", k=4)) for i in range(2)]
            buf_free["xt", 0] = buf_free["xt", 1] = buf_free["gt", 0] = buf_free["gt", 1] = d

            def gather(i, icol, rdy):
                n_xg[i % 2] += 1
                return pool.gather_rows(xg[i % 2], HD[:, :], IDX[:, icol:icol + 1], s_xg[i % 2], n_xg[i % 2],
                                        after=[rdy, hd_ready, buf_free.get(("xg", i % 2))])

            xt_r, g_t = {}, {}

            def fetch(i, e_, j, rdy):
                g_t[i] = gather(i, 16 * j + e_, rdy)

            def prep(i):
                xh, xl_ = xts[i % 2]
                xt_r[i] = to_T(xg[i % 2], 8, xh, xl_, rot, g_t[i], buf_free["xt", i % 2])
                buf_free["xg", i % 2] = xt_r[i]

            def up(i, e_):
                xh, xl_ = xts[i % 2]
                ba, bb_ = rot.take(), rot.take()
                ra = proj(("w_gate_2", l, e_), 0, DE, xh, xl_, [0], [ba], xt_r[i])
                sr = bank_free[ba] = act.activation(sbuf[i % 2], PS[ba][:, :], ACT.Silu,
                                                    after=[ra, buf_free.get(("s", i % 2))])
                rb = proj(("w_up_2", l, e_), 0, DE, xh, xl_, [0], [bb_])
                buf_free["xt", i % 2] = rb[0]
                gr = bank_free[bb_] = dve.tensor_tensor(gbuf[i % 2], sbuf[i % 2], PS[bb_][:, :], ALU.mult,
                                                        after=[rb, sr, buf_free.get(("g", i % 2))])
                buf_free["s", i % 2] = gr
                return gr

            def turn(i, gr):
                gh, gw = gts[i % 2]
                buf_free["g", i % 2] = to_T(gbuf[i % 2], 4, gh, gw, rot, gr, buf_free["gt", i % 2])
                return buf_free["g", i % 2]

            def down(i, e_, j, tl):
                gh, gw = gts[i % 2]
                for h in range(2):
                    by = rot.take()
                    r = gemm(("w_down_2", l, e_), 0, 4, 512 * h, 512, gh, gw, [0], [by], True, True, tl)
                    y = bank_free[by] = act.activation(ysb[i % 2][:, 512 * h:512 * h + 512], PS[by][:, :], ACT.Copy,
                                                       after=[r, buf_free.get(("y", i % 2))])
                buf_free["gt", i % 2] = r[0]
                n_yd[i % 2] += 1
                base = (j * NE + e_) * P
                buf_free["y", i % 2] = act.dma(YD[base:base + P, :], ysb[i % 2], s_yd[i % 2], n_yd[i % 2], y, yd_free[0],
                                             filled)

            gates = [HB[:, 0, :], HB[:, 1, :]]
            gates_r = [gate_tile(w, gates[w], rot, h_free[w]) for w in range(2 if NT == 4 else 1)]
            if l == 0:
                load_mod(1, 0)
            rdy = {e_: indices(e_, 0, places(e_, 0, pos_r)) for e_ in range(2)}
            fetch(0, 0, 0, rdy[0])
            prep(0)
            gr = [None] * NE
            for i in range(NE + 1):
                if i + 1 < NE:
                    fetch(i + 1, i + 1, 0, rdy[i + 1])
                if i + 2 < NE:
                    ys = places(i + 2, 0, pos_r)
                if i:
                    tl = turn(i - 1, gr[i - 1])
                if i < NE:
                    gr[i] = up(i, i)
                    if i + 2 < NE:
                        rdy[i + 2] = indices(i + 2, 0, ys)
                if i + 1 < NE:
                    prep(i + 1)
                if i:
                    down(i - 1, i - 1, 0, tl)
            for q in engines:
                q.wait(cnt_r)
            n_tile = [NE]

            def further(j):
                begin()
                for e_ in range(NE):
                    begin()
                    i = n_tile[0]
                    n_tile[0] += 1
                    fetch(i, e_, j, indices(e_, j, places(e_, j, pos_r)))
                    prep(i)
                    down(i, e_, j, turn(i, up(i, e_)))
                    end(CNT[0:1, e_:e_ + 1], P * j)
                if j + 1 < NT:
                    further(j + 1)
                end(CNT[0:1, 16:17], P * j)

            further(1)
            r = [(pe.sem, pe.n)]
            xt_free[0] = buf_free["gt", 0] = buf_free["gt", 1] = r[0]
            hd_free[0] = both(s_xg, n_xg)
            yd_all = both(s_yd, n_yd)
            ya = [(xg[0], xg[1]), (ysb[0], ysb[1])]
            yfree = [[buf_free["xg", 0], buf_free["xg", 1]], [yd_all]]

            got, stats = {}, {}
            if l == 0:
                fold(0, gl, bl, (fold_to[0], fold_to[2]), rot, None)
                fold(1, gl, bl, (fold_to[1], fold_to[3]), rot, [buf_free["g", 0], buf_free["g", 1]])

            def add_up(t):
                pr = ya[t % 2]
                y = act.activation(pr[0], pr[0], ACT.Copy, scale=w0[:, t:t + 1], after=[got[t], w_r])
                y = dve.scalar_tensor_tensor(pr[0], pr[1], w1[:, t:t + 1], pr[0], ALU.mult, ALU.add, after=[y])
                x, rd = (XL, x_ready) if t < 2 else (XC, c_ready)
                for h in range(2):
                    us = pr[0][:, 512 * h:512 * h + 512]
                    _, f, st_ = add_half(x[:, t % 2, :], h, us, us, gates[t // 2], 16 * t, [y, gates_r[t // 2], rd[t % 2]])
                stats[t] = ln_stats(16 * t, st_)
                yfree[t % 2] = [f]
                h_free[t // 2] = [f]
                if t + 2 < NT:
                    take(t + 2)
                yd_free[0] = both(s_yg, n_yg)

            def take(t):
                for k in range(2):
                    n_yg[t % 2] += 1
                    got[t] = pool.gather_rows(ya[t % 2][k], YD[0:NT * NE * P, :], sidx[:, k, t:t + 1], s_yg[t % 2],
                                              n_yg[t % 2], after=[yd_all, filled, sidx_r, yfree[t % 2]])

            for t in range(2):
                take(t)
            for t in range(2):
                add_up(t)
            norm_last.append((stats, gl, bl, [0, 1]))
            if l == 1:
                norm_now()
            return add_up

        rot2 = Banks([4, 5, 6, 7])
        for l in range(2):
            rotp = Banks([0, 1, 2, 3])
            oT = attn_a(rotp) if l == 0 else attn_b(rotp, add_up)
            attn_out(l, ("wo_a_2" if l == 0 else "wo_b_2", 0), [0, 1, 2, 3] if l == 0 else [0, 1], oT,
                     Banks(list(range(8))))
            add_up = moe(l, 4 if l == 0 else 2)
        for t in range(2):
            fin = sp.dma(out[0, t * P:t * P + P, :], XL[:, t, :], s_out, t + 1, x_ready[t])
        sp.wait(fin, both(s_hd, n_hd), both(s_yd, n_yd))

        if plan is None:
            return W.log
        assert len(plan) == len(W.log) and W.split == len(W.parts)
        block = ctx.enter_context(nc.Block())

        @block.sync
        def _(e):
            sp.play(e)

        @block.gpsimd
        def _(e):
            pool.play(e)

        @block.scalar
        def _(e):
            act.play(e)

        @block.vector
        def _(e):
            dve.play(e)

        @block.tensor
        def _(e):
            pe.play(e)


_INS = ["x", "norm_ffn1", "w_ffn1_in", "w_ffn1_out", "norm_mix", "w_in", "b_forget", "ret_norm", "w_o_ret", "w_o_fox",
        "w_out", "norm_ffn2", "w_ffn2_in", "w_ffn2_out", "norm_final", "c_2", "ctx_2", "c_ctx_2", "w_ada_2", "b_ada_2",
        "wqkv_a_2", "wo_a_2", "sink_a_2", "wqkv_b_2", "wo_b_2", "lambda_b_2", "subln_b_2", "ln_attn_g_2",
        "ln_attn_b_2", "ln_ffn_g_2", "ln_ffn_b_2", "w_router_2", "router_bias_2", "w_gate_2", "w_up_2", "w_down_2"]


def kernel(**inputs):
    import concourse.bacc as _bacc
    from concourse.bass_utils import run_bass_kernel_spmd as _run

    arrays = {f"in_{n}": np.ascontiguousarray(inputs[n]) for n in _INS}
    arrays["consts"], arrays["decay"] = constants()

    def program(plan):
        nc = _bacc.Bacc("TRN2", target_bir_lowering=False, num_devices=1)
        ap = {n: nc.dram_tensor(n, a.shape, mybir.dt.from_np(a.dtype), kind="ExternalInput").ap()
              for n, a in arrays.items()}
        out = nc.dram_tensor("out_0", (1, 256, D), F32, kind="ExternalOutput").ap()
        return nc, build(nc, {n: ap[f"in_{n}"] for n in _INS}, out, ap["consts"], ap["decay"], plan)

    _, plan = program(None)
    nc, _ = program(plan)
    r = _run(nc, [arrays], core_ids=[0])
    return r.results[0]["out_0"]
```
